# Optimizing a Trainium2 kernel written in Bass

```python
import math
import jax
import jax.numpy as jnp
from jax import lax
import numpy as np

D_MODEL = 1024
BATCH = 1
SEQ = 256
DEPTH = 1

SSM_EXPAND = 2
SSM_D_INNER = SSM_EXPAND * D_MODEL
SSM_HEAD_DIM = 64
SSM_HEADS = SSM_D_INNER // SSM_HEAD_DIM
SSM_GROUPS = 4
SSM_HPG = SSM_HEADS // SSM_GROUPS
SSM_STATE = 128
SSM_CONV = 4
SSM_CHUNK = 128
SSM_CONV_DIM = SSM_D_INNER + 2 * SSM_GROUPS * SSM_STATE

NSA_HEADS = 16
NSA_HEAD_DIM = 64
NSA_WIDTH = NSA_HEADS * NSA_HEAD_DIM
NSA_KV_GROUPS = 2
NSA_HPG = NSA_HEADS // NSA_KV_GROUPS
NSA_KV_WIDTH = NSA_KV_GROUPS * NSA_HEAD_DIM
CMP_BLOCK = 32
CMP_STRIDE = 16
CMP_HIDDEN = 256
SEL_BLOCK = 64
SEL_TOPK = 4
WINDOW = 512
NSA_QBLOCK = 64
ROPE_THETA = 10000.0

MOE_GROUPS = 4
EXPERTS_PER_GROUP = 8
N_EXPERTS = MOE_GROUPS * EXPERTS_PER_GROUP
EXPERT_TOPK = 2
EXPERT_HIDDEN = 256

NORM_EPS = 1e-6

IN_SIZES = (SSM_D_INNER, SSM_CONV_DIM, SSM_HEADS, NSA_WIDTH, NSA_KV_WIDTH, NSA_KV_WIDTH, NSA_KV_WIDTH, NSA_KV_WIDTH, NSA_KV_WIDTH, NSA_KV_WIDTH, 3 * NSA_HEADS, D_MODEL, D_MODEL)
IN_WIDTH = SSM_D_INNER + SSM_CONV_DIM + SSM_HEADS + NSA_WIDTH + 6 * NSA_KV_WIDTH + 3 * NSA_HEADS + 2 * D_MODEL


def _rmsnorm(x, g):
    xf = x.astype(jnp.float32)
    y = xf * lax.rsqrt(jnp.mean(xf * xf, axis=-1, keepdims=True) + NORM_EPS)
    return (y * g.astype(jnp.float32)).astype(x.dtype)

def _masked_softmax(s, mask):
    s = jnp.where(mask, s.astype(jnp.float32), -1e30)
    m = jnp.max(s, axis=-1, keepdims=True)
    p = jnp.where(mask, jnp.exp(s - m), 0.0)
    return p / jnp.maximum(jnp.sum(p, axis=-1, keepdims=True), 1e-30)

def _rope(t, cos, sin):
    shape = cos.shape[:2] + (1,) * (t.ndim - 3) + cos.shape[2:]
    cos = cos.reshape(shape)
    sin = sin.reshape(shape)
    t1, t2 = jnp.split(t.astype(jnp.float32), 2, axis=-1)
    return jnp.concatenate([t1 * cos - t2 * sin, t2 * cos + t1 * sin], axis=-1).astype(t.dtype)

def _ssd_chunked_scan(xh, dt, a, bm, cm):
    b, s = xh.shape[:2]
    nc = s // SSM_CHUNK

    def chunks(t):
        t = t.astype(jnp.float32)
        return jnp.moveaxis(t.reshape((b, nc, SSM_CHUNK) + t.shape[2:]), 1, 0)

    tril = jnp.tril(jnp.ones((SSM_CHUNK, SSM_CHUNK), dtype=bool))[None, :, :, None, None]
    a = a.astype(jnp.float32)

    def step(state, inp):
        xc, dtc, bc, cc = inp
        acum = jnp.cumsum(dtc * a, axis=1)
        seg = acum[:, :, None] - acum[:, None, :]
        decay = jnp.exp(jnp.where(tril, seg, -jnp.inf))
        cb = jnp.einsum('btgn,bsgn->bgts', cc, bc)
        y_diag = jnp.einsum('bgts,btsgr,bsgr,bsgrp->btgrp', cb, decay, dtc, xc)
        y_off = jnp.einsum('btgn,bgrpn->btgrp', cc, state) * jnp.exp(acum)[..., None]
        w_end = jnp.exp(acum[:, -1:] - acum) * dtc
        new_state = state * jnp.exp(acum[:, -1])[..., None, None] + jnp.einsum('bsgn,bsgr,bsgrp->bgrpn', bc, w_end, xc)
        return new_state, y_diag + y_off

    state0 = jnp.zeros((b, SSM_GROUPS, SSM_HPG, SSM_HEAD_DIM, SSM_STATE), jnp.float32)
    _, ys = lax.scan(step, state0, (chunks(xh), chunks(dt), chunks(bm), chunks(cm)))
    return jnp.moveaxis(ys, 0, 1).reshape(xh.shape).astype(xh.dtype)

def _mamba2_mixer(h_z, h_xbc, h_dt, conv_w, conv_b, dt_bias, a_log, d_skip, ssm_norm_g):
    b, s, _ = h_xbc.shape
    xbc = lax.conv_general_dilated(h_xbc, conv_w[:, None, :], window_strides=(1,), padding=[(SSM_CONV - 1, 0)], dimension_numbers=('NWC', 'WIO', 'NWC'), feature_group_count=SSM_CONV_DIM)
    xbc = jax.nn.silu(xbc + conv_b)
    xs, bm, cm = jnp.split(xbc, [SSM_D_INNER, SSM_D_INNER + SSM_GROUPS * SSM_STATE], axis=-1)
    xh = xs.reshape(b, s, SSM_GROUPS, SSM_HPG, SSM_HEAD_DIM)
    bm = bm.reshape(b, s, SSM_GROUPS, SSM_STATE)
    cm = cm.reshape(b, s, SSM_GROUPS, SSM_STATE)
    dt = jax.nn.softplus((h_dt + dt_bias).astype(jnp.float32)).reshape(b, s, SSM_GROUPS, SSM_HPG)
    a = -jnp.exp(a_log.astype(jnp.float32)).reshape(SSM_GROUPS, SSM_HPG)
    y = _ssd_chunked_scan(xh, dt, a, bm, cm) + d_skip.reshape(SSM_GROUPS, SSM_HPG, 1) * xh
    y = y.reshape(b, s, SSM_D_INNER) * jax.nn.silu(h_z)
    yg = y.astype(jnp.float32).reshape(b, s, SSM_GROUPS, SSM_D_INNER // SSM_GROUPS)
    yg = yg * lax.rsqrt(jnp.mean(yg * yg, axis=-1, keepdims=True) + NORM_EPS)
    return (yg.reshape(b, s, SSM_D_INNER) * ssm_norm_g).astype(h_z.dtype)

def _compress(t, pe, w1, w2, idx):
    b = t.shape[0]
    blk = t[:, idx] + pe[None, None, :, None, :]
    blk = jnp.moveaxis(blk, 3, 2).reshape(b, idx.shape[0], NSA_KV_GROUPS, CMP_BLOCK * NSA_HEAD_DIM)
    return jax.nn.silu(blk @ w1) @ w2

def _nsa_mixer(q, kc, vc, ksl, vsl, kw, vw, gates, cos, sin, cmp_pe_k, cmp_w1_k, cmp_w2_k, cmp_pe_v, cmp_w1_v, cmp_w2_v):
    b, s = q.shape[:2]
    G, R, dk = NSA_KV_GROUPS, NSA_HPG, NSA_HEAD_DIM
    q = _rope(q.reshape(b, s, G, R, dk), cos, sin)
    kc = _rope(kc.reshape(b, s, G, dk), cos, sin)
    ksl = _rope(ksl.reshape(b, s, G, dk), cos, sin)
    kw = _rope(kw.reshape(b, s, G, dk), cos, sin)
    vc = vc.reshape(b, s, G, dk)
    vsl = vsl.reshape(b, s, G, dk)
    vw = vw.reshape(b, s, G, dk)
    gates = jax.nn.sigmoid(gates.astype(jnp.float32)).reshape(b, s, G, R, 3)
    n_cmp = (s - CMP_BLOCK) // CMP_STRIDE + 1
    cidx = jnp.arange(n_cmp)[:, None] * CMP_STRIDE + jnp.arange(CMP_BLOCK)[None, :]
    kcmp = _compress(kc, cmp_pe_k, cmp_w1_k, cmp_w2_k, cidx)
    vcmp = _compress(vc, cmp_pe_v, cmp_w1_v, cmp_w2_v, cidx)
    cstart = jnp.arange(n_cmp) * CMP_STRIDE
    cmp_end = cstart + CMP_BLOCK - 1
    n_sel = s // SEL_BLOCK
    sstart = jnp.arange(n_sel) * SEL_BLOCK
    overlap = ((cstart[:, None] < sstart[None, :] + SEL_BLOCK) & (cstart[:, None] + CMP_BLOCK > sstart[None, :])).astype(jnp.float32)
    ksb = jnp.moveaxis(ksl.reshape(b, n_sel, SEL_BLOCK, G, dk), 3, 1)
    vsb = jnp.moveaxis(vsl.reshape(b, n_sel, SEL_BLOCK, G, dk), 3, 1)
    kwp = jnp.pad(kw, ((0, 0), (WINDOW, 0), (0, 0), (0, 0)))
    vwp = jnp.pad(vw, ((0, 0), (WINDOW, 0), (0, 0), (0, 0)))
    scale = NSA_HEAD_DIM ** -0.5
    bi = jnp.arange(b)[:, None, None, None]
    gi = jnp.arange(G)[None, :, None, None]
    sel_j = jnp.arange(n_sel)
    win_off = jnp.arange(WINDOW + NSA_QBLOCK) - WINDOW

    def block(qi):
        s0 = qi * NSA_QBLOCK
        t = s0 + jnp.arange(NSA_QBLOCK)
        qb = lax.dynamic_slice_in_dim(q, s0, NSA_QBLOCK, axis=1)
        gb = lax.dynamic_slice_in_dim(gates, s0, NSA_QBLOCK, axis=1)
        mask_c = (cmp_end[None, :] <= t[:, None])[None, :, None, None, :]
        pc = _masked_softmax(jnp.einsum('bqgrd,bcgd->bqgrc', qb, kcmp) * scale, mask_c)
        o_cmp = jnp.einsum('bqgrc,bcgd->bqgrd', pc, vcmp)
        local = t // SEL_BLOCK
        prio = jnp.where(sel_j[None, :] == local[:, None], 1e6, jnp.where(sel_j[None, :] > local[:, None], -jnp.inf, jnp.where(sel_j[None, :] == 0, 5e5, 0.0)))
        imp = jnp.einsum('bqgrc,cj->bqgj', pc, overlap) + prio[None, :, None, :]
        _, sel = lax.top_k(imp, SEL_TOPK)
        sel = jnp.swapaxes(sel, 1, 2)
        k_g = ksb[bi, gi, sel]
        v_g = vsb[bi, gi, sel]
        kpos = sel[..., None] * SEL_BLOCK + jnp.arange(SEL_BLOCK)
        mask_s = jnp.swapaxes(kpos <= t[None, None, :, None, None], 1, 2).reshape(b, NSA_QBLOCK, G, 1, SEL_TOPK * SEL_BLOCK)
        ss = jnp.einsum('bqgrd,bgqkld->bqgrkl', qb, k_g).reshape(b, NSA_QBLOCK, G, R, SEL_TOPK * SEL_BLOCK) * scale
        ps = _masked_softmax(ss, mask_s).reshape(b, NSA_QBLOCK, G, R, SEL_TOPK, SEL_BLOCK)
        o_slc = jnp.einsum('bqgrkl,bgqkld->bqgrd', ps, v_g)
        kwb = lax.dynamic_slice_in_dim(kwp, s0, WINDOW + NSA_QBLOCK, axis=1)
        vwb = lax.dynamic_slice_in_dim(vwp, s0, WINDOW + NSA_QBLOCK, axis=1)
        kpos_w = s0 + win_off
        mask_w = ((kpos_w[None, :] <= t[:, None]) & (kpos_w[None, :] > t[:, None] - WINDOW) & (kpos_w[None, :] >= 0))[None, :, None, None, :]
        pw = _masked_softmax(jnp.einsum('bqgrd,bkgd->bqgrk', qb, kwb) * scale, mask_w)
        o_win = jnp.einsum('bqgrk,bkgd->bqgrd', pw, vwb)
        return gb[..., 0:1] * o_cmp + gb[..., 1:2] * o_slc + gb[..., 2:3] * o_win

    out = lax.map(block, jnp.arange(s // NSA_QBLOCK))
    return jnp.moveaxis(out, 0, 1).reshape(b, s, NSA_WIDTH).astype(q.dtype)

def _hier_moe(h, w_rg, b_rg, w_re, b_re, w_g, w_u, w_d):
    b, s, d = h.shape
    t = h.reshape(b * s, d)
    tf = t.astype(jnp.float32)
    p_group = jax.nn.softmax(tf @ w_rg.astype(jnp.float32) + b_rg.astype(jnp.float32), axis=-1)
    pg, gsel = lax.top_k(p_group, 1)
    le = (tf @ w_re.astype(jnp.float32) + b_re.astype(jnp.float32)).reshape(-1, MOE_GROUPS, EXPERTS_PER_GROUP)
    le_g = jnp.einsum('tge,tg->te', le, jax.nn.one_hot(gsel[:, 0], MOE_GROUPS, dtype=jnp.float32))
    pe = jax.nn.softmax(le_g, axis=-1)
    pv, pi = lax.top_k(pe, EXPERT_TOPK)
    wts = pg * pv / jnp.sum(pv, axis=-1, keepdims=True)
    ids = gsel * EXPERTS_PER_GROUP + pi
    combine = jnp.sum(jax.nn.one_hot(ids, N_EXPERTS, dtype=jnp.float32) * wts[..., None], axis=1)
    out = jnp.zeros((b * s, d), jnp.float32)
    for e in range(N_EXPERTS):
        he = jax.nn.silu(t @ w_g[e]) * (t @ w_u[e])
        out = out + combine[:, e:e + 1] * (he @ w_d[e])
    return out.reshape(b, s, d).astype(h.dtype)

def _hybrid_layer(h, c, cos, sin, w_ada, b_ada, norm1_g, w_in, conv_w, conv_b, dt_bias, a_log, d_skip, ssm_norm_g, w_ssm_out, cmp_pe_k, cmp_w1_k, cmp_w2_k, cmp_pe_v, cmp_w1_v, cmp_w2_v, w_nsa_out, w_o, norm2_g, w_router_group, b_router_group, w_router_expert, b_router_expert, w_exp_gate, w_exp_up, w_exp_down):
    ada = jax.nn.silu(c) @ w_ada + b_ada
    shift1, scale1, gate1, shift2, scale2, gate2 = [a[:, None, :] for a in jnp.split(ada, 6, axis=-1)]
    hn = _rmsnorm(h, norm1_g) * (1.0 + scale1) + shift1
    offsets = [int(o) for o in np.cumsum(IN_SIZES)[:-1]]
    w_z, w_xbc, w_dt, w_q, w_kc, w_vc, w_ks, w_vs, w_kw, w_vw, w_gn, w_gs, w_ga = jnp.split(w_in, offsets, axis=1)
    y_ssm = _mamba2_mixer(hn @ w_z, hn @ w_xbc, hn @ w_dt, conv_w, conv_b, dt_bias, a_log, d_skip, ssm_norm_g) @ w_ssm_out
    y_nsa = _nsa_mixer(hn @ w_q, hn @ w_kc, hn @ w_vc, hn @ w_ks, hn @ w_vs, hn @ w_kw, hn @ w_vw, hn @ w_gn, cos, sin, cmp_pe_k, cmp_w1_k, cmp_w2_k, cmp_pe_v, cmp_w1_v, cmp_w2_v) @ w_nsa_out
    merged = jax.nn.sigmoid(hn @ w_gs) * y_ssm + jax.nn.sigmoid(hn @ w_ga) * y_nsa
    h = h + gate1 * (merged @ w_o)
    hn2 = _rmsnorm(h, norm2_g) * (1.0 + scale2) + shift2
    h = h + gate2 * _hier_moe(hn2, w_router_group, b_router_group, w_router_expert, b_router_expert, w_exp_gate, w_exp_up, w_exp_down)
    return h

def first_inputs(seed: int = 0) -> dict:
    key = jax.random.key(seed)
    ks = jax.random.split(key, 40)
    f32 = jnp.float32

    def nrm(k, shape, fan_in):
        return jax.random.normal(k, shape, f32) * fan_in ** -0.5

    def gain(k, shape):
        return 1.0 + 0.05 * jax.random.normal(k, shape, f32)

    def small(k, shape, s=0.02):
        return s * jax.random.normal(k, shape, f32)

    L = DEPTH
    dt0 = jnp.exp(jax.random.uniform(ks[9], (L, SSM_HEADS), f32) * (math.log(0.1) - math.log(0.001)) + math.log(0.001))
    return {
        'x': jax.random.normal(ks[0], (BATCH, SEQ, D_MODEL), f32),
        'c': jax.random.normal(ks[1], (BATCH, D_MODEL), f32),
        'positions': jnp.arange(SEQ, dtype=jnp.int32)[None, :] + jax.random.randint(ks[2], (BATCH, 1), 0, 4096, dtype=jnp.int32),
        'w_ada': nrm(ks[3], (L, D_MODEL, 6 * D_MODEL), D_MODEL),
        'b_ada': small(ks[4], (L, 6 * D_MODEL)),
        'norm1_g': gain(ks[5], (L, D_MODEL)),
        'w_in': nrm(ks[6], (L, D_MODEL, IN_WIDTH), D_MODEL),
        'conv_w': nrm(ks[7], (L, SSM_CONV, SSM_CONV_DIM), SSM_CONV),
        'conv_b': small(ks[8], (L, SSM_CONV_DIM)),
        'dt_bias': dt0 + jnp.log(-jnp.expm1(-dt0)),
        'a_log': jnp.log(jax.random.uniform(ks[10], (L, SSM_HEADS), f32, minval=1.0, maxval=16.0)),
        'd_skip': 1.0 + 0.1 * jax.random.normal(ks[11], (L, SSM_HEADS), f32),
        'ssm_norm_g': gain(ks[12], (L, SSM_D_INNER)),
        'w_ssm_out': nrm(ks[13], (L, SSM_D_INNER, D_MODEL), SSM_D_INNER),
        'cmp_pe_k': small(ks[14], (L, CMP_BLOCK, NSA_HEAD_DIM)),
        'cmp_w1_k': nrm(ks[15], (L, CMP_BLOCK * NSA_HEAD_DIM, CMP_HIDDEN), CMP_BLOCK * NSA_HEAD_DIM),
        'cmp_w2_k': nrm(ks[16], (L, CMP_HIDDEN, NSA_HEAD_DIM), CMP_HIDDEN),
        'cmp_pe_v': small(ks[17], (L, CMP_BLOCK, NSA_HEAD_DIM)),
        'cmp_w1_v': nrm(ks[18], (L, CMP_BLOCK * NSA_HEAD_DIM, CMP_HIDDEN), CMP_BLOCK * NSA_HEAD_DIM),
        'cmp_w2_v': nrm(ks[19], (L, CMP_HIDDEN, NSA_HEAD_DIM), CMP_HIDDEN),
        'w_nsa_out': nrm(ks[20], (L, NSA_WIDTH, D_MODEL), NSA_WIDTH),
        'w_o': nrm(ks[21], (L, D_MODEL, D_MODEL), D_MODEL),
        'norm2_g': gain(ks[22], (L, D_MODEL)),
        'w_router_group': nrm(ks[23], (L, D_MODEL, MOE_GROUPS), D_MODEL),
        'b_router_group': small(ks[24], (L, MOE_GROUPS), 0.01),
        'w_router_expert': nrm(ks[25], (L, D_MODEL, N_EXPERTS), D_MODEL),
        'b_router_expert': small(ks[26], (L, N_EXPERTS), 0.01),
        'w_exp_gate': nrm(ks[27], (L, N_EXPERTS, D_MODEL, EXPERT_HIDDEN), D_MODEL),
        'w_exp_up': nrm(ks[28], (L, N_EXPERTS, D_MODEL, EXPERT_HIDDEN), D_MODEL),
        'w_exp_down': nrm(ks[29], (L, N_EXPERTS, EXPERT_HIDDEN, D_MODEL), EXPERT_HIDDEN),
        'final_g': gain(ks[30], (D_MODEL,)),
    }

def first_block(x, c, positions, w_ada, b_ada, norm1_g, w_in, conv_w, conv_b, dt_bias, a_log, d_skip, ssm_norm_g, w_ssm_out, cmp_pe_k, cmp_w1_k, cmp_w2_k, cmp_pe_v, cmp_w1_v, cmp_w2_v, w_nsa_out, w_o, norm2_g, w_router_group, b_router_group, w_router_expert, b_router_expert, w_exp_gate, w_exp_up, w_exp_down, final_g):
    inv_freq = ROPE_THETA ** (-jnp.arange(0, NSA_HEAD_DIM, 2, dtype=jnp.float32) / NSA_HEAD_DIM)
    ang = positions.astype(jnp.float32)[..., None] * inv_freq
    cos, sin = jnp.cos(ang), jnp.sin(ang)
    h = x
    for l in range(DEPTH):
        h = _hybrid_layer(h, c, cos, sin, w_ada[l], b_ada[l], norm1_g[l], w_in[l], conv_w[l], conv_b[l], dt_bias[l], a_log[l], d_skip[l], ssm_norm_g[l], w_ssm_out[l], cmp_pe_k[l], cmp_w1_k[l], cmp_w2_k[l], cmp_pe_v[l], cmp_w1_v[l], cmp_w2_v[l], w_nsa_out[l], w_o[l], norm2_g[l], w_router_group[l], b_router_group[l], w_router_expert[l], b_router_expert[l], w_exp_gate[l], w_exp_up[l], w_exp_down[l])
    return _rmsnorm(h, final_g)


DEPTH_2 = 2

GRID_W = 64
CTX_LEN = 256
N_MIXERS = 4
Q_BLOCK = 128
ROPE_BASE = 10000.0
EPS = 1e-6
NEG_INF = -1e30

GQA_HEADS = 16
GQA_KV_HEADS = 4
GQA_HEAD_DIM = 64
MLA_HEADS = 16
MLA_NOPE_DIM = 64
MLA_ROPE_DIM = 32
MLA_V_DIM = 64
MLA_Q_LORA = 384
MLA_KV_LORA = 256
DIFF_HEADS = 8
DIFF_HEAD_DIM = 64
NA_HEADS = 16
NA_HEAD_DIM = 64
NA_ROWS = 8
NA_COLS = 16
NA_QROWS = Q_BLOCK // GRID_W
FFN_DIM = 2816


def rms_norm(x, g):
    xf = x.astype(jnp.float32)
    y = xf * lax.rsqrt(jnp.mean(xf * xf, axis=-1, keepdims=True) + EPS)
    return (y * g.astype(jnp.float32)).astype(x.dtype)

def norm_modulate(h, g, shift, scale):
    return rms_norm(h, g) * (1 + scale) + shift

def softmax_f32(s):
    return jax.nn.softmax(s.astype(jnp.float32), axis=-1)

def axial_rope(n_tokens, rot_dim, dtype):
    t = jnp.arange(n_tokens)
    row = (t // GRID_W).astype(jnp.float32)
    col = (t % GRID_W).astype(jnp.float32)
    half = rot_dim // 2
    inv = ROPE_BASE ** (-jnp.arange(0, half, 2, dtype=jnp.float32) / half)
    ar, ac = row[:, None] * inv, col[:, None] * inv
    ang = jnp.concatenate([ar, ar, ac, ac], axis=-1)
    return jnp.cos(ang).astype(dtype), jnp.sin(ang).astype(dtype)

def apply_rope(x, cos, sin):
    x1, x2, x3, x4 = jnp.split(x, 4, axis=-1)
    rot = jnp.concatenate([-x2, x1, -x4, x3], axis=-1)
    shape = (cos.shape[0],) + (1,) * (x.ndim - 3) + (cos.shape[1],)
    return x * cos.reshape(shape) + rot * sin.reshape(shape)

def sweep_query_blocks(fn, *qs):
    b, t = qs[0].shape[:2]
    nb = t // Q_BLOCK
    blocks = tuple(jnp.moveaxis(q.reshape(b, nb, Q_BLOCK, *q.shape[2:]), 1, 0) for q in qs)
    out = lax.map(lambda qb: fn(*qb), blocks)
    return jnp.moveaxis(out, 0, 1).reshape(b, t, *out.shape[3:])

def gqa_mixer(hx, hc, w_in, q_g, k_g, w_out, ctx_out):
    b, t, d = hx.shape
    grp = GQA_HEADS // GQA_KV_HEADS
    splits = [GQA_HEADS * GQA_HEAD_DIM, (GQA_HEADS + GQA_KV_HEADS) * GQA_HEAD_DIM]

    def project(h):
        n = h.shape[1]
        q, k, v = jnp.split(h @ w_in, splits, axis=-1)
        q = rms_norm(q.reshape(b, n, GQA_KV_HEADS, grp, GQA_HEAD_DIM), q_g)
        k = rms_norm(k.reshape(b, n, GQA_KV_HEADS, GQA_HEAD_DIM), k_g)
        return q, k, v.reshape(b, n, GQA_KV_HEADS, GQA_HEAD_DIM)

    qx, kx, vx = project(hx)
    qc, kc, vc = project(hc)
    cos, sin = axial_rope(t, GQA_HEAD_DIM, hx.dtype)
    qx, kx = apply_rope(qx, cos, sin), apply_rope(kx, cos, sin)
    k_all = jnp.concatenate([kc, kx], axis=1)
    v_all = jnp.concatenate([vc, vx], axis=1)
    scale = GQA_HEAD_DIM ** -0.5

    def attend(q, k, v):
        s = jnp.einsum('bqhgd,bkhd->bhgqk', q, k) * scale
        p = softmax_f32(s).astype(v.dtype)
        return jnp.einsum('bhgqk,bkhd->bqhgd', p, v)

    out_x = sweep_query_blocks(lambda qb: attend(qb, k_all, v_all), qx).reshape(b, t, d) @ w_out
    out_c = attend(qc, kc, vc).reshape(b, hc.shape[1], d) @ w_out if ctx_out else None
    return out_x, out_c

def mla_mixer(hx, hc, w_in, q_norm_g, kv_norm_g, w_uq, w_ukv, w_out, ctx_out):
    b, t, d = hx.shape
    qk_dim = MLA_NOPE_DIM + MLA_ROPE_DIM

    def project(h):
        n = h.shape[1]
        cq, ckv, k_rope = jnp.split(h @ w_in, [MLA_Q_LORA, MLA_Q_LORA + MLA_KV_LORA], axis=-1)
        q = (rms_norm(cq, q_norm_g) @ w_uq).reshape(b, n, MLA_HEADS, qk_dim)
        kv = (rms_norm(ckv, kv_norm_g) @ w_ukv).reshape(b, n, MLA_HEADS, MLA_NOPE_DIM + MLA_V_DIM)
        q_nope, q_rope = jnp.split(q, [MLA_NOPE_DIM], axis=-1)
        k_nope, v = jnp.split(kv, [MLA_NOPE_DIM], axis=-1)
        return q_nope, q_rope, k_nope, k_rope, v

    qnx, qrx, knx, krx, vx = project(hx)
    qnc, qrc, knc, krc, vc = project(hc)
    cos, sin = axial_rope(t, MLA_ROPE_DIM, hx.dtype)
    qrx, krx = apply_rope(qrx, cos, sin), apply_rope(krx, cos, sin)
    kn_all = jnp.concatenate([knc, knx], axis=1)
    kr_all = jnp.concatenate([krc, krx], axis=1)
    v_all = jnp.concatenate([vc, vx], axis=1)
    scale = qk_dim ** -0.5

    def attend(qn, qr, kn, kr, v):
        s = (jnp.einsum('bqhd,bkhd->bhqk', qn, kn) + jnp.einsum('bqhd,bkd->bhqk', qr, kr)) * scale
        p = softmax_f32(s).astype(v.dtype)
        return jnp.einsum('bhqk,bkhd->bqhd', p, v)

    ox = sweep_query_blocks(lambda qn, qr: attend(qn, qr, kn_all, kr_all, v_all), qnx, qrx)
    out_x = ox.reshape(b, t, MLA_HEADS * MLA_V_DIM) @ w_out
    out_c = attend(qnc, qrc, knc, krc, vc).reshape(b, hc.shape[1], MLA_HEADS * MLA_V_DIM) @ w_out if ctx_out else None
    return out_x, out_c

def diff_mixer(hx, hc, w_in, lam, subln_g, w_out, layer_idx, ctx_out):
    b, t, d = hx.shape
    lambda_init = 0.8 - 0.6 * math.exp(-0.3 * layer_idx)
    lf = lam.astype(jnp.float32)
    lam_full = jnp.exp(jnp.sum(lf[0] * lf[1])) - jnp.exp(jnp.sum(lf[2] * lf[3])) + lambda_init

    def project(h):
        n = h.shape[1]
        q, k, v = jnp.split(h @ w_in, 3, axis=-1)
        q = q.reshape(b, n, DIFF_HEADS, 2, DIFF_HEAD_DIM)
        k = k.reshape(b, n, DIFF_HEADS, 2, DIFF_HEAD_DIM)
        return q, k, v.reshape(b, n, DIFF_HEADS, 2 * DIFF_HEAD_DIM)

    qx, kx, vx = project(hx)
    qc, kc, vc = project(hc)
    cos, sin = axial_rope(t, DIFF_HEAD_DIM, hx.dtype)
    qx, kx = apply_rope(qx, cos, sin), apply_rope(kx, cos, sin)
    k_all = jnp.concatenate([kc, kx], axis=1)
    v_all = jnp.concatenate([vc, vx], axis=1)
    scale = DIFF_HEAD_DIM ** -0.5

    def attend(q, k, v):
        s = jnp.einsum('bqhjd,bkhjd->bhjqk', q, k) * scale
        p = softmax_f32(s)
        p = p[:, :, 0] - lam_full * p[:, :, 1]
        o = jnp.einsum('bhqk,bkhe->bqhe', p.astype(v.dtype), v)
        return rms_norm(o, subln_g) * (1 - lambda_init)

    out_x = sweep_query_blocks(lambda qb: attend(qb, k_all, v_all), qx).reshape(b, t, d) @ w_out
    out_c = attend(qc, kc, vc).reshape(b, hc.shape[1], d) @ w_out if ctx_out else None
    return out_x, out_c

def na_mixer(hx, hc, w_in, rpb, w_out, ctx_out):
    b, t, d = hx.shape
    rows = t // GRID_W
    win_rows = min(NA_ROWS, rows)
    band_rows = min(win_rows + 1, rows)
    band = band_rows * GRID_W
    n_ctx = hc.shape[1]

    def project(h):
        n = h.shape[1]
        q, k, v = jnp.split(h @ w_in, 3, axis=-1)
        return tuple(a.reshape(b, n, NA_HEADS, NA_HEAD_DIM) for a in (q, k, v))

    qx, kx, vx = project(hx)
    qc, kc, vc = project(hc)
    scale = NA_HEAD_DIM ** -0.5
    k_grid = kx.reshape(b, rows, GRID_W, NA_HEADS, NA_HEAD_DIM)
    v_grid = vx.reshape(b, rows, GRID_W, NA_HEADS, NA_HEAD_DIM)
    nb = t // Q_BLOCK
    q_blocks = jnp.moveaxis(qx.reshape(b, nb, Q_BLOCK, NA_HEADS, NA_HEAD_DIM), 1, 0)
    q_off, k_off = jnp.arange(Q_BLOCK), jnp.arange(band)
    q_dr, q_col = q_off // GRID_W, q_off % GRID_W
    k_dr, k_col = k_off // GRID_W, k_off % GRID_W
    col_start = jnp.clip(q_col - NA_COLS // 2, 0, GRID_W - NA_COLS)
    col_in = (k_col[None, :] >= col_start[:, None]) & (k_col[None, :] < col_start[:, None] + NA_COLS)
    dc_idx = jnp.clip(k_col[None, :] - q_col[:, None] + NA_COLS - 1, 0, 2 * NA_COLS - 2)

    def block(args):
        j, qb = args
        r = j * NA_QROWS + q_dr
        row_start = jnp.clip(r - win_rows // 2, 0, rows - win_rows)
        b0 = jnp.minimum(row_start[0], rows - band_rows)
        k_band = lax.dynamic_slice_in_dim(k_grid, b0, band_rows, axis=1).reshape(b, band, NA_HEADS, NA_HEAD_DIM)
        v_band = lax.dynamic_slice_in_dim(v_grid, b0, band_rows, axis=1).reshape(b, band, NA_HEADS, NA_HEAD_DIM)
        k_row = b0 + k_dr
        in_win = col_in & (k_row[None, :] >= row_start[:, None]) & (k_row[None, :] < row_start[:, None] + win_rows)
        dr_idx = jnp.clip(k_row[None, :] - r[:, None] + NA_ROWS - 1, 0, 2 * NA_ROWS - 2)
        bias = rpb[:, dr_idx, dc_idx].astype(jnp.float32)
        s_lat = jnp.einsum('bqhd,bkhd->bhqk', qb, k_band).astype(jnp.float32) * scale + bias
        s_lat = jnp.where(in_win, s_lat, NEG_INF)
        s_ctx = jnp.einsum('bqhd,bkhd->bhqk', qb, kc).astype(jnp.float32) * scale
        p = softmax_f32(jnp.concatenate([s_ctx, s_lat], axis=-1)).astype(vx.dtype)
        return (jnp.einsum('bhqk,bkhd->bqhd', p[..., :n_ctx], vc)
                + jnp.einsum('bhqk,bkhd->bqhd', p[..., n_ctx:], v_band))

    ox = lax.map(block, (jnp.arange(nb), q_blocks))
    out_x = jnp.moveaxis(ox, 0, 1).reshape(b, t, d) @ w_out
    if ctx_out:
        s = jnp.einsum('bqhd,bkhd->bhqk', qc, kc) * scale
        p = softmax_f32(s).astype(vc.dtype)
        out_c = jnp.einsum('bhqk,bkhd->bqhd', p, vc).reshape(b, n_ctx, d) @ w_out
    else:
        out_c = None
    return out_x, out_c

def dwconv_centred(u, w, bias):
    p = jnp.pad(u, ((0, 0), (1, 1), (0, 0)))
    return p[:, :-2] * w[0] + p[:, 1:-1] * w[1] + p[:, 2:] * w[2] + bias

def conv_ffn(h, w_up, conv_w, conv_b, w_down):
    u = dwconv_centred(h @ w_up, conv_w, conv_b)
    val, gate = jnp.split(u, 2, axis=-1)
    return (jax.nn.silu(gate) * val) @ w_down

def second_inputs(seed: int = 0) -> dict:
    key = jax.random.key(seed)
    ks = iter(jax.random.split(key, 32))
    D = D_MODEL

    def nrm(shape, scale=1.0):
        return jax.random.normal(next(ks), shape, jnp.float32) * scale

    def gain(shape):
        return 1.0 + nrm(shape, 0.02)

    la, lb, lc, ld = (len(range(m, DEPTH_2, N_MIXERS)) for m in range(N_MIXERS))
    gqa_in = (GQA_HEADS + 2 * GQA_KV_HEADS) * GQA_HEAD_DIM
    mla_in = MLA_Q_LORA + MLA_KV_LORA + MLA_ROPE_DIM
    return {
        'x': nrm((BATCH, SEQ, D)),
        'c': nrm((BATCH, D)),
        'ctx': nrm((BATCH, CTX_LEN, D)),
        'c_ctx': nrm((D,)),
        'ada_w': nrm((DEPTH_2, D, 6 * D), 0.5 * D ** -0.5),
        'ada_b': nrm((DEPTH_2, 6 * D), 0.02),
        'norm1_g': gain((DEPTH_2, D)),
        'norm2_g': gain((DEPTH_2, D)),
        'ffn_w_up': nrm((DEPTH_2, D, 2 * FFN_DIM), D ** -0.5),
        'ffn_conv_w': nrm((DEPTH_2, 3, 2 * FFN_DIM), 3 ** -0.5),
        'ffn_conv_b': nrm((DEPTH_2, 2 * FFN_DIM), 0.02),
        'ffn_w_down': nrm((DEPTH_2, FFN_DIM, D), FFN_DIM ** -0.5),
        'gqa_w_in': nrm((la, D, gqa_in), D ** -0.5),
        'gqa_q_norm_g': gain((la, GQA_HEAD_DIM)),
        'gqa_k_norm_g': gain((la, GQA_HEAD_DIM)),
        'gqa_w_out': nrm((la, GQA_HEADS * GQA_HEAD_DIM, D), (GQA_HEADS * GQA_HEAD_DIM) ** -0.5),
        'mla_w_in': nrm((lb, D, mla_in), D ** -0.5),
        'mla_q_norm_g': gain((lb, MLA_Q_LORA)),
        'mla_kv_norm_g': gain((lb, MLA_KV_LORA)),
        'mla_w_uq': nrm((lb, MLA_Q_LORA, MLA_HEADS * (MLA_NOPE_DIM + MLA_ROPE_DIM)), MLA_Q_LORA ** -0.5),
        'mla_w_ukv': nrm((lb, MLA_KV_LORA, MLA_HEADS * (MLA_NOPE_DIM + MLA_V_DIM)), MLA_KV_LORA ** -0.5),
        'mla_w_out': nrm((lb, MLA_HEADS * MLA_V_DIM, D), (MLA_HEADS * MLA_V_DIM) ** -0.5),
        'diff_w_in': nrm((lc, D, 3 * D), D ** -0.5),
        'diff_lambda': nrm((lc, 4, DIFF_HEAD_DIM), 0.1),
        'diff_subln_g': gain((lc, 2 * DIFF_HEAD_DIM)),
        'diff_w_out': nrm((lc, D, D), D ** -0.5),
        'na_w_in': nrm((ld, D, 3 * D), D ** -0.5),
        'na_rpb': nrm((ld, NA_HEADS, 2 * NA_ROWS - 1, 2 * NA_COLS - 1), 0.05),
        'na_w_out': nrm((ld, D, D), D ** -0.5),
        'final_norm_g': gain((D,)),
    }

def second_block(x, c, ctx, c_ctx, ada_w, ada_b, norm1_g, norm2_g, ffn_w_up, ffn_conv_w, ffn_conv_b, ffn_w_down,
              gqa_w_in, gqa_q_norm_g, gqa_k_norm_g, gqa_w_out,
              mla_w_in, mla_q_norm_g, mla_kv_norm_g, mla_w_uq, mla_w_ukv, mla_w_out,
              diff_w_in, diff_lambda, diff_subln_g, diff_w_out,
              na_w_in, na_rpb, na_w_out, final_norm_g):
    silu_c = jax.nn.silu(c)
    silu_cc = jax.nn.silu(c_ctx)
    for i in range(DEPTH_2):
        ctx_out = i < DEPTH_2 - 1
        m, j = i % N_MIXERS, i // N_MIXERS
        sh1, sc1, g1, sh2, sc2, g2 = (a[:, None, :] for a in jnp.split(silu_c @ ada_w[i] + ada_b[i], 6, axis=-1))
        csh1, csc1, cg1, csh2, csc2, cg2 = jnp.split(silu_cc @ ada_w[i] + ada_b[i], 6, axis=-1)
        hx = norm_modulate(x, norm1_g[i], sh1, sc1)
        hc = norm_modulate(ctx, norm1_g[i], csh1, csc1)
        if m == 0:
            ox, oc = gqa_mixer(hx, hc, gqa_w_in[j], gqa_q_norm_g[j], gqa_k_norm_g[j], gqa_w_out[j], ctx_out)
        elif m == 1:
            ox, oc = mla_mixer(hx, hc, mla_w_in[j], mla_q_norm_g[j], mla_kv_norm_g[j], mla_w_uq[j],
                               mla_w_ukv[j], mla_w_out[j], ctx_out)
        elif m == 2:
            ox, oc = diff_mixer(hx, hc, diff_w_in[j], diff_lambda[j], diff_subln_g[j], diff_w_out[j], i, ctx_out)
        else:
            ox, oc = na_mixer(hx, hc, na_w_in[j], na_rpb[j], na_w_out[j], ctx_out)
        x = x + g1 * ox
        x = x + g2 * conv_ffn(norm_modulate(x, norm2_g[i], sh2, sc2),
                              ffn_w_up[i], ffn_conv_w[i], ffn_conv_b[i], ffn_w_down[i])
        if ctx_out:
            ctx = ctx + cg1 * oc
            ctx = ctx + cg2 * conv_ffn(norm_modulate(ctx, norm2_g[i], csh2, csc2),
                                       ffn_w_up[i], ffn_conv_w[i], ffn_conv_b[i], ffn_w_down[i])
    return rms_norm(x, final_norm_g)


def setup_inputs(seed=0):
    out = dict(first_inputs(seed))
    for name, value in second_inputs(seed + 1).items():
        if name != "x":
            out[name + "_2"] = value
    return out


def reference(
    x, c, positions, w_ada, b_ada, norm1_g, w_in, conv_w, conv_b, dt_bias, a_log, d_skip,
    ssm_norm_g, w_ssm_out, cmp_pe_k, cmp_w1_k, cmp_w2_k, cmp_pe_v, cmp_w1_v, cmp_w2_v,
    w_nsa_out, w_o, norm2_g, w_router_group, b_router_group, w_router_expert, b_router_expert,
    w_exp_gate, w_exp_up, w_exp_down, final_g, c_2, ctx_2, c_ctx_2, ada_w_2, ada_b_2, norm1_g_2,
    norm2_g_2, ffn_w_up_2, ffn_conv_w_2, ffn_conv_b_2, ffn_w_down_2, gqa_w_in_2, gqa_q_norm_g_2,
    gqa_k_norm_g_2, gqa_w_out_2, mla_w_in_2, mla_q_norm_g_2, mla_kv_norm_g_2, mla_w_uq_2,
    mla_w_ukv_2, mla_w_out_2, diff_w_in_2, diff_lambda_2, diff_subln_g_2, diff_w_out_2,
    na_w_in_2, na_rpb_2, na_w_out_2, final_norm_g_2,
):
    x = first_block(
        x, c, positions, w_ada, b_ada, norm1_g, w_in, conv_w, conv_b, dt_bias, a_log, d_skip,
        ssm_norm_g, w_ssm_out, cmp_pe_k, cmp_w1_k, cmp_w2_k, cmp_pe_v, cmp_w1_v, cmp_w2_v,
        w_nsa_out, w_o, norm2_g, w_router_group, b_router_group, w_router_expert,
        b_router_expert, w_exp_gate, w_exp_up, w_exp_down, final_g,
    )
    return second_block(
        x, c_2, ctx_2, c_ctx_2, ada_w_2, ada_b_2, norm1_g_2, norm2_g_2, ffn_w_up_2,
        ffn_conv_w_2, ffn_conv_b_2, ffn_w_down_2, gqa_w_in_2, gqa_q_norm_g_2, gqa_k_norm_g_2,
        gqa_w_out_2, mla_w_in_2, mla_q_norm_g_2, mla_kv_norm_g_2, mla_w_uq_2, mla_w_ukv_2,
        mla_w_out_2, diff_w_in_2, diff_lambda_2, diff_subln_g_2, diff_w_out_2, na_w_in_2,
        na_rpb_2, na_w_out_2, final_norm_g_2,
    )


_drawn_inputs = setup_inputs


def setup_inputs(seed=0):
    import zlib

    import numpy as np

    out = dict(_drawn_inputs(seed))
    spreads = {}
    factors = {'cmp_pe_k': 8.0,
     'cmp_pe_v': 8.0,
     'b_router_group': 5.32,
     'b_router_expert': 4.677,
     'norm1_g_2': 8.0,
     'norm2_g_2': 6.491,
     'ffn_conv_b_2': 7.038,
     'gqa_q_norm_g_2': 8.0,
     'gqa_k_norm_g_2': 8.0,
     'mla_q_norm_g_2': 8.0,
     'mla_kv_norm_g_2': 8.0,
     'final_norm_g_2': 2.785}
    for name, (base, spread) in spreads.items():
        noise = np.random.default_rng([zlib.crc32(name.encode()), seed]).standard_normal(out[name].shape)
        drawn = base * np.exp(spread * noise) if base else spread * noise
        out[name] = jnp.asarray(drawn.astype(out[name].dtype))
    for name, factor in factors.items():
        out[name] = (out[name] * factor).astype(out[name].dtype)
    return out
```

```python
import math
from contextlib import ExitStack


import numpy as np

import concourse.bass as bass
from concourse import mybir

F32 = mybir.dt.float32
I32 = mybir.dt.int32
ACT = mybir.ActivationFunctionType
ALU = mybir.AluOpType
AX = mybir.AxisListType
ds = bass.ds

P = 128
D = 1024
KD = D // P
T = 256
TT = T // P
T2 = 2 * T
EPS = 1e-6
NEG = -1e30

GRP, HPG, HD, ST, CONV = 4, 8, 64, 128, 4
HEADS = GRP * HPG
DIN = HEADS * HD
CONV_DIM = DIN + 2 * GRP * ST
NH, NKV, DH = 16, 2, 64
CMP, STRIDE, HID = 32, 16, 256
NCMP = (T - CMP) // STRIDE + 1
NG, EPG, FH = 4, 8, 256
NE = NG * EPG
SLOTS = 64
PAIRS = NE // 2
KVG = 4
QL, KVL, RD, ND = 384, 256, 32, 64
QK = ND + RD
FFN = 2816
FB = FFN // P

_sizes = (DIN, CONV_DIM, HEADS, NH * DH) + (NKV * DH,) * 6 + (3 * NH, D, D)
O_Z, O_XBC, O_DT, O_Q, O_KC, O_VC, O_KS, O_VS, O_KW, O_VW, O_GN, O_GS, O_GA = (
    sum(_sizes[:i]) for i in range(len(_sizes)))

SLOTW = 4096
NSLOT = 6

CONSTS = [("ident", P), ("ones", P), ("tri", P), ("trix", P), ("mneg", P), ("halves", P), ("pnsa", P),
          ("pgqa", P), ("dup0", P), ("dup1", P), ("pmla", QK), ("invf", 1), ("eps", 1), ("eps64", 1),
          ("gcos", T), ("gsin", T), ("mcos", T), ("msin", T), ("cneg", 2 * NCMP), ("c01", 2 * NCMP),
          ("iota", SLOTS), ("rev4", NG), ("rev8", EPG), ("zero", 4)]
CO, _o = {}, 0
for _n, _w in CONSTS:
    CO[_n] = (_o, _w)
    _o += _w
CW = _o

VECS = [("c", 8), ("b_ada", 48), ("norm1_g", 8), ("conv_b", 24), ("norm2_g", 8), ("final_g", 8),
        ("ssm_norm_g", 16), ("conv_w", 96), ("d_skip", 16), ("cmp_pe_k", 16), ("cmp_pe_v", 16),
        ("c_2", 8), ("c_ctx_2", 8), ("ada_b_2", 96), ("norm1_g_2", 16), ("norm2_g_2", 16),
        ("ffn_conv_b_2", 88), ("final_norm_g_2", 8), ("ffn_conv_w_2", 264), ("mla_q_norm_g_2", 3),
        ("mla_kv_norm_g_2", 2), ("gqa_q_norm_g_2", 1), ("gqa_k_norm_g_2", 1)]
VO, _o = {}, 0
for _n, _r in VECS:
    VO[_n] = _o
    _o += _r
VR = _o
VT = -(-VR // P)

STREAMS = {
    "ada": (12, 4096), "z": (4, 4096), "x": (4, 4096), "bc": (4, 2048), "wso": (4, 4096), "gs": (4, 2048),
    "kv": (2, 3072), "cw1": (2, 4096), "q": (4, 2048), "nga": (4, 4096), "wo": (4, 2048),
    "egu": (NE, 4096), "edn": (PAIRS, 4096),
    "ada2": (24, 4096), "gqa": (4, 3584), "gqao": (4, 2048), "up": (2 * FB, 2048), "down": (16, FB * P),
    "mla": (2, 3072), "mlah": (8, 1088), "mlao": (4, 2048),
}


TWO_PI = (6.28125, 0.0019350051879882812,
          2 * math.pi - 6.28125 - 0.0019350051879882812)
PI_BELOW = 3.1415925
MOE_PHASE, LAST_PHASE = 9, 25
SETUP_DMAS = 1 + VT + 8


class Unit:

    def __init__(self, scores=None, values=None, before=None, tiles=(), branches=1, w=0, gate=None):
        self.scores, self.values, self.before, self.tiles = scores, values, before, tiles
        self.branches, self.w, self.gate = branches, w, gate


def pack(w, *cols):
    w = np.concatenate([w[:, a:b] for a, b in cols], axis=1) if cols else w
    k, n = w.shape
    return w.reshape(k // P, P, n).transpose(1, 0, 2).reshape(P, -1)


def constants():
    c = np.zeros((P, CW), np.float32)

    def put(name, a):
        o, w = CO[name]
        c[:a.shape[0], o:o + w] = a

    i, j = np.arange(P)[:, None], np.arange(P)[None, :]
    put("ident", i == j)
    put("ones", np.ones((P, P)))
    put("tri", i <= j)
    put("trix", i < j)
    put("mneg", np.where(i <= j, 0.0, NEG))
    put("halves", i // 64 == j // 64)

    def rot(n, quarter):
        m = np.zeros((n, n))
        for o in range(n):
            b = o // quarter
            src, sign = (o + quarter, -1.0) if b % 2 == 0 else (o - quarter, 1.0)
            m[src, o] = sign
        return m

    put("pnsa", rot(P, 32))
    put("pgqa", rot(P, 16))
    m = np.zeros((QK, QK))
    m[ND:, ND:] = rot(RD, RD // 4)
    put("pmla", m)
    put("dup0", i == j % 64)
    put("dup1", i == 64 + j % 64)
    f = np.float32(10000.0) ** (-np.arange(0, DH, 2, dtype=np.float32) / np.float32(DH))
    put("invf", f[np.arange(P) % 32][:, None])
    put("eps", np.full((P, 1), EPS))
    put("eps64", np.full((P, 1), 64 * EPS))

    def axial(dim):
        t = np.arange(T)
        half = dim // 2
        inv = np.float32(10000.0) ** (-np.arange(0, half, 2, dtype=np.float32) / np.float32(half))
        ar = (t // 64).astype(np.float32)[:, None] * inv
        ac = (t % 64).astype(np.float32)[:, None] * inv
        a = np.concatenate([ar, ar, ac, ac], axis=1).T
        return np.cos(a), np.sin(a)

    gc, gs = axial(64)
    put("gcos", np.concatenate([gc, gc]))
    put("gsin", np.concatenate([gs, gs]))
    mc, ms = axial(RD)
    put("mcos", np.concatenate([np.ones((ND, T)), mc]))
    put("msin", np.concatenate([np.zeros((ND, T)), ms]))
    t = np.arange(P)[:, None, None] + P * np.arange(2)[None, :, None]
    ok = STRIDE * np.arange(NCMP)[None, None, :] + CMP - 1 <= t
    put("c01", ok.reshape(P, -1))
    put("cneg", np.where(ok, 0.0, NEG).reshape(P, -1))
    put("iota", np.broadcast_to(np.arange(SLOTS), (P, SLOTS)))
    put("rev4", np.broadcast_to(NG - np.arange(NG), (P, NG)))
    put("rev8", np.broadcast_to(EPG - np.arange(EPG), (P, EPG)))
    return c


def build(nc, dr):
    with ExitStack() as ctx:
        def sb(name, shape, dt=F32):
            return ctx.enter_context(nc.sbuf_tensor(name, shape, dt))

        def sem(name):
            return ctx.enter_context(nc.semaphore(name))

        bank = [ctx.enter_context(nc.psum_tensor(f"bank{i}", [P, 512], F32)) for i in range(8)]

        consts = sb("consts", [P, CW])
        cols = sb("cols", [P, VR])
        resid = sb("resid", [P, KD, T2])
        hn = sb("hn", [P, KD, T2])
        ring = sb("ring", [P, NSLOT * SLOTW])
        w_small = sb("w_small", [P, KD, HEADS + 3 * NH])
        w_route = sb("w_route", [P, KD, NG + NE])
        w_cmp2 = sb("w_cmp2", [P, 2, 192])
        rows32 = sb("rows32", [P, 3 * HEADS + NG + NE])
        ncos = sb("ncos", [P, T])
        nsin = sb("nsin", [P, T])
        ada = sb("ada", [P, 48, 2])
        mod = sb("mod", [P, 2, 2, KD])
        csil = sb("csil", [P, 3, KD])
        sq = sb("sq", [P, 2, 512])
        rstd = sb("rstd", [P, 512])
        arena = sb("arena", [P, 12600])

        def C(name, rows=P):
            o, w = CO[name]
            return consts[0:rows, o:o + w]

        def col(name, i=0):
            return cols[:, VO[name] + i:VO[name] + i + 1] if isinstance(i, int) else cols[:, ds(i + VO[name], 1)]

        def slot(s, w=SLOTW):
            return ring[:, s * SLOTW:s * SLOTW + w]

        class Place:

            def __init__(self, buf, at=0):
                self.buf, self.at = buf, at

            def __call__(self, *shape):
                n = int(np.prod(shape))
                ap = self.buf[:, self.at:self.at + n]
                self.at += n
                if len(shape) == 2:
                    ap = ap.rearrange("p (a b) -> p a b", a=shape[0])
                if len(shape) == 3:
                    ap = ap.rearrange("p (a b c) -> p a b c", a=shape[0], b=shape[1])
                return ap

        ident, ones = C("ident"), C("ones")

        setup_landed = sem("setup_landed")
        slot_landed = [sem(f"slot{i}_landed") for i in range(NSLOT)]
        slot_free = [sem(f"slot{i}_free") for i in range(NSLOT)]
        moe_landed = [sem(f"moe_slot{i}_landed") for i in range(NSLOT)]
        moe_free = [sem(f"moe_slot{i}_free") for i in range(NSLOT)]
        phase = sem("phase_ended")
        names = """
            vec_turned vec_ready csil_ready ada_mm ada_ready
            sq_ready sq_used ss_ready std_ready hn_scaled hn_ready rope_reduced rope_sin
            dt_pe dt_dve dt_act group_done gsm_ready
            ssm_z ssm_x ssm_acc ssm_taps ssm_conv ssm_tok ssm_bcb ssm_xw ssm_E ssm_Ex ssm_state ssm_stT ssm_seg
            ssm_exp ssm_M ssm_yd ssm_yoff ssm_yo ssm_y ssm_sq ssm_ss ssm_std
            out_mm out_sig out_ev gemm_mm gemm_ev
            kv_mm kv_raw kv_rot kv_roped kv_dup kv_ready gates_ready hid_mm hid_silu cmp_mm cmp_ready
            q_mm q_raw q_rot q_roped q_sq q_ss q_std q_normed
            cs_mm cs_max cs_exp cs_ready ct_mm ct_ev
            att_S att_max att_exp att_scaled att_T att_PT att_O att_ev
            route_pe route_dve route_act tok_mm tok_ev
            moe_S moe_X moe_Xev moe_h moe_silu moe_he moe_ct moe_ctev moe_y moe_yev moe_sc
            ffn_mm ffn_acc ffn_taps ffn_silu ffn_ev stored""".split()
        s = {n: sem(n) for n in names}

        def counts():
            return dict.fromkeys(names, 0)

        spare = ring[:, 4 * SLOTW:6 * SLOTW]
        pl = Place(arena)
        vec_rows = pl(VT, P)
        pos_i, pos_f, ang, turns, tmp_rope = pl(T), pl(T), pl(T), pl(T), pl(T)
        pl = Place(arena)
        gates = pl(2, 3 * NH)
        ncos8, nsin8 = pl(T), pl(T)
        merged = pl(KD, T)
        after_merged = pl.at
        dt_in, dt_a, dt_b, dt_c, dt_d = (pl(2, HEADS) for _ in range(5))
        ssm_small = pl(4 * 2, HEADS)
        gsm = pl(4 * 2, HPG)
        a_neg = pl(HEADS)
        ynorm = pl(DIN // P, T)
        zs = pl(4, T)
        conv = pl(6, T)
        xdt = pl(2, 512)
        yssm = pl(4, T)
        pl = Place(spare)
        xw, bcb, state_t, e_bc, yoff = pl(512), pl(3, P), pl(512), pl(512), pl(4, P)
        mexp = pl(2, 512)
        ysq = pl(4 * T)
        rs_ssm = pl(T)
        dt_wide = pl(512)
        out_sig = pl(4, T)
        out_tmp = pl(2, T)
        pl = Place(arena, after_merged)
        k_raw, k_roped, k_tmp = pl(3, T), pl(3, T), pl(3, T)
        vc_raw = pl(T)
        v_tok = pl(2, 2, P)
        kk = [pl(2, T) for _ in range(NKV)]
        blk = [pl(16, 2 * NCMP) for _ in range(2)]
        hid = pl(4, 2 * NCMP)
        k_cmp = pl(2 * NCMP)
        v_cmp = pl(2, DH)
        o_t = pl(KD, T)
        gsel = pl(3, 8)
        cs, cs_m, cs_s = pl(4, 2 * NCMP), pl(8), pl(8)
        ct = pl(8 * P)
        pl = Place(spare)
        q_raw, q_t, q_tmp = pl(2, T), pl(2, T), pl(2, T)
        probs = [pl(512) for _ in range(3)]
        probs_t = [pl(512) for _ in range(2)]
        nmax, psum_, pfac = pl(3, 2), pl(3, 2), pl(3, 2)
        pl = Place(arena)
        h_tok = pl(2, D)
        lg = pl(2, NG + NE)
        t2a, t2b, t2c, t2d, t2e, t2f = (pl(2, 1) for _ in range(6))
        g4a, g4b, g4c = (pl(2, NG) for _ in range(3))
        e8a, e8b, e8c, e8d, e8e = (pl(2, EPG) for _ in range(5))
        e32 = pl(2, NG, EPG)
        comb, selm, rank = pl(2, NE), pl(2, NE), pl(2, NE)
        cmax, cflag = pl(1), pl(1)
        rounds_i = pl(1)
        sel = [pl(2, P) for _ in range(2)]
        wsel = [pl(2, P) for _ in range(2)]
        x_t = pl(KD, P)
        hsil = pl(2, P)
        he = pl(2, P)
        y_slot = pl(D)
        c_t = pl(T)
        zeros = pl(512)
        pl = Place(arena)
        o2 = pl(KD, T2)
        gq_sq = pl(3, 512)
        gq_std = pl(3, 512)
        gq_n = pl(3, 512)
        gk = pl(512)
        gv = pl(4, DH)
        pl = Place(arena, KD * T2)
        cqn = pl(3, T)
        ckvn = pl(2, T2)
        kr_raw, kr_roped = pl(512), pl(512)
        kcat = [pl(512) for _ in range(2)]
        mv = pl(4, P)
        qcos, qsin = pl(T), pl(T)
        mq_raw, mq_t, mq_tmp = pl(2, T), pl(2, T), pl(2, T)
        cq_sq, ckv_sq = pl(3, T), pl(2, T2)
        act = Place(arena)(FB, T2)
        ffn_acc = Place(spare)(4, T2)

        block = ctx.enter_context(nc.Block())

        @block.sync
        def _(sp):
            used = [0] * NSLOT

            def stream(trips, plan):
                def body(i):
                    for name, sl, chunk in plan:
                        sp.wait_ge(slot_free[sl], i + used[sl] + 1)
                        sp.dma_start(slot(sl, STREAMS[name][1]), dr[name][bass.ts(chunk(i), P), :]) \
                            .then_inc(slot_landed[sl], 16)
                if trips > 1:
                    with sp.Fori(0, trips) as i:
                        body(i)
                else:
                    body(0)
                for _, sl, _ in plan:
                    used[sl] += trips

            sp.dma_start(consts[:, :], dr["consts"]).then_inc(setup_landed, 16)
            for v in range(VT):
                r = min(P, VR - v * P)
                sp.dma_start(vec_rows[0:r, v, :], dr["vecs"][v * P:v * P + r, :]).then_inc(setup_landed, 16)
            sp.dma_start(resid[:, :, 0:T], dr["xt"].rearrange("p (k t) -> p k t", k=KD)).then_inc(setup_landed, 16)
            sp.dma_start(resid[:, :, T:T2], dr["ctxt"].rearrange("p (k t) -> p k t", k=KD)).then_inc(setup_landed, 16)
            sp.dma_start(pos_i.bitcast(I32), dr["positions"]).then_inc(setup_landed, 16)
            sp.dma_start(rows32[:, 0:2 * HEADS], dr["ssm_rows"]).then_inc(setup_landed, 16)
            sp.dma_start(rows32[:, 3 * HEADS:], dr["route_rows"]).then_inc(setup_landed, 16)
            sp.dma_start(w_small[:, :, :], dr["w_small"].rearrange("p (k n) -> p k n", k=KD)).then_inc(setup_landed, 16)
            sp.dma_start(w_route[:, :, :], dr["w_route"].rearrange("p (k n) -> p k n", k=KD)).then_inc(setup_landed, 16)
            sp.dma_start(w_cmp2[:, :, :], dr["w_cmp2"].rearrange("p (k n) -> p k n", k=2)).then_inc(setup_landed, 16)

            def c4(q):
                return lambda i: i * 4 + q

            def c2(q):
                return lambda i: i * 2 + q

            def c1(i):
                return i

            def at(n):
                return lambda i: n + i

            stream(3, [("ada", q, c4(q)) for q in range(4)])
            stream(GRP, [("z", 0, c1), ("x", 1, c1), ("bc", 2, c1)])
            stream(2, [("wso", 0, c2(0)), ("gs", 1, c2(0)), ("wso", 2, c2(1)), ("gs", 3, c2(1))])
            stream(1, [("kv", 0, at(0)), ("kv", 1, at(1)), ("cw1", 2, at(0)), ("cw1", 3, at(1))])
            stream(4, [("q", 0, c1)])
            stream(2, [("nga", 1, c2(0)), ("nga", 2, c2(1))])
            stream(2, [("wo", 3, c2(0)), ("wo", 0, c2(1))])

            for sl in range(4):
                sp.wait_ge(slot_free[sl], used[sl] + 1)
            sp.wait_ge(s["route_dve"], 4)
            rounds = sp.value_load(rounds_i.bitcast(I32)[0:1, 0:1], min_val=1, max_val=4)
            with sp.Fori(0, rounds) as r:
                with sp.Fori(0, PAIRS // 2) as i:
                    for q in range(2):
                        for c, name in enumerate(("egu", "egu", "edn")):
                            sl = 3 * q + c
                            sp.wait_ge(moe_free[sl], r * (PAIRS // 2) + i + 1)
                            chunk = i * 4 + 2 * q + c if c < 2 else i * 2 + q
                            sp.dma_start(slot(sl), dr[name][bass.ts(chunk, P), :]).then_inc(moe_landed[sl], 16)
            sp.wait_ge(phase, 3 * MOE_PHASE)

            for l in range(2):
                stream(3, [("ada2", q, (lambda q: lambda i: i * 4 + q + 12 * l)(q)) for q in range(4)])
                if l == 0:
                    stream(4, [("gqa", 0, c1)])
                    stream(2, [("gqao", 1, c2(0)), ("gqao", 2, c2(1))])
                else:
                    stream(1, [("mla", 0, at(0)), ("mla", 1, at(1))])
                    stream(4, [("mlah", 2, c2(0)), ("mlah", 3, c2(1))])
                    stream(2, [("mlao", 0, c2(0)), ("mlao", 1, c2(1))])
                stream(FB // 2, [("up", 2, (lambda i: i * 2 + FB * l)), ("up", 3, (lambda i: i * 2 + 1 + FB * l))])
                stream(2, [("down", q, (lambda q: lambda i: i * 4 + q + 8 * l)(q)) for q in range(4)])

            sp.wait_ge(phase, 3 * LAST_PHASE)
            sp.dma_start(dr["out"].rearrange("p (k t) -> p k t", k=KD), resid[:, :, 0:T]).then_inc(s["stored"], 16)
            sp.wait_ge(s["stored"], 16)

        @block.tensor
        def _(pe):
            used = [0] * NSLOT
            n = counts()
            ended = [0]
            mm, tr = nc.tensor.matmul, nc.tensor.transpose
            for sl in range(NSLOT):
                pe.sem_inc(slot_free[sl], 1)
                pe.sem_inc(moe_free[sl], 1)
            pe.sem_inc(s["att_T"], 3)
            pe.sem_inc(s["att_O"], 2)
            pe.sem_inc(s["moe_X"], 2)
            pe.sem_inc(s["moe_sc"], 1)

            def end_phase():
                pe.drain().then_inc(phase, 1)
                ended[0] += 1
                pe.wait_ge(phase, 3 * ended[0])

            def landed(sl, i=0):
                pe.wait_ge(slot_landed[sl], (i + used[sl] + 1) * 16)

            def free(*slots):
                for sl in slots:
                    pe.drain().then_inc(slot_free[sl], 1)

            def taken(trips, *slots):
                for sl in slots:
                    used[sl] += trips

            def dot(out, lhs, rhs, k):
                for i in range(k):
                    last = mm(out, lhs(i), rhs(i), start=i == 0, stop=i == k - 1)
                return last

            def adaln(ncol, which):
                with pe.Fori(0, 3) as i:
                    for q in range(4):
                        landed(q, i)
                        for b in range(4):
                            last = dot(bank[7][:, ds(i * 32 + (q * 8 + b * 2), ncol)],
                                       lambda k: slot(q)[:, k * 512 + b * P:k * 512 + b * P + P],
                                       lambda k: csil[:, which:which + ncol, k], KD)
                        last.then_inc(slot_free[q], 1)
                taken(3, 0, 1, 2, 3)
                pe.drain().then_inc(s["ada_mm"], 1)

            def norm(w):
                for k in range(KD):
                    pe.wait_ge(s["sq_ready"], n["sq_ready"] + k + 1)
                    last = mm(bank[0][:, 0:w], ones, sq[:, k % 2, 0:w], start=k == 0, stop=k == KD - 1)
                    if k < KD - 2:
                        last.then_inc(s["sq_used"], 1)
                last.then_inc(s["ss_ready"], 1)
                n["sq_ready"] += KD
                n["hn_ready"] += KD
                pe.wait_ge(s["hn_ready"], n["hn_ready"])

            def gemm(trips, slots, per, kb, rhs, w):
                q4 = len(slots) * per
                with pe.Fori(0, trips) as i:
                    for c, sl in enumerate(slots):
                        landed(sl, i)
                        for b in range(per):
                            m = c * per + b
                            pe.wait_ge(s["gemm_ev"], i * q4 + (n["gemm_mm"] + m + 1))
                            last = dot(bank[m % 4][:, 0:w],
                                       lambda k: slot(sl)[:, (k * per + b) * P:(k * per + b + 1) * P],
                                       lambda k: rhs(k), kb)
                            last.then_inc(s["gemm_mm"], 1)
                        free(sl)
                taken(trips, *slots)
                n["gemm_mm"] += trips * q4

            def gated_out(pairs, kb, rhs, gate_at):
                with pe.Fori(0, 2) as i:
                    for c, (sl, gsl) in enumerate(pairs):
                        landed(sl, i)
                        if gsl != sl:
                            landed(gsl, i)
                        for b in range(2):
                            m = c * 2 + b
                            pe.wait_ge(s["out_ev"], i * 4 + (n["out_mm"] + m + 1))
                            dot(bank[m][:, 0:T], lambda k: slot(sl)[:, (k * 2 + b) * P:(k * 2 + b + 1) * P], rhs, kb)
                            last = dot(bank[m][:, T:T2],
                                       lambda k: slot(gsl)[:, gate_at + (k * 2 + b) * P:gate_at + (k * 2 + b + 1) * P],
                                       lambda k: hn[:, k, 0:T], KD)
                            last.then_inc(s["out_mm"], 1)
                        free(*sorted({sl, gsl}))
                for sl, gsl in pairs:
                    taken(2, *{sl, gsl})
                n["out_mm"] += 8

            def attention(units, done):
                U = len(units)
                for t in range(U + 3):
                    if t < U:
                        pe.wait_ge(s["att_exp"], done + (t + 1))
                        units[t].scores(bank[t % 3]).then_inc(s["att_S"], 1)
                    if 0 <= t - 2 < U:
                        v = t - 2
                        pe.wait_ge(s["att_scaled"], done + (v + 1))
                        pe.wait_ge(s["att_PT"], done + (v + 1))
                        for x, c in enumerate(units[v].tiles):
                            last = tr(bank[3 + v % 2][:, x * P:(x + 1) * P], probs[v % 3][:, c:c + P], ident)
                        last.then_inc(s["att_T"], 1)
                    if 0 <= t - 3 < U:
                        v = t - 3
                        if units[v].before:
                            units[v].before()
                        pe.wait_ge(s["att_PT"], done + (v + 3))
                        units[v].values(probs_t[v % 2]).then_inc(s["att_O"], 1)

            pe.wait_ge(setup_landed, 16 * SETUP_DMAS)
            for v in range(VT):
                r = min(P, VR - v * P)
                last = tr(bank[v][:, 0:r], vec_rows[0:r, v, :], ident[0:r, 0:r])
            last.then_inc(s["vec_turned"], 1)
            pe.wait_ge(s["csil_ready"], 1)
            adaln(1, 0)
            norm(T)
            end_phase()

            for c in range(2):
                last = dot(bank[7][:, c * 80:(c + 1) * 80], lambda k: hn[:, k, c * P:(c + 1) * P],
                           lambda k: w_small[:, k, :], KD)
            last.then_inc(s["dt_pe"], 1)
            pe.wait_ge(s["dt_dve"], 3)
            for c in range(2):
                mm(bank[6][:, c * HEADS:(c + 1) * HEADS], C("tri"), ssm_small[:, c, :], start=True, stop=True)
            mm(bank[6][:, 2 * HEADS:3 * HEADS], ones, ssm_small[:, 0, :], start=True, stop=True).then_inc(s["dt_pe"], 1)

            xt = [conv[:, b, :] for b in range(4)]
            b_t, c_tt = conv[:, 4, :], conv[:, 5, :]
            dtag = [gsm[:, c, :] for c in range(2)]
            with pe.Fori(0, GRP) as g:
                pe.wait_ge(s["group_done"], g + 1)
                landed(0, g)
                for b in range(4):
                    last = dot(bank[b // 2][:, (b % 2) * T:(b % 2 + 1) * T],
                               lambda k: slot(0)[:, k * 512 + b * P:k * 512 + b * P + P], lambda k: hn[:, k, 0:T], KD)
                last.then_inc(s["ssm_z"], 1)
                landed(1, g)
                for b in range(4):
                    last = dot(bank[2 + b // 2][:, (b % 2) * T:(b % 2 + 1) * T],
                               lambda k: slot(1)[:, k * 512 + b * P:k * 512 + b * P + P], lambda k: hn[:, k, 0:T], KD)
                last.then_inc(s["ssm_x"], 1)
                landed(2, g)
                for b in range(2):
                    last = dot(bank[4][:, b * T:(b + 1) * T],
                               lambda k: slot(2)[:, k * T + b * P:k * T + b * P + P], lambda k: hn[:, k, 0:T], KD)
                last.then_inc(s["ssm_x"], 1)
                free(0, 1, 2)
                pe.wait_ge(s["ssm_conv"], g + 1)
                for c in range(2):
                    for b in range(4):
                        tr(bank[5 + c][:, b * P:(b + 1) * P], xt[b][:, c * P:(c + 1) * P], ident)
                tr(bank[4][:, 0:P], b_t[:, 0:P], ident)
                for c in range(2):
                    last = mm(bank[4][:, (1 + c) * P:(2 + c) * P], b_t[:, c * P:(c + 1) * P], c_tt[:, c * P:(c + 1) * P],
                              start=True, stop=True)
                last.then_inc(s["ssm_tok"], 1)
                pe.wait_ge(s["gsm_ready"], g + 1)
                for pr in range(4):
                    last = mm(bank[7][:, pr * P:(pr + 1) * P], dt_wide[:, pr * P:(pr + 1) * P], C("tri"),
                              start=True, stop=True)
                last.then_inc(s["ssm_E"], 1)
                pe.wait_ge(s["ssm_xw"], g + 1)
                pe.wait_ge(s["ssm_bcb"], g + 1)
                mm(bank[5][:, :], bcb[:, 0, :], xw, start=True, stop=True).then_inc(s["ssm_state"], 1)

                def within(u):
                    c, hh = u // 2, u % 2
                    pe.wait_ge(s["ssm_M"], g * 4 + (u + 1))
                    for h in range(4):
                        head = 4 * hh + h
                        o = (h // 2) * T + c * P
                        last = mm(bank[2 + hh][64 * (h % 2):64 * (h % 2) + 64, o:o + P],
                                  xdt[:, c, head * HD:(head + 1) * HD], mexp[:, u % 2, h * P:(h + 1) * P],
                                  start=True, stop=True)
                    last.then_inc(s["ssm_yd"], 1)

                for u in range(4):
                    c, hh = u // 2, u % 2
                    if u >= 2:
                        pe.wait_ge(s["ssm_exp"], g * 4 + (u - 1))
                    mm(bank[u % 2][:, :], ident, C("mneg").unsqueeze(1).to_broadcast([P, 4, P]), start=True, stop=False)
                    for h in range(4):
                        head = 4 * hh + h
                        last = mm(bank[u % 2][:, h * P:(h + 1) * P], dtag[c][:, head:head + 1].to_broadcast([P, P]),
                                  C("tri"), start=False, stop=h == 3)
                    last.then_inc(s["ssm_seg"], 1)
                    if u >= 1:
                        within(u - 1)
                pe.wait_ge(s["ssm_stT"], g + 1)
                for pr in range(4):
                    last = mm(bank[6][:, pr * P:(pr + 1) * P], state_t[:, pr * P:(pr + 1) * P], c_tt[:, P:T],
                              start=True, stop=True)
                last.then_inc(s["ssm_yoff"], 1)
                within(3)
                pe.wait_ge(s["ssm_sq"], g + 1)
                dot(bank[7][:, 0:T], lambda b: ones, lambda b: ysq[:, b * T:(b + 1) * T], 4).then_inc(s["ssm_ss"], 1)
            taken(GRP, 0, 1, 2)
            pe.wait_ge(s["group_done"], GRP + 1)
            end_phase()
            gated_out([(0, 1), (2, 3)], DIN // P, lambda k: ynorm[:, k, :], 0)
            end_phase()

            def kvw(sl, x):
                return lambda k: slot(sl)[:, k * 384 + x * P:k * 384 + (x + 1) * P]

            def hx(k):
                return hn[:, k, 0:T]

            landed(0)
            dot(bank[0][:, 0:T], kvw(0, 0), hx, KD)
            dot(bank[0][:, T:T2], kvw(0, 1), hx, KD)
            dot(bank[1][:, 0:T], kvw(0, 2), hx, KD)
            landed(1)
            dot(bank[1][:, T:T2], kvw(1, 1), hx, KD)
            for br in range(2):
                for t in range(TT):
                    last = dot(bank[2][:, (br * 2 + t) * P:(br * 2 + t + 1) * P], lambda k: hn[:, k, t * P:(t + 1) * P],
                               kvw(1, 2 * br), KD)
            last.then_inc(s["kv_mm"], 1)
            free(0, 1)
            pe.wait_ge(s["kv_raw"], 1)
            mm(bank[3][:, :], C("pnsa"), k_raw[:, 0:2, :], start=True, stop=True)
            mm(bank[4][:, 0:T], C("pnsa"), k_raw[:, 2, :], start=True, stop=True).then_inc(s["kv_rot"], 1)
            pe.wait_ge(s["kv_roped"], 1)
            for g in range(NKV):
                dup = C(f"dup{g}")
                mm(bank[5][:, g * T:(g + 1) * T], dup, k_roped[:, 0, :], start=True, stop=True)
                mm(bank[6][:, g * T:(g + 1) * T], dup, vc_raw, start=True, stop=True)
                last = mm(bank[g][:, :], dup, k_roped[:, 1:3, :], start=True, stop=True)
            last.then_inc(s["kv_dup"], 1)
            pe.wait_ge(s["kv_ready"], 1)
            for x in range(2):
                landed(2 + x)
                for hb in range(2):
                    o = (x * 2 + hb) * 2 * NCMP
                    last = dot(bank[7][:, o:o + 2 * NCMP],
                               lambda k: slot(2 + x)[:, k * HID + hb * P:k * HID + hb * P + P],
                               lambda k: blk[x][:, k, :], 16)
            last.then_inc(s["hid_mm"], 1)
            free(2, 3)
            taken(1, 0, 1, 2, 3)
            pe.wait_ge(s["hid_silu"], 1)
            dot(bank[4][:, 256:256 + 2 * NCMP], lambda k: w_cmp2[:, k, 0:P], lambda k: hid[:, k, :], 2)
            for g in range(NKV):
                last = dot(bank[4][0:NCMP, 320 + g * DH:320 + (g + 1) * DH],
                           lambda k: hid[:, 2 + k, g * NCMP:(g + 1) * NCMP], lambda k: w_cmp2[:, k, P:P + DH], 2)
            last.then_inc(s["cmp_mm"], 1)
            pe.wait_ge(s["cmp_ready"], 1)
            end_phase()
            with pe.Fori(0, 4) as j:
                landed(0, j)
                for u in range(2):
                    last = dot(bank[6][:, u * T:(u + 1) * T], lambda k: slot(0)[:, (2 * k + u) * P:(2 * k + u + 1) * P], hx, KD)
                last.then_inc(s["q_mm"], 1)
                free(0)
                pe.wait_ge(s["q_raw"], j + 1)
                mm(bank[7][:, :], C("pnsa"), q_raw, start=True, stop=True).then_inc(s["q_rot"], 1)
                pe.wait_ge(s["q_roped"], j + 1)

                def q_of(u, half, qt):
                    return q_t[64 * half:64 * half + 64, u, qt * P:(qt + 1) * P]

                order = [(u, half, qt) for u in range(2) for half in range(2) for qt in range(2)]
                for t, (u, half, qt) in enumerate(order):
                    last = mm(bank[7 - half][:, (2 * u + qt) * NCMP:(2 * u + qt + 1) * NCMP], q_of(u, half, qt),
                              k_cmp[64 * half:64 * half + 64, u * NCMP:(u + 1) * NCMP], start=True, stop=True)
                last.then_inc(s["cs_mm"], 1)

                def turn_cmp():
                    pe.wait_ge(s["cs_ready"], j + 1)
                    for t in range(8):
                        last = tr(bank[6 + t // 4][0:NCMP, (t % 4) * P:(t % 4 + 1) * P],
                                  cs[:, t // 2, (t % 2) * NCMP:(t % 2 + 1) * NCMP], ident)
                    last.then_inc(s["ct_mm"], 1)
                    pe.wait_ge(s["ct_ev"], j + 1)
                    pe.wait_ge(s["att_ev"], j + 1)

                def unit(t):
                    u, half, qt = order[t]
                    w = P * (qt + 1)

                    def scores(b):
                        kh = kk[u][64 * half:64 * half + 64, :, 0:w]
                        mm(b[:, 0:2 * w], q_of(u, half, qt), kh, start=True, stop=False)
                        diag = b[:, 0:2 * w].rearrange("p (b k) -> p b k", b=2)[:, :, qt * P:w]
                        return mm(diag, C("mneg"), ident.unsqueeze(1).to_broadcast([P, 2, P]), start=False, stop=True)

                    def values(pt):
                        out = bank[5][64 * half:64 * half + 64, u * T + qt * P:u * T + (qt + 1) * P]
                        for x in range(2 * (qt + 1)):
                            br, kt = x // (qt + 1), x % (qt + 1)
                            mm(out, v_tok[:, br, kt, u * DH:(u + 1) * DH], pt[:, x * P:(x + 1) * P], start=x == 0, stop=False)
                        return mm(out, v_cmp[0:NCMP, u, :], ct[0:NCMP, t * P:(t + 1) * P], start=False, stop=True)

                    return Unit(scores=scores, values=values, before=turn_cmp if t == 0 else None,
                                           tiles=[x * P for x in range(2 * (qt + 1))])

                attention([unit(t) for t in range(8)], j * 8)
            taken(4, 0)
            n["att_S"] += 32
            n["q_mm"] += 4
            n["att_ev"] += 4
            pe.wait_ge(s["att_ev"], n["att_ev"] + 1)
            end_phase()
            gated_out([(1, 1), (2, 2)], KD, lambda k: o_t[:, k, :], 2048)
            end_phase()
            gemm(2, (3, 0), 2, KD, lambda k: merged[:, k, :], T)
            end_phase()
            norm(T)
            end_phase()

            for t in range(TT):
                last = dot(bank[0][:, t * 36:(t + 1) * 36], lambda k: hn[:, k, t * P:(t + 1) * P],
                           lambda k: w_route[:, k, :], KD)
            last.then_inc(s["route_pe"], 1)
            for t in range(TT):
                for k in range(KD):
                    last = tr(bank[2 + 2 * t + k // 4][:, (k % 4) * P:(k % 4 + 1) * P], hn[:, k, t * P:(t + 1) * P], ident)
            last.then_inc(s["tok_mm"], 1)
            pe.wait_ge(s["route_dve"], 3)
            mm(bank[1][:, 0:NE], C("trix"), selm[:, 0, :], start=True, stop=True)
            mm(bank[1][:, NE:2 * NE], C("trix"), selm[:, 1, :], start=True, stop=False)
            mm(bank[1][:, NE:2 * NE], ones, selm[:, 0, :], start=False, stop=True)
            mm(bank[1][:, 2 * NE:3 * NE], ones, selm[:, 0, :], start=True, stop=False)
            mm(bank[1][:, 2 * NE:3 * NE], ones, selm[:, 1, :], start=False, stop=True).then_inc(s["route_pe"], 1)
            pe.wait_ge(s["route_dve"], 4)
            pe.wait_ge(s["tok_ev"], 1)
            rounds = pe.value_load(rounds_i.bitcast(I32)[0:1, 0:1], min_val=1, max_val=4)
            for b in range(4):
                mm(bank[b][:, :], zeros[:, 0:P], zeros, start=True, stop=True, skip_group_check=True)
            with pe.Fori(0, rounds) as r:
                with pe.Fori(0, PAIRS // 2) as i:
                    trip = r * (PAIRS // 2) + i
                    for q in range(2):
                        p = trip * 2 + q
                        pe.wait_ge(s["moe_S"], p + 1)
                        pe.wait_ge(s["moe_yev"], p * 2 + 2)
                        for k in range(KD):
                            last = dot(bank[4 + k // 4][:, (k % 4) * P:(k % 4 + 1) * P],
                                       lambda t: h_tok[:, t, k * P:(k + 1) * P], lambda t: sel[q][:, t, :], TT)
                        last.then_inc(s["moe_X"], 1)
                        for t in range(TT):
                            last = tr(bank[6][:, t * P:(t + 1) * P], wsel[q][:, t, :], ident)
                        last.then_inc(s["moe_ct"], 1)
                        pe.wait_ge(s["moe_Xev"], p * 2 + 2)
                        pe.wait_ge(s["moe_ctev"], p + 1)
                        for e in range(2):
                            sl = 3 * q + e
                            pe.wait_ge(moe_landed[sl], (trip + 1) * 16)
                            for m in range(4):
                                last = dot(bank[6 + e][:, m * SLOTS:(m + 1) * SLOTS],
                                           lambda k: slot(sl)[:, k * 512 + m * P:k * 512 + (m + 1) * P],
                                           lambda k: x_t[:, k, e * SLOTS:(e + 1) * SLOTS], KD)
                            last.then_inc(s["moe_h"], 1)
                        pe.drain().then_inc(moe_free[3 * q], 1)
                        pe.drain().then_inc(moe_free[3 * q + 1], 1)
                        sl = 3 * q + 2
                        pe.wait_ge(moe_landed[sl], (trip + 1) * 16)
                        for e in range(2):
                            pe.wait_ge(s["moe_he"], p * 2 + (e + 1))
                            for half in range(2):
                                last = dot(bank[4 + half][e * SLOTS:(e + 1) * SLOTS, :],
                                           lambda k: he[:, e, k * SLOTS:(k + 1) * SLOTS],
                                           lambda k: slot(sl)[:, (e * 2 + k) * D + half * 512:(e * 2 + k) * D + half * 512 + 512],
                                           2)
                        last.then_inc(s["moe_y"], 1)
                        pe.drain().then_inc(moe_free[sl], 1)
                        pe.wait_ge(s["moe_yev"], p * 2 + 4)
                        for m in range(KD):
                            last = mm(bank[m // 2][:, (m % 2) * T:(m % 2 + 1) * T], y_slot[:, m * P:(m + 1) * P], c_t,
                                      start=False, stop=True, skip_group_check=True)
                        last.then_inc(s["moe_sc"], 1)
            end_phase()
            assert ended[0] == MOE_PHASE
            end_phase()
            norm(T)
            end_phase()

            for l in range(2):
                adaln(2, 1)
                norm(T2)
                end_phase()
                if l == 0:
                    with pe.Fori(0, KVG) as g:
                        landed(0, g)

                        def wq(b):
                            return lambda k: slot(0)[:, k * 448 + b * P:k * 448 + (b + 1) * P]

                        for b in range(3):
                            dot(bank[b][:, :], wq(b), lambda k: hn[:, k, :], KD)
                        for t in range(4):
                            last = dot(bank[3][:, t * DH:(t + 1) * DH], lambda k: hn[:, k, t * P:(t + 1) * P],
                                       lambda k: slot(0)[:, k * 448 + 384:k * 448 + 448], KD)
                        last.then_inc(s["q_mm"], 1)
                        free(0)
                        pe.wait_ge(s["q_sq"], g + 1)
                        for b in range(3):
                            last = mm(bank[5 + b][:, :], C("halves"), gq_sq[:, b, :], start=True, stop=True)
                        last.then_inc(s["q_ss"], 1)
                        pe.wait_ge(s["q_normed"], g + 1)
                        for b in range(3):
                            last = mm(bank[5 + b][:, 0:T], C("pgqa"), gq_n[:, b, 0:T], start=True, stop=True)
                        last.then_inc(s["q_rot"], 1)
                        pe.wait_ge(s["q_roped"], g + (4 + 1))

                        def unit(b, half, qt):
                            x = qt < 2
                            nk = 4 if x else 2
                            k0 = 0 if x else T

                            def scores(bk):
                                return mm(bk[:, 0:nk * P], gq_n[64 * half:64 * half + 64, b, qt * P:(qt + 1) * P],
                                          gq_n[64 * half:64 * half + 64, 2, k0:T2], start=True, stop=True)

                            def values(pt):
                                out = bank[5 + b][64 * half:64 * half + 64, qt * P:(qt + 1) * P]
                                return dot(out, lambda k: gv[:, k + k0 // P, :], lambda k: pt[:, k * P:(k + 1) * P], nk)

                            return Unit(scores=scores, values=values, before=None,
                                                   tiles=[k * P for k in range(nk)])

                        attention([unit(b, h, t) for b in range(2) for h in range(2) for t in range(4)], g * 16 + n["att_S"])
                        pe.wait_ge(s["att_ev"], g + (n["att_ev"] + 2))
                    taken(4, 0)
                    n["att_S"] += 64
                    n["att_ev"] += 4
                    end_phase()
                    gemm(2, (1, 2), 2, KD, lambda k: o2[:, k, :], T2)
                else:
                    landed(0)
                    for b in range(3):
                        last = dot(bank[1 + b][:, 0:T], lambda k: slot(0)[:, k * 384 + b * P:k * 384 + (b + 1) * P],
                                   lambda k: hn[:, k, 0:T], KD)
                    landed(1)
                    for b in range(2):
                        dot(bank[4 + b][:, :], lambda k: slot(1)[:, k * 288 + b * P:k * 288 + (b + 1) * P],
                            lambda k: hn[:, k, :], KD)
                    dot(bank[6][ND:QK, :], lambda k: slot(1)[:, k * 288 + 256:k * 288 + 288], lambda k: hn[:, k, :], KD) \
                        .then_inc(s["kv_mm"], 1)
                    free(0, 1)
                    taken(1, 0, 1)
                    pe.wait_ge(s["kv_raw"], 2)
                    dot(bank[0][:, 0:T], lambda b: ones, lambda b: cq_sq[:, b, :], 3)
                    dot(bank[7][:, :], lambda b: ones, lambda b: ckv_sq[:, b, :], 2).then_inc(s["kv_rot"], 1)
                    pe.wait_ge(s["kv_ready"], 2)
                    mm(bank[6][ND:QK, 0:T], C("pmla")[ND:QK, ND:QK], kr_raw[ND:QK, 0:T], start=True, stop=True) \
                        .then_inc(s["kv_dup"], 1)
                    pe.wait_ge(s["cmp_ready"], 2)
                    end_phase()
                    with pe.Fori(0, 4) as i:
                        for q in range(2):
                            sl = 2 + q
                            it = i * 2 + q
                            landed(sl, i)
                            uq = slot(sl)[:, 0:576].rearrange("p (k h c) -> p k h c", k=3, h=2)
                            ukv = slot(sl)[:, 576:1088].rearrange("p (k h c) -> p k h c", k=2, h=2)
                            pe.wait_ge(s["att_ev"], it + (n["att_ev"] + 1))
                            for hh in range(2):
                                dot(bank[6][0:QK, hh * T:(hh + 1) * T], lambda k: uq[:, k, hh, :], lambda k: cqn[:, k, :], 3)
                                dot(bank[hh][0:ND, :], lambda k: ukv[:, k, hh, 0:ND], lambda k: ckvn[:, k, :], 2)
                            for t in range(4):
                                last = dot(bank[2][:, t * P:(t + 1) * P], lambda k: ckvn[:, k, t * P:(t + 1) * P],
                                           lambda k: ukv[:, k, :, ND:P], 2)
                            last.then_inc(s["q_mm"], 1)
                            free(sl)
                            pe.wait_ge(s["q_raw"], it + (4 + 1))
                            mm(bank[7][0:QK, :], C("pmla", QK), mq_raw[0:QK], start=True, stop=True).then_inc(s["q_rot"], 1)
                            pe.wait_ge(s["q_roped"], it + (8 + 1))

                            def unit(hh, qt):
                                def scores(bk):
                                    return mm(bk[:, :], mq_t[0:QK, hh, qt * P:(qt + 1) * P], kcat[hh][0:QK, :],
                                              start=True, stop=True)

                                def values(pt):
                                    return dot(bank[5][64 * hh:64 * hh + 64, qt * P:(qt + 1) * P],
                                               lambda k: mv[:, k, hh * 64:(hh + 1) * 64],
                                               lambda k: pt[:, k * P:(k + 1) * P], 4)

                                return Unit(scores=scores, values=values, before=None,
                                                       tiles=[k * P for k in range(4)])

                            attention([unit(h, t) for h in range(2) for t in range(2)], it * 4 + n["att_S"])
                    taken(4, 2, 3)
                    n["att_S"] += 32
                    n["att_ev"] += 8
                    pe.wait_ge(s["att_ev"], n["att_ev"] + 1)
                    end_phase()
                    gemm(2, (0, 1), 2, KD, lambda k: o2[:, k, 0:T], T)
                end_phase()
                w = T2 if l == 0 else T
                norm(w)
                end_phase()
                with pe.Fori(0, FB // 2) as i:
                    for q in range(2):
                        landed(2 + q, i)
                        pe.wait_ge(s["ffn_ev"], i * 2 + (n["ffn_ev"] + q + 1))
                        for x in range(2):
                            dot(bank[2 * q + x][:, 0:w], lambda k: slot(2 + q)[:, (2 * k + x) * P:(2 * k + x + 1) * P],
                                lambda k: hn[:, k, 0:w], KD).then_inc(s["ffn_mm"], 1)
                        free(2 + q)
                taken(FB // 2, 2, 3)
                n["ffn_ev"] += FB
                end_phase()
                gemm(2, (0, 1, 2, 3), 1, FB, lambda k: act[:, k, 0:w], w)
                end_phase()
            norm(T)
            end_phase()

        @block.scalar
        def _(act_e):
            n = counts()
            norms = [0]
            ended = [0]
            fn = nc.scalar.activation
            act_e.sem_inc(s["att_exp"], 3)
            act_e.sem_inc(s["att_PT"], 2)
            act_e.sem_inc(s["moe_yev"], 2)

            def end_phase():
                act_e.drain().then_inc(phase, 1)
                ended[0] += 1
                act_e.wait_ge(phase, 3 * ended[0])

            def norm(w, shift=None):
                b = norms[0]
                for k in range(KD):
                    if k >= 2:
                        act_e.wait_ge(s["sq_used"], 6 * b + k - 1)
                    fn(sq[:, k % 2, 0:w], resid[:, k, 0:w], ACT.Square).then_inc(s["sq_ready"], 1)
                act_e.wait_ge(s["ss_ready"], b + 1)
                fn(rstd[:, 0:w], bank[0][:, 0:w], ACT.Sqrt, scale=1.0 / D, bias=C("eps")).then_inc(s["std_ready"], 1)
                if shift is not None:
                    for k in range(KD):
                        act_e.wait_ge(s["hn_scaled"], n["hn_scaled"] + k + 1)
                        for part in range(w // T):
                            x = hn[:, k, part * T:(part + 1) * T]
                            last = fn(x, x, ACT.Identity, bias=ada[:, shift + k, part:part + 1])
                        last.then_inc(s["hn_ready"], 1)
                    n["hn_scaled"] += KD
                norms[0] += 1

            def gated_out():
                with act_e.Fori(0, 2) as i:
                    for m in range(4):
                        act_e.wait_ge(s["out_mm"], i * 4 + (n["out_mm"] + m + 1))
                        act_e.wait_ge(s["out_ev"], i * 4 + (n["out_mm"] + m + 1))
                        fn(out_sig[:, m, :], bank[m][:, T:T2], ACT.Sigmoid).then_inc(s["out_sig"], 1)
                n["out_mm"] += 8

            def attention(units, done, after):
                U = len(units)
                for t in range(U + 2):
                    if t < U:
                        u = units[t]
                        act_e.wait_ge(s["att_max"], done + (t + 1))
                        act_e.wait_ge(s["att_T"], done + (t + 1))
                        for b in range(u.branches):
                            o = b * u.w
                            last = fn(probs[t % 3][:, o:o + u.w], bank[t % 3][:, o:o + u.w], ACT.Exp,
                                      bias=nmax[:, t % 3, b:b + 1], accum_out=psum_[:, t % 3, b:b + 1])
                        last.then_inc(s["att_exp"], 1)
                    if t >= 2:
                        v = t - 2
                        w = units[v].branches * units[v].w
                        act_e.wait_ge(s["att_T"], done + (v + 4))
                        act_e.wait_ge(s["att_O"], done + (v + 1))
                        fn(probs_t[v % 2][:, 0:w], bank[3 + v % 2][:, 0:w], ACT.Copy).then_inc(s["att_PT"], 1)
                    if t in after:
                        after[t]()

            act_e.wait_ge(s["vec_turned"], 1)
            for v in range(VT):
                r = min(P, VR - v * P)
                fn(cols[:, v * P:v * P + r], bank[v][:, 0:r], ACT.Copy)
            act_e.drain()
            for x, name in enumerate(("c", "c_2", "c_ctx_2")):
                last = fn(csil[:, x, :], cols[:, VO[name]:VO[name] + KD], ACT.Silu)
            last.then_inc(s["csil_ready"], 1)
            act_e.wait_ge(s["rope_reduced"], 1)
            fn(nsin[:, :], ang, ACT.Sin)
            fn(ncos[:, :], tmp_rope, ACT.Sin).then_inc(s["rope_sin"], 1)
            act_e.wait_ge(s["ada_ready"], 1)
            norm(T, 0)
            end_phase()

            act_e.wait_ge(s["dt_pe"], 1)
            fn(gates, bank[7][:, 0:160].rearrange("p (c n) -> p c n", c=2)[:, :, HEADS:80], ACT.Sigmoid).then_inc(s["gates_ready"], 1)
            fn(a_neg, rows32[:, HEADS:2 * HEADS], ACT.Exp)
            act_e.wait_ge(s["dt_dve"], 1)
            fn(dt_b, dt_a, ACT.Exp).then_inc(s["dt_act"], 1)
            act_e.wait_ge(s["dt_dve"], 2)
            fn(dt_a, dt_c, ACT.Ln).then_inc(s["dt_act"], 1)
            act_e.wait_ge(s["dt_dve"], 4)
            fn(ssm_small[:, 6, :], ssm_small[:, 7, :], ACT.Exp).then_inc(s["dt_act"], 1)

            with act_e.Fori(0, GRP) as g:
                act_e.wait_ge(s["ssm_z"], g + 1)
                for b in range(2):
                    fn(zs[:, 2 * b:2 * b + 2, :], bank[b][:, :], ACT.Silu)
                for b in range(6):
                    if b in (0, 4):
                        act_e.wait_ge(s["ssm_x"], g * 2 + (1 if b == 0 else 2))
                    j = g + (16 if b == 4 else 20) if b >= 4 else g * 4 + b
                    fn(conv[:, b, :], bank[2 + b // 2][:, (b % 2) * T:(b % 2 + 1) * T], ACT.Identity,
                       scale=cols[:, ds(j + (VO["conv_w"] + 3 * 24), 1)], bias=cols[:, ds(j + VO["conv_b"], 1)]) \
                        .then_inc(s["ssm_acc"], 1)
                act_e.wait_ge(s["ssm_taps"], g + 1)
                fn(conv, conv, ACT.Silu).then_inc(s["ssm_conv"], 1)
                act_e.wait_ge(s["ssm_tok"], g + 1)
                fn(bcb, bank[4][:, 0:3 * P], ACT.Copy).then_inc(s["ssm_bcb"], 1)
                act_e.wait_ge(s["ssm_E"], g + 1)
                fn(e_bc, bank[7][:, :], ACT.Exp).then_inc(s["ssm_Ex"], 1)
                act_e.wait_ge(s["ssm_state"], g + 1)
                fn(state_t, bank[5][:, :], ACT.Copy).then_inc(s["ssm_stT"], 1)
                for u in range(4):
                    c, hh = u // 2, u % 2
                    act_e.wait_ge(s["ssm_seg"], g * 4 + (u + 1))
                    if u >= 2:
                        act_e.wait_ge(s["ssm_yd"], g * 4 + (u - 1))
                    for h in range(4):
                        last = fn(mexp[:, u % 2, h * P:(h + 1) * P], bank[u % 2][:, h * P:(h + 1) * P], ACT.Exp,
                                  bias=gsm[:, 2 + c, 4 * hh + h:4 * hh + h + 1])
                    last.then_inc(s["ssm_exp"], 1)
                act_e.wait_ge(s["ssm_y"], g + 1)
                fn(ysq, yssm, ACT.Square).then_inc(s["ssm_sq"], 1)
                act_e.wait_ge(s["ssm_ss"], g + 1)
                fn(rs_ssm, bank[7][:, 0:T], ACT.Sqrt, scale=1.0 / 512, bias=C("eps")).then_inc(s["ssm_std"], 1)
            end_phase()
            gated_out()
            end_phase()

            act_e.wait_ge(s["kv_mm"], 1)
            fn(k_raw[:, 0, :], bank[0][:, 0:T], ACT.Copy)
            fn(vc_raw, bank[0][:, T:T2], ACT.Copy)
            fn(k_raw[:, 1:3, :], bank[1][:, :], ACT.Copy).then_inc(s["kv_raw"], 1)
            act_e.wait_ge(s["kv_dup"], 1)
            for g in range(NKV):
                fn(kk[g], bank[g][:, :], ACT.Copy)
            act_e.wait_ge(s["hid_mm"], 1)
            fn(hid, bank[7][:, 0:8 * NCMP], ACT.Silu).then_inc(s["hid_silu"], 1)
            end_phase()

            def nsa_unit(t):
                return Unit(branches=2, w=P * (t % 2 + 1))

            with act_e.Fori(0, 4) as j:
                act_e.wait_ge(s["q_mm"], j + 1)
                fn(q_raw, bank[6][:, :], ACT.Copy).then_inc(s["q_raw"], 1)
                act_e.wait_ge(s["cs_max"], j + 1)
                fn(cs, cs, ACT.Exp).then_inc(s["cs_exp"], 1)

                def copy_cmp():
                    act_e.wait_ge(s["ct_mm"], j + 1)
                    fn(ct[0:NCMP, 0:512], bank[6][0:NCMP, :], ACT.Copy)
                    fn(ct[0:NCMP, 512:1024], bank[7][0:NCMP, :], ACT.Copy).then_inc(s["ct_ev"], 1)

                attention([nsa_unit(t) for t in range(8)], j * 8, {3: copy_cmp})
            n["att_S"] += 32
            end_phase()
            gated_out()
            end_phase()
            end_phase()
            norm(T, 24)
            end_phase()

            act_e.wait_ge(s["tok_mm"], 1)
            for t in range(TT):
                for x in range(2):
                    last = fn(h_tok[:, t, x * 512:(x + 1) * 512], bank[2 + 2 * t + x][:, :], ACT.Copy)
            last.then_inc(s["tok_ev"], 1)
            act_e.wait_ge(s["route_dve"], 1)
            fn(g4b, g4a, ACT.Exp).then_inc(s["route_act"], 1)
            act_e.wait_ge(s["route_dve"], 2)
            fn(e8b, e8a, ACT.Exp).then_inc(s["route_act"], 1)
            act_e.wait_ge(s["route_dve"], 4)
            rounds = act_e.value_load(rounds_i.bitcast(I32)[0:1, 0:1], min_val=1, max_val=4)
            with act_e.Fori(0, rounds) as r:
                with act_e.Fori(0, PAIRS // 2) as i:
                    for q in range(2):
                        p = (r * (PAIRS // 2) + i) * 2 + q
                        act_e.wait_ge(s["moe_X"], p + 3)
                        fn(x_t[:, 0:4, :], bank[4][:, :], ACT.Copy).then_inc(s["moe_Xev"], 1)
                        act_e.wait_ge(s["moe_ct"], p + 1)
                        act_e.wait_ge(s["moe_sc"], p + 1)
                        fn(c_t, bank[6][:, 0:T], ACT.Copy).then_inc(s["moe_ctev"], 1)
                        for e in range(2):
                            act_e.wait_ge(s["moe_h"], p * 2 + (e + 1))
                            fn(hsil[:, e, :], bank[6 + e][:, 0:P], ACT.Silu).then_inc(s["moe_silu"], 1)
                        act_e.wait_ge(s["moe_y"], p + 1)
                        fn(y_slot[:, 0:512], bank[4][:, :], ACT.Copy).then_inc(s["moe_yev"], 1)
            end_phase()
            end_phase()
            norm(T)
            end_phase()

            for l in range(2):
                act_e.wait_ge(s["ada_ready"], 2 + l)
                norm(T2, 0)
                end_phase()
                if l == 0:
                    with act_e.Fori(0, KVG) as g:
                        act_e.wait_ge(s["q_mm"], g + 5)
                        for b in range(3):
                            last = fn(gq_sq[:, b, :], bank[b][:, :], ACT.Square)
                        last.then_inc(s["q_sq"], 1)
                        fn(gv, bank[3][:, 0:4 * DH], ACT.Copy)
                        act_e.wait_ge(s["q_ss"], g + 1)
                        for b in range(2):
                            fn(gq_std[:, b, :], bank[5 + b][:, :], ACT.Sqrt, bias=C("eps64"))
                        fn(gq_std[:, 2, :], bank[7][:, :], ACT.Sqrt, scale=1.0 / DH, bias=C("eps")).then_inc(s["q_std"], 1)
                        attention([Unit(branches=1, w=512 if t < 2 else 256)
                                   for _ in range(4) for t in range(4)], g * 16 + n["att_S"], {})
                    n["att_S"] += 64
                    end_phase()
                else:
                    act_e.wait_ge(s["kv_mm"], 2)
                    for b in range(3):
                        fn(cq_sq[:, b, :], bank[1 + b][:, 0:T], ACT.Square)
                    for b in range(2):
                        fn(ckv_sq[:, b, :], bank[4 + b][:, :], ACT.Square)
                    fn(kr_raw[ND:QK, :], bank[6][ND:QK, :], ACT.Copy).then_inc(s["kv_raw"], 1)
                    act_e.wait_ge(s["kv_rot"], 2)
                    fn(rstd[:, 0:T], bank[0][:, 0:T], ACT.Sqrt, scale=1.0 / QL, bias=C("eps"))
                    fn(sq[:, 0, :], bank[7][:, :], ACT.Sqrt, scale=1.0 / KVL, bias=C("eps")).then_inc(s["kv_roped"], 1)
                    end_phase()
                    with act_e.Fori(0, 4) as i:
                        for q in range(2):
                            it = i * 2 + q
                            act_e.wait_ge(s["q_mm"], it + 9)
                            fn(mq_raw[0:QK], bank[6][0:QK, :], ACT.Copy)
                            for hh in range(2):
                                fn(kcat[hh][0:ND, :], bank[hh][0:ND, :], ACT.Copy)
                            fn(mv, bank[2][:, :], ACT.Copy).then_inc(s["q_raw"], 1)
                            attention([Unit(branches=1, w=512) for _ in range(4)], it * 4 + n["att_S"], {})
                    n["att_S"] += 32
                    end_phase()
                end_phase()
                w = T2 if l == 0 else T
                norm(w, 24)
                end_phase()
                cw, cb = VO["ffn_conv_w_2"] + l * 3 * 2 * FB, VO["ffn_conv_b_2"] + l * 2 * FB
                with act_e.Fori(0, FB // 2) as i:
                    for q in range(2):
                        j = i * 2 + q
                        act_e.wait_ge(s["ffn_ev"], j + (n["ffn_ev"] + 1))
                        for x in range(2):
                            act_e.wait_ge(s["ffn_mm"], j * 2 + (2 * n["ffn_ev"] + x + 1))
                            fn(ffn_acc[:, 2 * q + x, 0:w], bank[2 * q + x][:, 0:w], ACT.Identity,
                               scale=cols[:, ds(j + (cw + 2 * FB + x * FB), 1)], bias=cols[:, ds(j + (cb + x * FB), 1)]) \
                                .then_inc(s["ffn_acc"], 1)
                        act_e.wait_ge(s["ffn_taps"], j + (n["ffn_ev"] + 1))
                        g = ffn_acc[:, 2 * q + 1, 0:w]
                        fn(g, g, ACT.Silu).then_inc(s["ffn_silu"], 1)
                n["ffn_ev"] += FB
                end_phase()
                end_phase()
            norm(T)
            end_phase()

        @block.vector
        def _(ve):
            n = counts()
            norms = [0]
            ended = [0]
            V = nc.vector
            ve.sem_inc(s["out_ev"], 4)
            ve.sem_inc(s["gemm_ev"], 4)
            ve.sem_inc(s["ffn_ev"], 2)
            ve.sem_inc(s["att_ev"], 1)

            def end_phase():
                ve.drain().then_inc(phase, 1)
                ended[0] += 1
                ve.wait_ge(phase, 3 * ended[0])

            def adaln(ncol, bias, gains, rnd):
                ve.wait_ge(s["ada_mm"], rnd)
                V.tensor_tensor(ada[:, :, 0:ncol], bank[7][:, 0:96].rearrange("p (n c) -> p n c", c=2)[:, :, 0:ncol],
                                cols[:, bias:bias + 48].unsqueeze(2).to_broadcast([P, 48, ncol]), ALU.add)
                ve.drain()
                for which in range(2):
                    for part in range(ncol):
                        last = V.scalar_tensor_tensor(mod[:, which, part, :], ada[:, 8 + 24 * which:16 + 24 * which, part], 1.0,
                                                      cols[:, gains[which]:gains[which] + KD], ALU.add, ALU.mult)
                last.then_inc(s["ada_ready"], 1)
                ve.drain()

            def norm(w, gain, out, shifted):
                ve.wait_ge(s["std_ready"], norms[0] + 1)
                V.reciprocal(rstd[:, 0:w], rstd[:, 0:w])
                ve.drain()
                for k in range(KD):
                    for part in range(w // T):
                        a, b = part * T, (part + 1) * T
                        last = V.scalar_tensor_tensor(out[:, k, a:b], resid[:, k, a:b], gain(part)[:, k:k + 1],
                                                      rstd[:, a:b], ALU.mult, ALU.mult)
                    last.then_inc(s["hn_scaled"] if shifted else s["hn_ready"], 1)
                norms[0] += 1

            def gated_out(first):
                with ve.Fori(0, 2) as i:
                    for m in range(4):
                        ve.wait_ge(s["out_sig"], i * 4 + (n["out_mm"] + m + 1))
                        dst = merged[:, ds(i * 4 + m, 1), :].rearrange("p a t -> p (a t)")
                        if first:
                            V.tensor_tensor(dst, bank[m][:, 0:T], out_sig[:, m, :], ALU.mult).then_inc(s["out_ev"], 1)
                        else:
                            V.tensor_tensor(out_tmp[:, m % 2, :], bank[m][:, 0:T], out_sig[:, m, :], ALU.mult)
                            ve.drain()
                            V.tensor_tensor(dst, dst, out_tmp[:, m % 2, :], ALU.add).then_inc(s["out_ev"], 1)
                n["out_mm"] += 8

            def gemm(trips, per_trip, w, gate):
                with ve.Fori(0, trips) as i:
                    for m in range(per_trip):
                        ve.wait_ge(s["gemm_mm"], i * per_trip + (n["gemm_mm"] + m + 1))
                        for part in range(w // T):
                            a, b = part * T, (part + 1) * T
                            dst = resid[:, ds(i * per_trip + m, 1), a:b].rearrange("p a t -> p (a t)")
                            last = V.scalar_tensor_tensor(
                                dst, bank[m % 4][:, a:b],
                                ada[:, ds(i * per_trip + (gate + m), 1), part:part + 1].rearrange("p a t -> p (a t)"),
                                dst, ALU.mult, ALU.add)
                        last.then_inc(s["gemm_ev"], 1)
                n["gemm_mm"] += trips * per_trip

            def attention(units, done):
                U = len(units)
                for t in range(U + 1):
                    if t < U:
                        u = units[t]
                        ve.wait_ge(s["att_S"], done + (t + 1))
                        V.tensor_reduce(nmax[:, t % 3, 0:u.branches],
                                        bank[t % 3][:, 0:u.branches * u.w].rearrange("p (b k) -> p b k", b=u.branches),
                                        AX.X, ALU.max, negate=True).then_inc(s["att_max"], 1)
                    if t >= 1:
                        v = t - 1
                        u = units[v]
                        ve.wait_ge(s["att_exp"], done + (v + 4))
                        fac = pfac[:, v % 3, 0:u.branches]
                        V.reciprocal(fac, psum_[:, v % 3, 0:u.branches])
                        ve.drain()
                        if u.gate is not None:
                            V.tensor_tensor(fac, fac, u.gate, ALU.mult)
                            ve.drain()
                        for b in range(u.branches):
                            pb = probs[v % 3][:, b * u.w:(b + 1) * u.w]
                            last = V.tensor_scalar(pb, pb, fac[:, b:b + 1], None, ALU.mult)
                        last.then_inc(s["att_scaled"], 1)

            ve.wait_ge(setup_landed, 16 * SETUP_DMAS)
            V.tensor_copy(pos_f, pos_i.bitcast(I32))
            ve.drain()
            V.tensor_scalar(ang, pos_f, C("invf"), None, ALU.mult)
            ve.drain()
            for quarter, dst in ((0.25, tmp_rope), (0.0, ang)):
                V.tensor_scalar(turns, ang, 1.0 / (2 * math.pi), quarter, ALU.mult, ALU.add)
                ve.drain()
                V.tensor_scalar(turns, turns, 1.5 * 2 ** 23, None, ALU.add)
                ve.drain()
                V.tensor_scalar(turns, turns, -1.5 * 2 ** 23, None, ALU.add)
                ve.drain()
                src = ang
                for part in TWO_PI:
                    V.scalar_tensor_tensor(dst, turns, -part, src, ALU.mult, ALU.add)
                    ve.drain()
                    src = dst
                if quarter:
                    V.tensor_scalar(dst, dst, math.pi / 2, None, ALU.add)
                    ve.drain()
                V.tensor_scalar(dst, dst, PI_BELOW, -PI_BELOW, ALU.min, ALU.max)
                ve.drain()
            ve.drain().then_inc(s["rope_reduced"], 1)
            ve.wait_ge(s["csil_ready"], 1)
            adaln(1, VO["b_ada"], (VO["norm1_g"], VO["norm2_g"]), 1)
            norm(T, lambda part: mod[:, 0, part, :], hn, True)
            end_phase()

            ve.wait_ge(s["rope_sin"], 1)
            V.tensor_scalar(ncos8, ncos[:, :], DH ** -0.5, None, ALU.mult)
            V.tensor_scalar(nsin8, nsin[:, :], DH ** -0.5, None, ALU.mult)
            ve.wait_ge(s["gates_ready"], 1)
            bias = rows32[:, 0:HEADS].unsqueeze(1).to_broadcast([P, 2, HEADS])
            V.tensor_tensor(dt_in, bank[7][:, 0:160].rearrange("p (c n) -> p c n", c=2)[:, :, 0:HEADS], bias, ALU.add)
            ve.drain()
            V.tensor_scalar(dt_a, dt_in, -1.0, None, ALU.mult)
            ve.drain()
            V.tensor_tensor(dt_a, dt_a, dt_in, ALU.min).then_inc(s["dt_dve"], 1)
            ve.wait_ge(s["dt_act"], 1)
            V.tensor_scalar(dt_c, dt_b, 1.0, None, ALU.add)
            ve.drain().then_inc(s["dt_dve"], 1)
            V.tensor_scalar(dt_d, dt_c, -1.0, None, ALU.add)
            ve.drain()
            ve.wait_ge(s["dt_act"], 2)
            V.tensor_scalar(dt_c, dt_d, 0.0, None, ALU.is_equal)
            ve.drain()
            V.tensor_tensor(dt_a, dt_a, dt_c, ALU.add)
            V.tensor_tensor(dt_d, dt_d, dt_c, ALU.add)
            ve.drain()
            V.reciprocal(dt_d, dt_d)
            V.tensor_tensor(dt_a, dt_a, dt_b, ALU.mult)
            ve.drain()
            V.tensor_tensor(dt_a, dt_a, dt_d, ALU.mult)
            V.tensor_scalar(dt_b, dt_in, 0.0, None, ALU.max)
            ve.drain()
            dt = ssm_small[:, 4:6, :]
            V.tensor_tensor(dt, dt_a, dt_b, ALU.add)
            ve.drain()
            V.tensor_tensor(ssm_small[:, 0:2, :], dt, a_neg.unsqueeze(1).to_broadcast([P, 2, HEADS]), ALU.mult)
            ve.drain()
            V.tensor_scalar(ssm_small[:, 0:2, :], ssm_small[:, 0:2, :], -1.0, None, ALU.mult)
            ve.drain().then_inc(s["dt_dve"], 1)
            ve.wait_ge(s["dt_pe"], 2)
            cum = bank[6][:, 0:2 * HEADS].rearrange("p (c n) -> p c n", c=2)
            V.tensor_scalar(ssm_small[:, 2:4, :], cum, -1.0, None, ALU.mult)
            ve.drain()
            V.tensor_tensor(ssm_small[:, 7, :], ssm_small[:, 2, :], bank[6][:, 2 * HEADS:3 * HEADS], ALU.add)
            ve.drain().then_inc(s["dt_dve"], 1)
            ve.wait_ge(s["dt_act"], 3)
            ve.drain().then_inc(s["group_done"], 1)

            with ve.Fori(0, GRP) as g:
                V.tensor_copy(gsm, ssm_small[:, :, ds(g * HPG, HPG)])
                ve.drain()
                V.tensor_copy(dt_wide.rearrange("p (h d) -> p h d", h=HPG), gsm[:, 1, :].unsqueeze(2).to_broadcast([P, HPG, HD])) \
                    .then_inc(s["gsm_ready"], 1)
                for back in range(1, CONV):
                    for b in range(6):
                        if back == 1 and b % 2 == 0:
                            ve.wait_ge(s["ssm_acc"], g * 6 + (b + 2))
                        j = g + (16 if b == 4 else 20) if b >= 4 else g * 4 + b
                        u = bank[2 + b // 2][:, (b % 2) * T:(b % 2 + 1) * T]
                        V.scalar_tensor_tensor(conv[:, b, back:T], u[:, 0:T - back],
                                               cols[:, ds(j + (VO["conv_w"] + (CONV - 1 - back) * 24), 1)],
                                               conv[:, b, back:T], ALU.mult, ALU.add)
                    if back < CONV - 1:
                        ve.drain()
                ve.drain().then_inc(s["ssm_taps"], 1)
                ve.wait_ge(s["ssm_tok"], g + 1)
                for c in range(2):
                    V.tensor_tensor(xdt[:, c, :].rearrange("p (h d) -> p h d", h=HPG),
                                    bank[5 + c][:, :].rearrange("p (h d) -> p h d", h=HPG),
                                    gsm[:, 4 + c, :].unsqueeze(2).to_broadcast([P, HPG, HD]), ALU.mult)
                ve.drain()
                V.tensor_tensor(xw.rearrange("p (h d) -> p h d", h=HPG), xdt[:, 0, :].rearrange("p (h d) -> p h d", h=HPG),
                                gsm[:, 6, :].unsqueeze(2).to_broadcast([P, HPG, HD]), ALU.mult).then_inc(s["ssm_xw"], 1)
                ve.wait_ge(s["ssm_bcb"], g + 1)
                for u in range(4):
                    ve.wait_ge(s["ssm_exp"], g * 4 + (u + 1))
                    m = mexp[:, u % 2, :].rearrange("p (h t) -> p h t", h=4)
                    V.tensor_tensor(m, m, bcb[:, 1 + u // 2, :].unsqueeze(1).to_broadcast([P, 4, P]), ALU.mult) \
                        .then_inc(s["ssm_M"], 1)
                ve.wait_ge(s["ssm_yoff"], g + 1)
                ve.wait_ge(s["ssm_Ex"], g + 1)
                V.tensor_tensor(yoff, bank[6][:, :].rearrange("p (b t) -> p b t", b=4),
                                e_bc.rearrange("p (b t) -> p b t", b=4), ALU.mult)
                ve.wait_ge(s["ssm_yd"], g * 4 + 4)
                for b in range(4):
                    V.scalar_tensor_tensor(yssm[:, b, :], conv[:, b, :], cols[:, ds(g * 4 + (VO["d_skip"] + b), 1)],
                                           bank[2 + b // 2][:, (b % 2) * T:(b % 2 + 1) * T], ALU.mult, ALU.add)
                ve.drain()
                V.tensor_tensor(yssm[:, :, P:T], yssm[:, :, P:T], yoff, ALU.add)
                ve.drain()
                V.tensor_tensor(yssm, yssm, zs, ALU.mult).then_inc(s["ssm_y"], 1)
                ve.wait_ge(s["ssm_std"], g + 1)
                V.reciprocal(rs_ssm, rs_ssm)
                ve.drain()
                for b in range(4):
                    last = V.scalar_tensor_tensor(ynorm[:, ds(g * 4 + b, 1), :].rearrange("p a t -> p (a t)"), yssm[:, b, :],
                                                  cols[:, ds(g * 4 + (VO["ssm_norm_g"] + b), 1)], rs_ssm, ALU.mult, ALU.mult)
                last.then_inc(s["group_done"], 1)
            end_phase()
            gated_out(True)
            end_phase()

            ve.wait_ge(s["kv_mm"], 1)
            V.tensor_copy(v_tok.rearrange("p b t d -> p (b t d)"), bank[2][:, :])
            ve.wait_ge(s["kv_raw"], 1)

            def over(table, m):
                return table.unsqueeze(1).to_broadcast([P, m, T])

            V.tensor_tensor(k_roped, k_raw, over(ncos[:, :], 3), ALU.mult)
            ve.wait_ge(s["kv_rot"], 1)
            V.tensor_tensor(k_tmp[:, 0:2, :], bank[3][:, :].rearrange("p (a t) -> p a t", a=2), over(nsin[:, :], 2), ALU.mult)
            V.tensor_tensor(k_tmp[:, 2, :], bank[4][:, 0:T], nsin[:, :], ALU.mult)
            ve.drain()
            V.tensor_tensor(k_roped, k_roped, k_tmp, ALU.add).then_inc(s["kv_roped"], 1)
            ve.wait_ge(s["kv_dup"], 1)
            for x, name in enumerate(("cmp_pe_k", "cmp_pe_v")):
                pe_cols = cols[:, VO[name]:VO[name] + 16]
                for g in range(NKV):
                    src = bank[5 + x][:, g * T:(g + 1) * T].rearrange("p (c j) -> p j c", j=STRIDE)
                    for h in range(2):
                        rows = slice(64 * h, 64 * h + 64)
                        for late in range(2):
                            V.tensor_tensor(blk[x][rows, 8 * late:8 * late + 8, g * NCMP:(g + 1) * NCMP],
                                            src[rows, h:STRIDE:2, late:late + NCMP],
                                            pe_cols[rows, 8 * late:8 * late + 8].unsqueeze(2).to_broadcast([64, 8, NCMP]), ALU.add)
            ve.drain().then_inc(s["kv_ready"], 1)
            ve.wait_ge(s["cmp_mm"], 1)
            V.tensor_copy(k_cmp, bank[4][:, 256:256 + 2 * NCMP])
            V.tensor_copy(v_cmp[0:NCMP].rearrange("p g d -> p (g d)"), bank[4][0:NCMP, 320:320 + 2 * DH])
            ve.drain().then_inc(s["cmp_ready"], 1)
            end_phase()

            with ve.Fori(0, 4) as j:
                gv_ = gates.rearrange("p q (u j h b) -> p u j h q b", u=2, j=4, h=2, b=3)
                for b in range(3):
                    for u in range(2):
                        V.tensor_copy(gsel[:, b, 4 * u:4 * u + 4].rearrange("p (h q) -> p h q", h=2),
                                      gv_[:, u, ds(j, 1), :, :, b].rearrange("p a h q -> p (a h) q"))
                ve.wait_ge(s["q_raw"], j + 1)
                V.tensor_tensor(q_t, q_raw, over(ncos8, 2), ALU.mult)
                ve.wait_ge(s["q_rot"], j + 1)
                V.tensor_tensor(q_tmp, bank[7][:, :].rearrange("p (a t) -> p a t", a=2), over(nsin8, 2), ALU.mult)
                ve.drain()
                V.tensor_tensor(q_t, q_t, q_tmp, ALU.add).then_inc(s["q_roped"], 1)
                ve.wait_ge(s["cs_mm"], j + 1)
                for half in range(2):
                    V.tensor_tensor(cs[:, half:4:2, :], bank[7 - half][:, 0:4 * NCMP].rearrange("p (a c) -> p a c", a=2),
                                    C("cneg").unsqueeze(1).to_broadcast([P, 2, 2 * NCMP]), ALU.add)
                ve.drain()
                cs8 = cs.rearrange("p a (q c) -> p (a q) c", q=2)
                V.tensor_reduce(cs_m, cs8, AX.X, ALU.max)
                ve.drain()
                V.tensor_tensor(cs8, cs8, cs_m.unsqueeze(2).to_broadcast([P, 8, NCMP]), ALU.subtract).then_inc(s["cs_max"], 1)
                ve.wait_ge(s["cs_exp"], j + 1)
                V.tensor_tensor(cs, cs, C("c01").unsqueeze(1).to_broadcast([P, 4, 2 * NCMP]), ALU.mult)
                ve.drain()
                V.tensor_reduce(cs_s, cs8, AX.X, ALU.add)
                ve.drain()
                V.tensor_scalar(cs_s, cs_s, 1e-30, None, ALU.max)
                ve.drain()
                V.reciprocal(cs_s, cs_s)
                ve.drain()
                V.tensor_tensor(cs_s, cs_s, gsel[:, 0, :], ALU.mult)
                ve.drain()
                V.tensor_tensor(cs8, cs8, cs_s.unsqueeze(2).to_broadcast([P, 8, NCMP]), ALU.mult).then_inc(s["cs_ready"], 1)
                attention([Unit(branches=2, w=P * (t % 2 + 1), gate=gsel[:, 1:3, t]) for t in range(8)], j * 8)
                ve.wait_ge(s["att_O"], j * 8 + 10)
                for u in range(2):
                    last = V.tensor_copy(o_t[:, ds(j + 4 * u, 1), :].rearrange("p a t -> p (a t)"), bank[5][:, u * T:(u + 1) * T])
                last.then_inc(s["att_ev"], 1)
            n["att_S"] += 32
            end_phase()
            gated_out(False)
            end_phase()
            gemm(2, 4, T, 16)
            end_phase()
            norm(T, lambda part: mod[:, 1, part, :], hn, True)
            end_phase()

            V.memset(zeros, 0.0)
            ve.wait_ge(s["route_pe"], 1)

            def b2(x, m):
                return x.to_broadcast([P, 2, m])

            def first_max(x, rev, top, key, out, m):
                V.tensor_reduce(top, x, AX.X, ALU.max)
                ve.drain()
                V.tensor_tensor(key, x, b2(top, m), ALU.is_equal)
                ve.drain()
                V.tensor_tensor(key, key, rev.unsqueeze(1).to_broadcast([P, 2, m]), ALU.mult)
                ve.drain()
                V.tensor_reduce(t2f, key, AX.X, ALU.max)
                ve.drain()
                V.tensor_tensor(out, key, b2(t2f, m), ALU.is_equal)
                ve.drain()

            V.tensor_tensor(lg, bank[0][:, 0:72].rearrange("p (t n) -> p t n", t=2),
                            rows32[:, 3 * HEADS:].unsqueeze(1).to_broadcast([P, 2, 36]), ALU.add)
            ve.drain()
            gl, el = lg[:, :, 0:NG], lg[:, :, NG:NG + NE]
            first_max(gl, C("rev4"), t2a, g4b, g4c, NG)
            V.tensor_tensor(g4a, gl, b2(t2a, NG), ALU.subtract)
            ve.drain().then_inc(s["route_dve"], 1)
            for t in range(2):
                V.tensor_tensor(e32[:, t], el[:, t].rearrange("p (g e) -> p g e", g=NG),
                                g4c[:, t, :].unsqueeze(2).to_broadcast([P, NG, EPG]), ALU.mult)
            ve.drain()
            for t in range(2):
                V.tensor_reduce(e8c[:, t, :], e32[:, t].rearrange("p g e -> p e g"), AX.X, ALU.add)
            ve.drain()
            V.tensor_reduce(t2b, e8c, AX.X, ALU.max)
            ve.drain()
            V.tensor_tensor(e8a, e8c, b2(t2b, EPG), ALU.subtract)
            ve.drain().then_inc(s["route_dve"], 1)
            ve.wait_ge(s["route_act"], 1)
            V.tensor_reduce(t2a, g4b, AX.X, ALU.add)
            ve.drain()
            V.reciprocal(t2a, t2a)
            ve.wait_ge(s["route_act"], 2)
            V.tensor_reduce(t2b, e8b, AX.X, ALU.add)
            ve.drain()
            V.reciprocal(t2b, t2b)
            ve.drain()
            V.tensor_tensor(e8b, e8b, b2(t2b, EPG), ALU.mult)
            ve.drain()
            first_max(e8b, C("rev8"), t2b, e8c, e8d, EPG)
            V.scalar_tensor_tensor(e8b, e8d, -2.0, e8b, ALU.mult, ALU.add)
            ve.drain()
            first_max(e8b, C("rev8"), t2c, e8c, e8e, EPG)
            V.tensor_tensor(t2d, t2b, t2c, ALU.add)
            ve.drain()
            V.reciprocal(t2d, t2d)
            V.tensor_tensor(t2b, t2b, t2a, ALU.mult)
            V.tensor_tensor(t2c, t2c, t2a, ALU.mult)
            ve.drain()
            V.tensor_tensor(t2b, t2b, t2d, ALU.mult)
            V.tensor_tensor(t2c, t2c, t2d, ALU.mult)
            V.tensor_tensor(e8c, e8d, e8e, ALU.add)
            ve.drain()
            V.tensor_tensor(e8d, e8d, b2(t2b, EPG), ALU.mult)
            V.tensor_tensor(e8e, e8e, b2(t2c, EPG), ALU.mult)
            ve.drain()
            V.tensor_tensor(e8d, e8d, e8e, ALU.add)
            ve.drain()
            for t in range(2):
                og = g4c[:, t, :].unsqueeze(2).to_broadcast([P, NG, EPG])
                for dst, src in ((comb, e8d), (selm, e8c)):
                    V.tensor_tensor(dst[:, t, :].rearrange("p (g e) -> p g e", g=NG), og,
                                    src[:, t, :].unsqueeze(1).to_broadcast([P, NG, EPG]), ALU.mult)
            ve.drain().then_inc(s["route_dve"], 1)
            ve.wait_ge(s["route_pe"], 2)
            V.scalar_tensor_tensor(rank, bank[1][:, 0:2 * NE].rearrange("p (t e) -> p t e", t=2), 1.0, selm, ALU.add, ALU.mult)
            V.tensor_reduce(cmax, bank[1][:, 2 * NE:3 * NE], AX.X, ALU.max)
            ve.drain()
            V.tensor_scalar(rank, rank, -1.0, None, ALU.add)
            V.tensor_scalar(cflag, cmax, float(SLOTS), 1.0, ALU.is_gt, ALU.add)
            ve.drain()
            for full in range(2, T // SLOTS):
                V.scalar_tensor_tensor(cflag, cmax, float(full * SLOTS), cflag, ALU.is_gt, ALU.add)
                ve.drain()
            V.tensor_copy(rounds_i.bitcast(I32), cflag)
            ve.drain().then_inc(s["route_dve"], 1)
            rounds = ve.value_load(rounds_i.bitcast(I32)[0:1, 0:1], min_val=1, max_val=4)
            with ve.Fori(0, rounds) as r:
                with ve.Fori(0, PAIRS // 2) as i:
                    for q in range(2):
                        p = (r * (PAIRS // 2) + i) * 2 + q
                        ve.wait_ge(s["moe_X"], p + 1)
                        ve.wait_ge(s["moe_sc"], p + 1)
                        for t in range(TT):
                            for e in range(2):
                                ex = i * 4 + (2 * q + e)
                                o = slice(e * SLOTS, (e + 1) * SLOTS)
                                at_rank = rank[:, t, ds(ex, 1)]
                                V.tensor_scalar(sel[q][:, t, o], C("iota"), at_rank, None, ALU.is_equal)
                                V.tensor_scalar(wsel[q][:, t, o], C("iota"), at_rank, comb[:, t, ds(ex, 1)],
                                                ALU.is_equal, ALU.mult)
                        ve.drain().then_inc(s["moe_S"], 1)
                        ve.wait_ge(s["moe_X"], p + 3)
                        V.tensor_copy(x_t[:, 4:8, :].rearrange("p a b -> p (a b)"), bank[5][:, :]).then_inc(s["moe_Xev"], 1)
                        for e in range(2):
                            ve.wait_ge(s["moe_silu"], p * 2 + (e + 1))
                            V.tensor_tensor(he[:, e, :], hsil[:, e, :], bank[6 + e][:, P:2 * P], ALU.mult) \
                                .then_inc(s["moe_he"], 1)
                        ve.wait_ge(s["moe_y"], p + 1)
                        V.tensor_copy(y_slot[:, 512:1024], bank[5][:, :]).then_inc(s["moe_yev"], 1)
                ve.drain()
                V.tensor_scalar(rank, rank, -float(SLOTS), None, ALU.add)
                ve.drain()
            end_phase()
            for k in range(KD):
                V.scalar_tensor_tensor(resid[:, k, 0:T], bank[k // 2][:, (k % 2) * T:(k % 2 + 1) * T], ada[:, 40 + k, 0:1],
                                       resid[:, k, 0:T], ALU.mult, ALU.add)
            end_phase()
            norm(T, lambda part: cols[:, VO["final_g"]:VO["final_g"] + KD], resid, False)
            end_phase()

            for l in range(2):
                adaln(2, VO["ada_b_2"] + 48 * l, (VO["norm1_g_2"] + KD * l, VO["norm2_g_2"] + KD * l), 2 + l)
                norm(T2, lambda part: mod[:, 0, part, :], hn, True)
                end_phase()
                if l == 0:
                    with ve.Fori(0, KVG) as g:
                        ve.wait_ge(s["q_std"], g + 1)
                        V.reciprocal(gq_std.rearrange("p a t -> p (a t)"), gq_std.rearrange("p a t -> p (a t)"))
                        ve.drain()
                        for b in range(3):
                            gain = VO["gqa_q_norm_g_2"] if b < 2 else VO["gqa_k_norm_g_2"]
                            V.scalar_tensor_tensor(gq_n[:, b, :], bank[b][:, :], cols[:, gain:gain + 1], gq_std[:, b, :],
                                                   ALU.mult, ALU.mult)
                        ve.drain().then_inc(s["q_normed"], 1)
                        ve.wait_ge(s["q_rot"], g + 5)
                        V.tensor_tensor(gq_sq[:, :, 0:T], gq_n[:, :, 0:T], over(C("gcos"), 3), ALU.mult)
                        for b in range(3):
                            V.tensor_tensor(gq_std[:, b, 0:T], bank[5 + b][:, 0:T], C("gsin"), ALU.mult)
                        ve.drain()
                        V.tensor_tensor(gq_n[:, :, 0:T], gq_sq[:, :, 0:T], gq_std[:, :, 0:T], ALU.add).then_inc(s["q_roped"], 1)
                        attention([Unit(branches=1, w=512 if t < 2 else 256, gate=None)
                                   for _ in range(4) for t in range(4)], g * 16 + n["att_S"])
                        ve.wait_ge(s["att_O"], g * 16 + (n["att_S"] + 18))
                        for b in range(2):
                            last = V.tensor_copy(o2[:, ds(g * 2 + b, 1), :].rearrange("p a t -> p (a t)"), bank[5 + b][:, :])
                        last.then_inc(s["att_ev"], 1)
                    n["att_S"] += 64
                    end_phase()
                    gemm(2, 4, T2, 16)
                else:
                    V.tensor_scalar(qcos[0:QK], C("mcos", QK), QK ** -0.5, None, ALU.mult)
                    V.tensor_scalar(qsin[0:QK], C("msin", QK), QK ** -0.5, None, ALU.mult)
                    ve.wait_ge(s["kv_roped"], 2)
                    V.reciprocal(rstd[:, 0:T], rstd[:, 0:T])
                    V.reciprocal(sq[:, 0, :], sq[:, 0, :])
                    ve.drain()
                    for b in range(3):
                        V.scalar_tensor_tensor(cqn[:, b, :], bank[1 + b][:, 0:T], col("mla_q_norm_g_2", b), rstd[:, 0:T],
                                               ALU.mult, ALU.mult)
                    for b in range(2):
                        V.scalar_tensor_tensor(ckvn[:, b, :], bank[4 + b][:, :], col("mla_kv_norm_g_2", b), sq[:, 0, :],
                                               ALU.mult, ALU.mult)
                    ve.drain().then_inc(s["kv_ready"], 1)
                    r = slice(ND, QK)
                    ve.wait_ge(s["kv_dup"], 2)
                    V.tensor_tensor(kr_roped[r, 0:T], kr_raw[r, 0:T], consts[r, CO["mcos"][0]:CO["mcos"][0] + T], ALU.mult)
                    V.tensor_tensor(kr_roped[r, T:T2], bank[6][r, 0:T], consts[r, CO["msin"][0]:CO["msin"][0] + T], ALU.mult)
                    ve.drain()
                    for hh in range(2):
                        V.tensor_tensor(kcat[hh][r, 0:T], kr_roped[r, 0:T], kr_roped[r, T:T2], ALU.add)
                        V.tensor_copy(kcat[hh][r, T:T2], kr_raw[r, T:T2])
                    ve.drain().then_inc(s["cmp_ready"], 1)
                    end_phase()
                    with ve.Fori(0, 4) as i:
                        for q in range(2):
                            it = i * 2 + q
                            ve.wait_ge(s["q_rot"], it + 9)
                            V.tensor_tensor(mq_t[0:QK], mq_raw[0:QK], qcos[0:QK].unsqueeze(1).to_broadcast([QK, 2, T]), ALU.mult)
                            V.tensor_tensor(mq_tmp[0:QK], bank[7][0:QK, :].rearrange("p (a t) -> p a t", a=2),
                                            qsin[0:QK].unsqueeze(1).to_broadcast([QK, 2, T]), ALU.mult)
                            ve.drain()
                            V.tensor_tensor(mq_t[0:QK], mq_t[0:QK], mq_tmp[0:QK], ALU.add).then_inc(s["q_roped"], 1)
                            attention([Unit(branches=1, w=512, gate=None) for _ in range(4)], it * 4 + n["att_S"])
                            ve.wait_ge(s["att_O"], it * 4 + (n["att_S"] + 6))
                            V.tensor_copy(o2[:, ds(it, 1), 0:T].rearrange("p a t -> p (a t)"), bank[5][:, 0:T]).then_inc(s["att_ev"], 1)
                    n["att_S"] += 32
                    end_phase()
                    gemm(2, 4, T, 16)
                end_phase()
                w = T2 if l == 0 else T
                norm(w, lambda part: mod[:, 1, part, :], hn, True)
                end_phase()
                cw = VO["ffn_conv_w_2"] + l * 3 * 2 * FB
                with ve.Fori(0, FB // 2) as i:
                    for q in range(2):
                        j = i * 2 + q
                        for tap in (0, 2):
                            for x in range(2):
                                if tap == 0:
                                    ve.wait_ge(s["ffn_acc"], j * 2 + (2 * n["ffn_ev"] + x + 1))
                                u = bank[2 * q + x][:, 0:w].rearrange("p (a t) -> p a t", t=T)
                                a = ffn_acc[:, 2 * q + x, 0:w].rearrange("p (a t) -> p a t", t=T)
                                uu, aa = (u[:, :, 0:T - 1], a[:, :, 1:T]) if tap == 0 else (u[:, :, 1:T], a[:, :, 0:T - 1])
                                V.scalar_tensor_tensor(aa, uu, cols[:, ds(j + (cw + tap * 2 * FB + x * FB), 1)], aa,
                                                       ALU.mult, ALU.add)
                            ve.drain() if tap == 0 else ve.drain().then_inc(s["ffn_taps"], 1)
                        ve.wait_ge(s["ffn_silu"], j + (n["ffn_ev"] + 1))
                        V.tensor_tensor(act[:, ds(j, 1), 0:w].rearrange("p a t -> p (a t)"), ffn_acc[:, 2 * q, 0:w],
                                        ffn_acc[:, 2 * q + 1, 0:w], ALU.mult).then_inc(s["ffn_ev"], 1)
                n["ffn_ev"] += FB
                end_phase()
                gemm(2, 4, w, 40)
                end_phase()
            norm(T, lambda part: cols[:, VO["final_norm_g_2"]:VO["final_norm_g_2"] + KD], resid, False)
            end_phase()


def kernel(**inputs):
    import concourse.bacc as bacc
    from concourse.bass_utils import run_bass_kernel_spmd as run

    x = {k: np.asarray(v) for k, v in inputs.items()}

    def rows(a):
        return np.broadcast_to(a, (P,) + a.shape)

    w_in, up, down, ada2 = x["w_in"][0], x["ffn_w_up_2"], x["ffn_w_down_2"], x["ada_w_2"]
    vec = dict(x)
    vec["d_skip"] = np.repeat(x["d_skip"], HD)
    for name in ("gqa_q_norm_g_2", "gqa_k_norm_g_2"):
        vec[name] = np.tile(x[name], 2)

    def span(o, i, w):
        return o + i * w, o + (i + 1) * w

    n256 = [span(0, i, 256) for i in range(4)]
    g_in, u_q, u_kv = x["gqa_w_in_2"][0], x["mla_w_uq_2"][0], x["mla_w_ukv_2"][0]
    wg, wu, wd = x["w_exp_gate"][0], x["w_exp_up"][0], x["w_exp_down"][0]
    o_b, o_c = O_XBC + DIN, O_XBC + DIN + GRP * ST
    mla_in = x["mla_w_in_2"][0]
    wide = np.zeros((P, 3072 - 2304), np.float32)
    chunks = {
        "ada": [pack(x["w_ada"][0], span(0, i, 512)) for i in range(12)],
        "z": [pack(w_in, span(O_Z, g, 512)) for g in range(4)],
        "x": [pack(w_in, span(O_XBC, g, 512)) for g in range(4)],
        "bc": [pack(w_in, span(o_b, g, P), span(o_c, g, P)) for g in range(4)],
        "wso": [pack(x["w_ssm_out"][0], c) for c in n256],
        "gs": [pack(w_in, span(O_GS, i, 256)) for i in range(4)],
        "kv": [pack(w_in, span(O_KC, i, 384)) for i in range(2)],
        "cw1": [pack(x["cmp_w1_k"][0]), pack(x["cmp_w1_v"][0])],
        "q": [pack(w_in, span(O_Q, j, P), span(O_Q, 4 + j, P)) for j in range(4)],
        "nga": [np.concatenate([pack(x["w_nsa_out"][0], c), pack(w_in, span(O_GA, i, 256))], axis=1)
                for i, c in enumerate(n256)],
        "wo": [pack(x["w_o"][0], c) for c in n256],
        "egu": [pack(np.concatenate([wg[e], wu[e]], axis=1)) for e in range(NE)],
        "edn": [np.concatenate([pack(wd[2 * p]), pack(wd[2 * p + 1])], axis=1) for p in range(PAIRS)],
        "ada2": [pack(ada2[i // 12], span(0, i % 12, 512)) for i in range(24)],
        "gqa": [pack(g_in, span(0, g, 256), span(1024, g, 64), span(1024, g, 64), span(1280, g, 64)) for g in range(4)],
        "gqao": [pack(x["gqa_w_out_2"][0], c) for c in n256],
        "up": [pack(up[i // FB], span(0, i % FB, P), span(FFN, i % FB, P)) for i in range(2 * FB)],
        "down": [pack(down[i // 8], span(0, i % 8, P)) for i in range(16)],
        "mla": [pack(mla_in, (0, 384)), np.concatenate([pack(mla_in, (384, 672)), wide], axis=1)],
        "mlah": [np.concatenate([pack(u_q, span(0, j, 192)), pack(u_kv, span(0, j, 256))], axis=1) for j in range(8)],
        "mlao": [pack(x["mla_w_out_2"][0], c) for c in n256],
    }
    arrays = {name: np.concatenate(c, axis=0) for name, c in chunks.items()}
    for name, (m, w) in STREAMS.items():
        assert arrays[name].shape == (m * P, w), (name, arrays[name].shape)
    arrays["consts"] = constants()
    arrays["vecs"] = np.concatenate([np.reshape(vec[name], (-1, P)) for name, _ in VECS], axis=0)
    arrays["xt"] = pack(x["x"][0].T)
    arrays["ctxt"] = pack(x["ctx_2"][0].T)
    arrays["positions"] = rows(x["positions"][0])
    arrays["ssm_rows"] = rows(np.concatenate([x["dt_bias"][0], x["a_log"][0]]))
    arrays["route_rows"] = rows(np.concatenate([x["b_router_group"][0], x["b_router_expert"][0]]))
    arrays["w_small"] = pack(w_in, (O_DT, O_DT + HEADS), (O_GN, O_GN + 3 * NH))
    arrays["w_route"] = pack(np.concatenate([x["w_router_group"][0], x["w_router_expert"][0]], axis=1))
    arrays["w_cmp2"] = pack(np.concatenate([x["cmp_w2_k"][0], x["cmp_w2_k"][0], x["cmp_w2_v"][0]], axis=1))

    nc = bacc.Bacc("TRN2", target_bir_lowering=False, num_devices=1)
    sent, dr = {}, {}
    for name, a in arrays.items():
        sent[f"in_{name}"] = np.ascontiguousarray(a)
        dr[name] = nc.dram_tensor(f"in_{name}", a.shape, mybir.dt.from_np(a.dtype), kind="ExternalInput").ap()
    dr["out"] = nc.dram_tensor("out", (P, KD * T), F32, kind="ExternalOutput").ap()
    build(nc, dr)
    got = run(nc, [sent], core_ids=[0]).results[0]["out"]
    return np.ascontiguousarray(got.reshape(P, KD, T).transpose(2, 1, 0).reshape(1, T, D))
```

```python
import math
from contextlib import ExitStack


import numpy as np

import concourse.bass as bass
from concourse import mybir

F32 = mybir.dt.float32
I32 = mybir.dt.int32
ACT = mybir.ActivationFunctionType
ALU = mybir.AluOpType
AX = mybir.AxisListType
ds = bass.ds

P = 128
D = 1024
KD = D // P
T = 256
TT = T // P
T2 = 2 * T
EPS = 1e-6
NEG = -1e30

GRP, HPG, HD, ST, CONV = 4, 8, 64, 128, 4
HEADS = GRP * HPG
DIN = HEADS * HD
CONV_DIM = DIN + 2 * GRP * ST
NH, NKV, DH = 16, 2, 64
CMP, STRIDE, HID = 32, 16, 256
NCMP = (T - CMP) // STRIDE + 1
NG, EPG, FH = 4, 8, 256
NE = NG * EPG
TOPK = 2
NPOS = TOPK * T
PT = NPOS // P
ITEMS = -(-(NE + PT - 1) // 4) * 4
KVG = 4
QL, KVL, RD, ND = 384, 256, 32, 64
QK = ND + RD
FFN = 2816
FB = FFN // P

_sizes = (DIN, CONV_DIM, HEADS, NH * DH) + (NKV * DH,) * 6 + (3 * NH, D, D)
O_Z, O_XBC, O_DT, O_Q, O_KC, O_VC, O_KS, O_VS, O_KW, O_VW, O_GN, O_GS, O_GA = (
    sum(_sizes[:i]) for i in range(len(_sizes)))

SLOTW = 4096
NSLOT = 6

CONSTS = [("ident", P), ("ones", P), ("tri", P), ("trix", P), ("mneg", P), ("halves", P), ("pnsa", P),
          ("pgqa", P), ("dup0", P), ("dup1", P), ("pmla", QK), ("invf", 1), ("eps", 1), ("eps64", 1),
          ("gcos", T), ("gsin", T), ("mcos", T), ("msin", T), ("cneg", 2 * NCMP), ("c01", 2 * NCMP),
          ("rev4", NG), ("rev8", EPG), ("place", PT), ("tile_end", PT - 1), ("tile", PT - 1), ("code", PT), ("fold", 2)]
CO, _o = {}, 0
for _n, _w in CONSTS:
    CO[_n] = (_o, _w)
    _o += _w
CW = _o

VECS = [("c", 8), ("b_ada", 48), ("norm1_g", 8), ("conv_b", 24), ("norm2_g", 8), ("final_g", 8),
        ("ssm_norm_g", 16), ("conv_w", 96), ("d_skip", 16), ("cmp_pe_k", 16), ("cmp_pe_v", 16),
        ("c_2", 8), ("c_ctx_2", 8), ("ada_b_2", 96), ("norm1_g_2", 16), ("norm2_g_2", 16),
        ("ffn_conv_b_2", 88), ("final_norm_g_2", 8), ("ffn_conv_w_2", 264), ("mla_q_norm_g_2", 3),
        ("mla_kv_norm_g_2", 2), ("gqa_q_norm_g_2", 1), ("gqa_k_norm_g_2", 1)]
VO, _o = {}, 0
for _n, _r in VECS:
    VO[_n] = _o
    _o += _r
VR = _o
VT = -(-VR // P)

STREAMS = {
    "ada": (12, 4096), "z": (4, 4096), "x": (4, 4096), "bc": (4, 2048), "wso": (4, 4096), "gs": (4, 2048),
    "kv": (2, 3072), "cw1": (2, 4096), "q": (4, 2048), "nga": (4, 4096), "wo": (4, 2048),
    "egu": (NE, 4096), "edn": (NE, 2048),
    "ada2": (24, 4096), "gqa": (4, 3584), "gqao": (4, 2048), "up": (2 * FB, 2048), "down": (16, FB * P),
    "mla": (2, 3072), "mlah": (8, 1088), "mlao": (4, 2048),
}


TWO_PI = (6.28125, 0.0019350051879882812,
          2 * math.pi - 6.28125 - 0.0019350051879882812)
PI_BELOW = 3.1415925
MOE_PHASE, LAST_PHASE = 9, 25
SETUP_DMAS = 1 + VT + 8


class Unit:

    def __init__(self, scores=None, values=None, before=None, tiles=(), branches=1, w=0, gate=None):
        self.scores, self.values, self.before, self.tiles = scores, values, before, tiles
        self.branches, self.w, self.gate = branches, w, gate


def pack(w, *cols):
    w = np.concatenate([w[:, a:b] for a, b in cols], axis=1) if cols else w
    k, n = w.shape
    return w.reshape(k // P, P, n).transpose(1, 0, 2).reshape(P, -1)


def constants():
    c = np.zeros((P, CW), np.float32)

    def put(name, a):
        o, w = CO[name]
        c[:a.shape[0], o:o + w] = a

    i, j = np.arange(P)[:, None], np.arange(P)[None, :]
    put("ident", i == j)
    put("ones", np.ones((P, P)))
    put("tri", i <= j)
    put("trix", i < j)
    put("mneg", np.where(i <= j, 0.0, NEG))
    put("halves", i // 64 == j // 64)

    def rot(n, quarter):
        m = np.zeros((n, n))
        for o in range(n):
            b = o // quarter
            src, sign = (o + quarter, -1.0) if b % 2 == 0 else (o - quarter, 1.0)
            m[src, o] = sign
        return m

    put("pnsa", rot(P, 32))
    put("pgqa", rot(P, 16))
    m = np.zeros((QK, QK))
    m[ND:, ND:] = rot(RD, RD // 4)
    put("pmla", m)
    put("dup0", i == j % 64)
    put("dup1", i == 64 + j % 64)
    f = np.float32(10000.0) ** (-np.arange(0, DH, 2, dtype=np.float32) / np.float32(DH))
    put("invf", f[np.arange(P) % 32][:, None])
    put("eps", np.full((P, 1), EPS))
    put("eps64", np.full((P, 1), 64 * EPS))

    def axial(dim):
        t = np.arange(T)
        half = dim // 2
        inv = np.float32(10000.0) ** (-np.arange(0, half, 2, dtype=np.float32) / np.float32(half))
        ar = (t // 64).astype(np.float32)[:, None] * inv
        ac = (t % 64).astype(np.float32)[:, None] * inv
        a = np.concatenate([ar, ar, ac, ac], axis=1).T
        return np.cos(a), np.sin(a)

    gc, gs = axial(64)
    put("gcos", np.concatenate([gc, gc]))
    put("gsin", np.concatenate([gs, gs]))
    mc, ms = axial(RD)
    put("mcos", np.concatenate([np.ones((ND, T)), mc]))
    put("msin", np.concatenate([np.zeros((ND, T)), ms]))
    t = np.arange(P)[:, None, None] + P * np.arange(2)[None, :, None]
    ok = STRIDE * np.arange(NCMP)[None, None, :] + CMP - 1 <= t
    put("c01", ok.reshape(P, -1))
    put("cneg", np.where(ok, 0.0, NEG).reshape(P, -1))
    put("place", i + P * np.arange(PT)[None, :])
    put("tile_end", np.broadcast_to(P * np.arange(1, PT), (P, PT - 1)))
    put("tile", np.broadcast_to(np.arange(PT - 1), (P, PT - 1)))
    put("fold", i % 32 == np.arange(2)[None, :])
    put("code", np.broadcast_to(2 * NE * np.arange(PT) - 1, (P, PT)))
    put("rev4", np.broadcast_to(NG - np.arange(NG), (P, NG)))
    put("rev8", np.broadcast_to(EPG - np.arange(EPG), (P, EPG)))
    return c


def build(nc, dr):
    with ExitStack() as ctx:
        def sb(name, shape, dt=F32):
            return ctx.enter_context(nc.sbuf_tensor(name, shape, dt))

        def sem(name):
            return ctx.enter_context(nc.semaphore(name))

        bank = [ctx.enter_context(nc.psum_tensor(f"bank{i}", [P, 512], F32)) for i in range(8)]

        consts = sb("consts", [P, CW])
        cols = sb("cols", [P, VR])
        resid = sb("resid", [P, KD, T2])
        hn = sb("hn", [P, KD, T2])
        ring = sb("ring", [P, NSLOT * SLOTW])
        w_small = sb("w_small", [P, KD, HEADS + 3 * NH])
        w_route = sb("w_route", [P, KD, NG + NE])
        w_cmp2 = sb("w_cmp2", [P, 2, 192])
        rows32 = sb("rows32", [P, 3 * HEADS + NG + NE])
        ncos = sb("ncos", [P, T])
        nsin = sb("nsin", [P, T])
        ada = [sb(f"ada{i}", [P, 48, 2]) for i in range(3)]
        mod = [sb(f"mod{i}", [P, 2, 2, KD]) for i in range(3)]
        csil = sb("csil", [P, 2, KD, 32])
        sq = sb("sq", [P, 2, 512])
        rstd = sb("rstd", [P, 512])
        arena = sb("arena", [P, 12288])

        def C(name, rows=P):
            o, w = CO[name]
            return consts[0:rows, o:o + w]

        def col(name, i=0):
            return cols[:, VO[name] + i:VO[name] + i + 1] if isinstance(i, int) else cols[:, ds(i + VO[name], 1)]

        def slot(s, w=SLOTW):
            return ring[:, s * SLOTW:s * SLOTW + w]

        def w_down(q):
            return ring[:, 2 * SLOTW + q * SLOTW // 2:2 * SLOTW + (q + 1) * SLOTW // 2]

        class Place:

            def __init__(self, buf, at=0):
                self.buf, self.at = buf, at

            def __call__(self, *shape):
                n = int(np.prod(shape))
                ap = self.buf[:, self.at:self.at + n]
                self.at += n
                assert self.at <= self.buf.shape[1]
                if len(shape) == 2:
                    ap = ap.rearrange("p (a b) -> p a b", a=shape[0])
                if len(shape) == 3:
                    ap = ap.rearrange("p (a b c) -> p a b c", a=shape[0], b=shape[1])
                return ap

        ident, ones = C("ident"), C("ones")

        setup_landed = sem("setup_landed")
        slot_landed = [sem(f"slot{i}_landed") for i in range(NSLOT)]
        slot_free = [sem(f"slot{i}_free") for i in range(NSLOT)]
        gu_landed = [sem(f"gate_up{i}_landed") for i in range(2)]
        dn_landed = [sem(f"down{i}_landed") for i in range(4)]
        phase = sem("phase_ended")
        names = """
            vec_turned vec_ready csil_zeroed csil_ready ada_mm ada_rows ada_cols ada_ready
            sq_ready sq_used ss_ready std_ready hn_scaled hn_ready rope_reduced rope_sin
            dt_pe dt_dve dt_act group_done gsm_ready
            ssm_z ssm_x ssm_acc ssm_taps ssm_conv ssm_tok ssm_bcb ssm_xw ssm_E ssm_Ex ssm_state ssm_stT ssm_seg
            ssm_exp ssm_M ssm_yd ssm_yoff ssm_yo ssm_y ssm_sq ssm_ss ssm_std
            out_mm out_sig out_ev gemm_mm gemm_ev
            kv_mm kv_raw kv_rot kv_roped kv_dup kv_ready gates_ready hid_mm hid_silu cmp_mm cmp_ready
            q_mm q_raw q_rot q_roped q_sq q_ss q_std q_normed
            cs_mm cs_max cs_exp cs_ready ct_mm ct_ev
            att_S att_max att_exp att_scaled att_T att_PT att_O att_ev
            route_pe route_dve route_act tok_mm tok_ev
            moe_iota moe_zeroed moe_G moe_X moe_Xev moe_St moe_Stev moe_xt moe_h moe_silu moe_he moe_hT moe_hTev
            moe_y moe_yacc moe_sc
            ffn_mm ffn_acc ffn_taps ffn_silu ffn_ev stored""".split()
        s = {n: sem(n) for n in names}

        def counts():
            return dict.fromkeys(names, 0)

        spare = ring[:, 4 * SLOTW:6 * SLOTW]
        row_buf = spare[:, 2 * SLOTW - 3 * 512:].rearrange("p (a n) -> p a n", a=3)
        pl = Place(arena)
        vec_rows = pl(VT, P)
        pos_i, pos_f, ang, turns, tmp_rope = pl(T), pl(T), pl(T), pl(T), pl(T)
        pl = Place(arena)
        gates = pl(2, 3 * NH)
        ncos8, nsin8 = pl(T), pl(T)
        merged = pl(KD, T)
        after_merged = pl.at
        dt_in, dt_a, dt_b, dt_c, dt_d = (pl(2, HEADS) for _ in range(5))
        ssm_small = pl(4 * 2, HEADS)
        gsm = pl(4 * 2, HPG)
        a_neg = pl(HEADS)
        ynorm = pl(DIN // P, T)
        zs = pl(4, T)
        conv = pl(6, T)
        xdt = pl(2, 512)
        yssm = pl(4, T)
        pl = Place(spare)
        xw, bcb, state_t, e_bc, yoff = pl(512), pl(3 * P + 16), pl(512), pl(512), pl(4, P)
        b_tok, cb, ssm_ada = bcb[:, 0:P], bcb[:, P:3 * P].rearrange("p (c t) -> p c t", c=2), bcb[:, 3 * P:]
        mexp = pl(2, 512)
        ysq = pl(4 * T)
        rs_ssm = pl(T)
        dt_wide = pl(512)
        assert pl.at <= 2 * SLOTW - 3 * 512
        pl = Place(spare)
        out_sig = pl(4, T)
        out_tmp = pl(2, T)
        pl = Place(arena, after_merged)
        k_raw, k_roped, k_tmp = pl(3, T), pl(3, T), pl(3, T)
        vc_raw = pl(T)
        v_tok = pl(2, 2, P)
        kk = [pl(2, T) for _ in range(NKV)]
        blk = [pl(16, 2 * NCMP) for _ in range(2)]
        hid = pl(4, 2 * NCMP)
        k_cmp = pl(2 * NCMP)
        v_cmp = pl(2, DH)
        o_t = pl(KD, T)
        gsel = pl(3, 8)
        cs, cs_m, cs_s = pl(4, 2 * NCMP), pl(8), pl(8)
        ct = pl(8 * P)
        pl = Place(spare)
        q_raw, q_t, q_tmp = pl(2, T), pl(2, T), pl(2, T)
        probs = [pl(512) for _ in range(3)]
        probs_t = [pl(512) for _ in range(2)]
        nmax, psum_, pfac = pl(3, 2), pl(3, 2), pl(3, 2)
        pl = Place(arena)
        h_tok = pl(2, D)
        xs = pl(KD, NPOS)
        ys = pl(PT, D)
        x_t = [pl(KD, P) for _ in range(2)]
        pl = Place(spare)
        iota = pl(NPOS)
        lg = pl(2, NG + NE)
        t2a, t2b, t2c, t2d, t2f, pos_a, pos_b = (pl(2, 1) for _ in range(7))
        g4a, g4b, g4c = (pl(2, NG) for _ in range(3))
        e8a, e8b, e8c, e8d, e8e = (pl(2, EPG) for _ in range(5))
        e32 = pl(2, NG, EPG)
        sel_a, sel_b, selm, pos = (pl(2, NE) for _ in range(4))
        cnt_col = pl(1)
        start = pl(NE)
        at_end, ends = pl(PT - 1, NE), pl(PT - 1)
        before_place, code_place = pl(PT, NE), pl(PT)
        tile_f3, tile_f, expert_f, code_item, mask = pl(PT - 1, ITEMS), pl(ITEMS), pl(ITEMS), pl(ITEMS), pl(ITEMS)
        tile_i, expert_i = pl(ITEMS), pl(ITEMS)
        pick, wpick, wpick_b = pl(2, NPOS), pl(2, NPOS), pl(NPOS)
        s_t = pl(PT, T)
        hsil, he, he_t = pl(2, FH), pl(2, FH), pl(2, FH)
        assert pl.at <= 2 * SLOTW
        pl = Place(arena)
        o2 = pl(KD, T2)
        gq_sq = pl(3, 512)
        gq_std = pl(3, 512)
        gq_n = pl(3, 512)
        gk = pl(512)
        gv = pl(4, DH)
        pl = Place(arena, KD * T2)
        cqn = pl(3, T)
        ckvn = pl(2, T2)
        kr_raw, kr_roped = pl(512), pl(512)
        kcat = [pl(512) for _ in range(2)]
        mv = pl(4, P)
        qcos, qsin = pl(T), pl(T)
        mq_raw, mq_t, mq_tmp = pl(2, T), pl(2, T), pl(2, T)
        cq_sq, ckv_sq = pl(3, T), pl(2, T2)
        act = Place(arena)(FB, T2)
        ffn_acc = Place(spare)(4, T2)

        def since(i, first):
            return not isinstance(i, int) or i >= first

        def upto(i, end):
            return not isinstance(i, int) or i < end

        block = ctx.enter_context(nc.Block())

        @block.sync
        def _(sp):
            used = [0] * NSLOT

            def stream(trips, plan):
                per = {sl: sum(e[1] == sl for e in plan) for _, sl, _ in plan}

                def body(i):
                    for x, (name, sl, chunk) in enumerate(plan):
                        before = sum(e[1] == sl for e in plan[:x])
                        sp.wait_ge(slot_free[sl], i * per[sl] + (used[sl] + before + 1))
                        sp.dma_start(slot(sl, STREAMS[name][1]), dr[name][bass.ts(chunk(i), P), :]) \
                            .then_inc(slot_landed[sl], 16)
                if trips > 1:
                    with sp.Fori(0, trips) as i:
                        body(i)
                else:
                    body(0)
                for _, sl, _ in plan:
                    used[sl] += trips

            sp.dma_start(consts[:, :], dr["consts"]).then_inc(setup_landed, 16)
            for v in range(VT):
                r = min(P, VR - v * P)
                sp.dma_start(vec_rows[0:r, v, :], dr["vecs"][v * P:v * P + r, :]).then_inc(setup_landed, 16)
            sp.dma_start(resid[:, :, 0:T], dr["xt"].rearrange("p (k t) -> p k t", k=KD)).then_inc(setup_landed, 16)
            sp.dma_start(resid[:, :, T:T2], dr["ctxt"].rearrange("p (k t) -> p k t", k=KD)).then_inc(setup_landed, 16)
            sp.dma_start(pos_i.bitcast(I32), dr["positions"]).then_inc(setup_landed, 16)
            sp.dma_start(rows32[:, 0:2 * HEADS], dr["ssm_rows"]).then_inc(setup_landed, 16)
            sp.dma_start(rows32[:, 3 * HEADS:], dr["route_rows"]).then_inc(setup_landed, 16)
            sp.dma_start(w_small[:, :, :], dr["w_small"].rearrange("p (k n) -> p k n", k=KD)).then_inc(setup_landed, 16)
            sp.dma_start(w_route[:, :, :], dr["w_route"].rearrange("p (k n) -> p k n", k=KD)).then_inc(setup_landed, 16)
            sp.dma_start(w_cmp2[:, :, :], dr["w_cmp2"].rearrange("p (k n) -> p k n", k=2)).then_inc(setup_landed, 16)

            def c4(q):
                return lambda i: i * 4 + q

            def c2(q):
                return lambda i: i * 2 + q

            def c1(i):
                return i

            def at(n):
                return lambda i: n + i

            def ada2(first):
                return [("ada2", 1 + q, (lambda q: lambda i: i * 3 + (first + q))(q)) for q in range(3)]

            stream(1, [("ada", q, at(q)) for q in range(4)])
            stream(GRP, [("z", 0, c1), ("ada", 3, lambda i: i * 2 + 4), ("x", 1, c1), ("bc", 2, c1),
                         ("ada", 3, lambda i: i * 2 + 5)])
            stream(2, [("wso", 0, c2(0)), ("gs", 1, c2(0)), ("wso", 2, c2(1)), ("gs", 3, c2(1))])
            stream(1, [("kv", 0, at(0)), ("kv", 1, at(1)), ("cw1", 2, at(0)), ("cw1", 3, at(1))])
            stream(4, [("q", 0, c1)] + ada2(0))
            stream(2, [("nga", 1, c2(0)), ("nga", 2, c2(1))])
            stream(2, [("wo", 3, c2(0)), ("wo", 0, c2(1))])

            for sl in range(4):
                sp.wait_ge(slot_free[sl], used[sl] + 1)
            sp.wait_ge(phase, 3 * (MOE_PHASE - 1))
            sp.dma_start(iota, dr["iota"]).then_inc(s["moe_iota"], 16)
            sp.wait_ge(s["route_dve"], 5)

            def load_item(i, q, first):
                e = sp.value_load(expert_i.bitcast(I32)[0:1, ds(i, 1)], min_val=0, max_val=NE - 1)
                if not first or q >= 2:
                    sp.wait_ge(s["moe_h"], i - 1)
                sp.dma_start(slot(q % 2), dr["egu"][bass.ts(e, P), :]).then_inc(gu_landed[q % 2], 16)
                if not first:
                    sp.wait_ge(s["moe_y"], i - 3)
                sp.dma_start(w_down(q), dr["edn"][bass.ts(e, P), :]).then_inc(dn_landed[q], 16)

            for q in range(4):
                load_item(q, q, True)
            with sp.Fori(0, ITEMS // 4 - 1) as i:
                for q in range(4):
                    load_item(i * 4 + (q + 4), q, False)
            sp.wait_ge(phase, 3 * MOE_PHASE)

            for l in range(2):
                if l == 0:
                    stream(4, [("gqa", 0, c1)] + ada2(12))
                    stream(2, [("gqao", 1, c2(0)), ("gqao", 2, c2(1))])
                else:
                    stream(1, [("mla", 0, at(0)), ("mla", 1, at(1))])
                    stream(4, [("mlah", 2, c2(0)), ("mlah", 3, c2(1))])
                    stream(2, [("mlao", 0, c2(0)), ("mlao", 1, c2(1))])
                stream(FB // 2, [("up", 2, (lambda i: i * 2 + FB * l)), ("up", 3, (lambda i: i * 2 + 1 + FB * l))])
                stream(2, [("down", q, (lambda q: lambda i: i * 4 + q + 8 * l)(q)) for q in range(4)])

            sp.wait_ge(phase, 3 * LAST_PHASE)
            sp.dma_start(dr["out"].rearrange("p (k t) -> p k t", k=KD), resid[:, :, 0:T]).then_inc(s["stored"], 16)
            sp.wait_ge(s["stored"], 16)

        @block.tensor
        def _(pe):
            used = [0] * NSLOT
            n = counts()
            ended = [0]
            mm, tr = nc.tensor.matmul, nc.tensor.transpose
            for sl in range(NSLOT):
                pe.sem_inc(slot_free[sl], 1)
            pe.sem_inc(s["att_T"], 3)
            pe.sem_inc(s["att_O"], 2)

            def end_phase():
                pe.drain().then_inc(phase, 1)
                ended[0] += 1
                pe.wait_ge(phase, 3 * ended[0])

            def landed(sl, i=0):
                pe.wait_ge(slot_landed[sl], (i + used[sl] + 1) * 16)

            def free(*slots):
                for sl in slots:
                    pe.drain().then_inc(slot_free[sl], 1)

            def taken(trips, *slots):
                for sl in slots:
                    used[sl] += trips

            def dot(out, lhs, rhs, k):
                for i in range(k):
                    last = mm(out, lhs(i), rhs(i), start=i == 0, stop=i == k - 1)
                return last

            def ada_rows(b, sl, count, which):
                pe.wait_ge(slot_landed[sl], count * 16)
                for k in range(KD):
                    o = 32 * (k % 4)
                    last = mm(bank[b][o:o + 32, :], csil[:, which, k, :], slot(sl)[:, k * 512:(k + 1) * 512],
                              start=k < 4, stop=k >= 4)
                last.then_inc(s["ada_mm"], 1)
                free(sl)

            def ada_cols(out, c, buf, ncol):
                pe.wait_ge(s["ada_rows"], c + 1)
                for x in range(4):
                    last = mm(out[:, 2 * x:2 * x + ncol], row_buf[:, buf, x * P:(x + 1) * P], C("fold")[:, 0:ncol],
                              start=True, stop=True)
                last.then_inc(s["ada_cols"], 1)

            def norm(w):
                for k in range(KD):
                    pe.wait_ge(s["sq_ready"], n["sq_ready"] + k + 1)
                    last = mm(bank[0][:, 0:w], ones, sq[:, k % 2, 0:w], start=k == 0, stop=k == KD - 1)
                    if k < KD - 2:
                        last.then_inc(s["sq_used"], 1)
                last.then_inc(s["ss_ready"], 1)
                n["sq_ready"] += KD
                n["hn_ready"] += KD
                pe.wait_ge(s["hn_ready"], n["hn_ready"])

            def gemm(trips, slots, per, kb, rhs, w):
                q4 = len(slots) * per
                with pe.Fori(0, trips) as i:
                    for c, sl in enumerate(slots):
                        landed(sl, i)
                        for b in range(per):
                            m = c * per + b
                            pe.wait_ge(s["gemm_ev"], i * q4 + (n["gemm_mm"] + m + 1))
                            last = dot(bank[m % 4][:, 0:w],
                                       lambda k: slot(sl)[:, (k * per + b) * P:(k * per + b + 1) * P],
                                       lambda k: rhs(k), kb)
                            last.then_inc(s["gemm_mm"], 1)
                        free(sl)
                taken(trips, *slots)
                n["gemm_mm"] += trips * q4

            def gated_out(pairs, kb, rhs, gate_at):
                with pe.Fori(0, 2) as i:
                    for c, (sl, gsl) in enumerate(pairs):
                        landed(sl, i)
                        if gsl != sl:
                            landed(gsl, i)
                        for b in range(2):
                            m = c * 2 + b
                            pe.wait_ge(s["out_ev"], i * 4 + (n["out_mm"] + m + 1))
                            dot(bank[m][:, 0:T], lambda k: slot(sl)[:, (k * 2 + b) * P:(k * 2 + b + 1) * P], rhs, kb)
                            last = dot(bank[m][:, T:T2],
                                       lambda k: slot(gsl)[:, gate_at + (k * 2 + b) * P:gate_at + (k * 2 + b + 1) * P],
                                       lambda k: hn[:, k, 0:T], KD)
                            last.then_inc(s["out_mm"], 1)
                        free(*sorted({sl, gsl}))
                for sl, gsl in pairs:
                    taken(2, *{sl, gsl})
                n["out_mm"] += 8

            def attention(units, done):
                U = len(units)
                for t in range(U + 3):
                    if t < U:
                        pe.wait_ge(s["att_exp"], done + (t + 1))
                        units[t].scores(bank[t % 3]).then_inc(s["att_S"], 1)
                    if 0 <= t - 2 < U:
                        v = t - 2
                        pe.wait_ge(s["att_scaled"], done + (v + 1))
                        pe.wait_ge(s["att_PT"], done + (v + 1))
                        for x, c in enumerate(units[v].tiles):
                            last = tr(bank[3 + v % 2][:, x * P:(x + 1) * P], probs[v % 3][:, c:c + P], ident)
                        last.then_inc(s["att_T"], 1)
                    if 0 <= t - 3 < U:
                        v = t - 3
                        if units[v].before:
                            units[v].before()
                        pe.wait_ge(s["att_PT"], done + (v + 3))
                        units[v].values(probs_t[v % 2]).then_inc(s["att_O"], 1)

            pe.wait_ge(setup_landed, 16 * SETUP_DMAS)
            for v in range(VT):
                r = min(P, VR - v * P)
                last = tr(bank[v][:, 0:r], vec_rows[0:r, v, :], ident[0:r, 0:r])
            last.then_inc(s["vec_turned"], 1)
            pe.wait_ge(s["csil_ready"], 1)
            for q in range(4):
                ada_rows(q, q, 1, 0)
                if q >= 1:
                    ada_cols(bank[4][:, (q - 1) * 8:q * 8], q - 1, (q - 1) % 3, 1)
            ada_cols(bank[4][:, 24:32], 3, 0, 1)
            taken(1, 0, 1, 2, 3)
            norm(T)
            end_phase()

            for c in range(2):
                last = dot(bank[7][:, c * 80:(c + 1) * 80], lambda k: hn[:, k, c * P:(c + 1) * P],
                           lambda k: w_small[:, k, :], KD)
            last.then_inc(s["dt_pe"], 1)
            pe.wait_ge(s["dt_dve"], 3)
            for c in range(2):
                mm(bank[6][:, c * HEADS:(c + 1) * HEADS], C("tri"), ssm_small[:, c, :], start=True, stop=True)
            mm(bank[6][:, 2 * HEADS:3 * HEADS], ones, ssm_small[:, 0, :], start=True, stop=True).then_inc(s["dt_pe"], 1)

            xt = [conv[:, b, :] for b in range(4)]
            b_t, c_tt = conv[:, 4, :], conv[:, 5, :]
            dtag = [gsm[:, c, :] for c in range(2)]
            with pe.Fori(0, GRP) as g:
                pe.wait_ge(s["group_done"], g + 1)
                ada_rows(5, 3, g * 2 + (used[3] + 1), 0)
                landed(0, g)
                for b in range(4):
                    last = dot(bank[b // 2][:, (b % 2) * T:(b % 2 + 1) * T],
                               lambda k: slot(0)[:, k * 512 + b * P:k * 512 + b * P + P], lambda k: hn[:, k, 0:T], KD)
                last.then_inc(s["ssm_z"], 1)
                landed(1, g)
                for b in range(4):
                    last = dot(bank[2 + b // 2][:, (b % 2) * T:(b % 2 + 1) * T],
                               lambda k: slot(1)[:, k * 512 + b * P:k * 512 + b * P + P], lambda k: hn[:, k, 0:T], KD)
                last.then_inc(s["ssm_x"], 1)
                landed(2, g)
                for b in range(2):
                    last = dot(bank[4][:, b * T:(b + 1) * T],
                               lambda k: slot(2)[:, k * T + b * P:k * T + b * P + P], lambda k: hn[:, k, 0:T], KD)
                last.then_inc(s["ssm_x"], 1)
                free(0, 1, 2)
                ada_rows(6, 3, g * 2 + (used[3] + 2), 0)
                pe.wait_ge(s["ssm_conv"], g + 1)
                for x in range(2):
                    ada_cols(bank[4][:, 3 * P + 8 * x:3 * P + 8 * x + 8], g * 2 + (4 + x), x, 1)
                for c in range(2):
                    for b in range(4):
                        tr(bank[5 + c][:, b * P:(b + 1) * P], xt[b][:, c * P:(c + 1) * P], ident)
                tr(bank[4][:, 0:P], b_t[:, 0:P], ident)
                for c in range(2):
                    last = mm(bank[4][:, (1 + c) * P:(2 + c) * P], b_t[:, c * P:(c + 1) * P], c_tt[:, c * P:(c + 1) * P],
                              start=True, stop=True)
                last.then_inc(s["ssm_tok"], 1)
                pe.wait_ge(s["gsm_ready"], g + 1)
                for pr in range(4):
                    last = mm(bank[7][:, pr * P:(pr + 1) * P], dt_wide[:, pr * P:(pr + 1) * P], C("tri"),
                              start=True, stop=True)
                last.then_inc(s["ssm_E"], 1)
                pe.wait_ge(s["ssm_xw"], g + 1)
                pe.wait_ge(s["ssm_bcb"], g + 1)
                mm(bank[5][:, :], b_tok, xw, start=True, stop=True).then_inc(s["ssm_state"], 1)

                def within(u):
                    c, hh = u // 2, u % 2
                    pe.wait_ge(s["ssm_M"], g * 4 + (u + 1))
                    for h in range(4):
                        head = 4 * hh + h
                        o = (h // 2) * T + c * P
                        last = mm(bank[2 + hh][64 * (h % 2):64 * (h % 2) + 64, o:o + P],
                                  xdt[:, c, head * HD:(head + 1) * HD], mexp[:, u % 2, h * P:(h + 1) * P],
                                  start=True, stop=True)
                    last.then_inc(s["ssm_yd"], 1)

                for u in range(4):
                    c, hh = u // 2, u % 2
                    if u >= 2:
                        pe.wait_ge(s["ssm_exp"], g * 4 + (u - 1))
                    mm(bank[u % 2][:, :], ident, C("mneg").unsqueeze(1).to_broadcast([P, 4, P]), start=True, stop=False)
                    for h in range(4):
                        head = 4 * hh + h
                        last = mm(bank[u % 2][:, h * P:(h + 1) * P], dtag[c][:, head:head + 1].to_broadcast([P, P]),
                                  C("tri"), start=False, stop=h == 3)
                    last.then_inc(s["ssm_seg"], 1)
                    if u >= 1:
                        within(u - 1)
                pe.wait_ge(s["ssm_stT"], g + 1)
                for pr in range(4):
                    last = mm(bank[6][:, pr * P:(pr + 1) * P], state_t[:, pr * P:(pr + 1) * P], c_tt[:, P:T],
                              start=True, stop=True)
                last.then_inc(s["ssm_yoff"], 1)
                within(3)
                pe.wait_ge(s["ssm_sq"], g + 1)
                dot(bank[7][:, 0:T], lambda b: ones, lambda b: ysq[:, b * T:(b + 1) * T], 4).then_inc(s["ssm_ss"], 1)
            taken(GRP, 0, 1, 2)
            taken(2 * GRP, 3)
            pe.wait_ge(s["group_done"], GRP + 1)
            end_phase()
            gated_out([(0, 1), (2, 3)], DIN // P, lambda k: ynorm[:, k, :], 0)
            end_phase()

            def kvw(sl, x):
                return lambda k: slot(sl)[:, k * 384 + x * P:k * 384 + (x + 1) * P]

            def hx(k):
                return hn[:, k, 0:T]

            landed(0)
            dot(bank[0][:, 0:T], kvw(0, 0), hx, KD)
            dot(bank[0][:, T:T2], kvw(0, 1), hx, KD)
            dot(bank[1][:, 0:T], kvw(0, 2), hx, KD)
            landed(1)
            dot(bank[1][:, T:T2], kvw(1, 1), hx, KD)
            for br in range(2):
                for t in range(TT):
                    last = dot(bank[2][:, (br * 2 + t) * P:(br * 2 + t + 1) * P], lambda k: hn[:, k, t * P:(t + 1) * P],
                               kvw(1, 2 * br), KD)
            last.then_inc(s["kv_mm"], 1)
            free(0, 1)
            pe.wait_ge(s["kv_raw"], 1)
            mm(bank[3][:, :], C("pnsa"), k_raw[:, 0:2, :], start=True, stop=True)
            mm(bank[4][:, 0:T], C("pnsa"), k_raw[:, 2, :], start=True, stop=True).then_inc(s["kv_rot"], 1)
            pe.wait_ge(s["kv_roped"], 1)
            for g in range(NKV):
                dup = C(f"dup{g}")
                mm(bank[5][:, g * T:(g + 1) * T], dup, k_roped[:, 0, :], start=True, stop=True)
                mm(bank[6][:, g * T:(g + 1) * T], dup, vc_raw, start=True, stop=True)
                last = mm(bank[g][:, :], dup, k_roped[:, 1:3, :], start=True, stop=True)
            last.then_inc(s["kv_dup"], 1)
            pe.wait_ge(s["kv_ready"], 1)
            for x in range(2):
                landed(2 + x)
                for hb in range(2):
                    o = (x * 2 + hb) * 2 * NCMP
                    last = dot(bank[7][:, o:o + 2 * NCMP],
                               lambda k: slot(2 + x)[:, k * HID + hb * P:k * HID + hb * P + P],
                               lambda k: blk[x][:, k, :], 16)
            last.then_inc(s["hid_mm"], 1)
            free(2, 3)
            taken(1, 0, 1, 2, 3)
            pe.wait_ge(s["hid_silu"], 1)
            dot(bank[4][:, 256:256 + 2 * NCMP], lambda k: w_cmp2[:, k, 0:P], lambda k: hid[:, k, :], 2)
            for g in range(NKV):
                last = dot(bank[4][0:NCMP, 320 + g * DH:320 + (g + 1) * DH],
                           lambda k: hid[:, 2 + k, g * NCMP:(g + 1) * NCMP], lambda k: w_cmp2[:, k, P:P + DH], 2)
            last.then_inc(s["cmp_mm"], 1)
            pe.wait_ge(s["cmp_ready"], 1)
            end_phase()
            with pe.Fori(0, 4) as j:
                for x in range(3):
                    ada_rows(x, 1 + x, j + (used[1 + x] + 1), 1)
                landed(0, j)
                for u in range(2):
                    last = dot(bank[6][:, u * T:(u + 1) * T], lambda k: slot(0)[:, (2 * k + u) * P:(2 * k + u + 1) * P], hx, KD)
                last.then_inc(s["q_mm"], 1)
                free(0)
                for x in range(3):
                    ada_cols(bank[3][:, 8 * x:8 * x + 8], j * 3 + (12 + x), x, 2)
                pe.wait_ge(s["q_raw"], j + 1)
                mm(bank[7][:, :], C("pnsa"), q_raw, start=True, stop=True).then_inc(s["q_rot"], 1)
                pe.wait_ge(s["q_roped"], j + 1)

                def q_of(u, half, qt):
                    return q_t[64 * half:64 * half + 64, u, qt * P:(qt + 1) * P]

                order = [(u, half, qt) for u in range(2) for half in range(2) for qt in range(2)]
                for t, (u, half, qt) in enumerate(order):
                    last = mm(bank[7 - half][:, (2 * u + qt) * NCMP:(2 * u + qt + 1) * NCMP], q_of(u, half, qt),
                              k_cmp[64 * half:64 * half + 64, u * NCMP:(u + 1) * NCMP], start=True, stop=True)
                last.then_inc(s["cs_mm"], 1)

                def turn_cmp():
                    pe.wait_ge(s["cs_ready"], j + 1)
                    for t in range(8):
                        last = tr(bank[6 + t // 4][0:NCMP, (t % 4) * P:(t % 4 + 1) * P],
                                  cs[:, t // 2, (t % 2) * NCMP:(t % 2 + 1) * NCMP], ident)
                    last.then_inc(s["ct_mm"], 1)
                    pe.wait_ge(s["ct_ev"], j + 1)
                    pe.wait_ge(s["att_ev"], j + 1)

                def unit(t):
                    u, half, qt = order[t]
                    w = P * (qt + 1)

                    def scores(b):
                        kh = kk[u][64 * half:64 * half + 64, :, 0:w]
                        mm(b[:, 0:2 * w], q_of(u, half, qt), kh, start=True, stop=False)
                        diag = b[:, 0:2 * w].rearrange("p (b k) -> p b k", b=2)[:, :, qt * P:w]
                        return mm(diag, C("mneg"), ident.unsqueeze(1).to_broadcast([P, 2, P]), start=False, stop=True)

                    def values(pt):
                        out = bank[5][64 * half:64 * half + 64, u * T + qt * P:u * T + (qt + 1) * P]
                        for x in range(2 * (qt + 1)):
                            br, kt = x // (qt + 1), x % (qt + 1)
                            mm(out, v_tok[:, br, kt, u * DH:(u + 1) * DH], pt[:, x * P:(x + 1) * P], start=x == 0, stop=False)
                        return mm(out, v_cmp[0:NCMP, u, :], ct[0:NCMP, t * P:(t + 1) * P], start=False, stop=True)

                    return Unit(scores=scores, values=values, before=turn_cmp if t == 0 else None,
                                           tiles=[x * P for x in range(2 * (qt + 1))])

                attention([unit(t) for t in range(8)], j * 8)
            taken(4, 0, 1, 2, 3)
            n["att_S"] += 32
            n["q_mm"] += 4
            n["att_ev"] += 4
            pe.wait_ge(s["att_ev"], n["att_ev"] + 1)
            end_phase()
            gated_out([(1, 1), (2, 2)], KD, lambda k: o_t[:, k, :], 2048)
            end_phase()
            gemm(2, (3, 0), 2, KD, lambda k: merged[:, k, :], T)
            end_phase()
            norm(T)
            end_phase()

            for t in range(TT):
                last = dot(bank[0][:, t * 36:(t + 1) * 36], lambda k: hn[:, k, t * P:(t + 1) * P],
                           lambda k: w_route[:, k, :], KD)
            last.then_inc(s["route_pe"], 1)
            for t in range(TT):
                for k in range(KD):
                    last = tr(bank[2 + 2 * t + k // 4][:, (k % 4) * P:(k % 4 + 1) * P], hn[:, k, t * P:(t + 1) * P], ident)
            last.then_inc(s["tok_mm"], 1)
            pe.wait_ge(s["route_dve"], 3)
            mm(bank[1][:, 0:NE], C("trix"), selm[:, 0, :], start=True, stop=True)
            mm(bank[1][:, NE:2 * NE], C("trix"), selm[:, 1, :], start=True, stop=False)
            mm(bank[1][:, NE:2 * NE], ones, selm[:, 0, :], start=False, stop=True)
            dot(bank[1][0:NE, 2 * NE:2 * NE + 1], lambda t: selm[:, t, :], lambda t: ones[:, 0:1], TT).then_inc(s["route_pe"], 1)
            pe.wait_ge(s["route_dve"], 4)
            mm(bank[0][:, 0:NE], cnt_col[0:NE].to_broadcast([NE, P]), C("trix", NE)[:, 0:NE], start=True, stop=True) \
                .then_inc(s["route_pe"], 1)
            pe.wait_ge(s["moe_G"], 1)
            pe.wait_ge(s["tok_ev"], 1)
            for k in range(KD):
                if k >= 4:
                    pe.wait_ge(s["moe_Xev"], k - 3)
                dot(bank[2 + k % 4][:, :], lambda t: h_tok[:, t, k * P:(k + 1) * P], lambda t: pick[:, t, :], TT) \
                    .then_inc(s["moe_X"], 1)
            pe.wait_ge(s["moe_G"], 2)
            for j in range(PT):
                for t in range(TT):
                    last = tr(bank[6 + j // 2][:, (j % 2) * T + t * P:(j % 2) * T + (t + 1) * P],
                              wpick[:, t, j * P:(j + 1) * P], ident)
            last.then_inc(s["moe_St"], 1)
            pe.wait_ge(s["moe_Stev"], 1)
            pe.wait_ge(s["moe_Xev"], KD)

            def step(i, q, trip):
                if upto(i, ITEMS):
                    pe.wait_ge(s["moe_xt"], i + 1)
                    pe.wait_ge(gu_landed[q % 2], trip * 32 + 16 * (q // 2 + 1))
                    if since(i, 2):
                        pe.wait_ge(s["moe_he"], i - 1)
                    dot(bank[q % 2][:, :], lambda k: x_t[q % 2][:, k, :], lambda k: slot(q % 2)[:, k * 512:(k + 1) * 512], KD) \
                        .then_inc(s["moe_h"], 1)
                if since(i, 1) and upto(i, ITEMS + 1):
                    x = (q + 1) % 2
                    pe.wait_ge(s["moe_he"], i)
                    for b in range(2):
                        last = tr(bank[2 + x][:, b * P:(b + 1) * P], he[:, x, b * P:(b + 1) * P], ident)
                    last.then_inc(s["moe_hT"], 1)
                if since(i, 2):
                    d = (q + 2) % 4
                    pe.wait_ge(s["moe_hTev"], i - 1)
                    pe.wait_ge(dn_landed[d], trip * 16 + (0 if q < 2 else 16))
                    if since(i, 4):
                        pe.wait_ge(s["moe_yacc"], i - 3)
                    for half in range(2):
                        last = dot(bank[4 + 2 * (q % 2) + half][:, :], lambda k: he_t[:, q % 2, k * P:(k + 1) * P],
                                   lambda k: w_down(d)[:, k * D + half * 512:k * D + half * 512 + 512], 2)
                    last.then_inc(s["moe_y"], 1)

            for q in range(4):
                step(q, q, 0)
            with pe.Fori(1, ITEMS // 4) as trip:
                for q in range(4):
                    step(trip * 4 + q, q, trip)
            for q in range(2):
                step(ITEMS + q, q, ITEMS // 4)
            pe.wait_ge(s["moe_yacc"], ITEMS)
            for m in range(KD):
                last = dot(bank[m // 2][:, (m % 2) * T:(m % 2 + 1) * T], lambda j: ys[:, j, m * P:(m + 1) * P],
                           lambda j: s_t[:, j, :], PT)
            end_phase()
            assert ended[0] == MOE_PHASE
            end_phase()
            norm(T)
            end_phase()

            for l in range(2):
                norm(T2)
                end_phase()
                if l == 0:
                    with pe.Fori(0, KVG) as g:
                        for x in range(3):
                            ada_rows(x, 1 + x, g + (used[1 + x] + 1), 1)
                        for x in range(3):
                            ada_cols(bank[4][:, 8 * x:8 * x + 8], g * 3 + (24 + x), x, 2)
                        landed(0, g)

                        def wq(b):
                            return lambda k: slot(0)[:, k * 448 + b * P:k * 448 + (b + 1) * P]

                        for b in range(3):
                            dot(bank[b][:, :], wq(b), lambda k: hn[:, k, :], KD)
                        for t in range(4):
                            last = dot(bank[3][:, t * DH:(t + 1) * DH], lambda k: hn[:, k, t * P:(t + 1) * P],
                                       lambda k: slot(0)[:, k * 448 + 384:k * 448 + 448], KD)
                        last.then_inc(s["q_mm"], 1)
                        free(0)
                        pe.wait_ge(s["q_sq"], g + 1)
                        for b in range(3):
                            last = mm(bank[5 + b][:, :], C("halves"), gq_sq[:, b, :], start=True, stop=True)
                        last.then_inc(s["q_ss"], 1)
                        pe.wait_ge(s["q_normed"], g + 1)
                        for b in range(3):
                            last = mm(bank[5 + b][:, 0:T], C("pgqa"), gq_n[:, b, 0:T], start=True, stop=True)
                        last.then_inc(s["q_rot"], 1)
                        pe.wait_ge(s["q_roped"], g + (4 + 1))

                        def unit(b, half, qt):
                            x = qt < 2
                            nk = 4 if x else 2
                            k0 = 0 if x else T

                            def scores(bk):
                                return mm(bk[:, 0:nk * P], gq_n[64 * half:64 * half + 64, b, qt * P:(qt + 1) * P],
                                          gq_n[64 * half:64 * half + 64, 2, k0:T2], start=True, stop=True)

                            def values(pt):
                                out = bank[5 + b][64 * half:64 * half + 64, qt * P:(qt + 1) * P]
                                return dot(out, lambda k: gv[:, k + k0 // P, :], lambda k: pt[:, k * P:(k + 1) * P], nk)

                            return Unit(scores=scores, values=values, before=None,
                                                   tiles=[k * P for k in range(nk)])

                        attention([unit(b, h, t) for b in range(2) for h in range(2) for t in range(4)], g * 16 + n["att_S"])
                        pe.wait_ge(s["att_ev"], g + (n["att_ev"] + 2))
                    taken(4, 0, 1, 2, 3)
                    n["att_S"] += 64
                    n["att_ev"] += 4
                    end_phase()
                    gemm(2, (1, 2), 2, KD, lambda k: o2[:, k, :], T2)
                else:
                    landed(0)
                    for b in range(3):
                        last = dot(bank[1 + b][:, 0:T], lambda k: slot(0)[:, k * 384 + b * P:k * 384 + (b + 1) * P],
                                   lambda k: hn[:, k, 0:T], KD)
                    landed(1)
                    for b in range(2):
                        dot(bank[4 + b][:, :], lambda k: slot(1)[:, k * 288 + b * P:k * 288 + (b + 1) * P],
                            lambda k: hn[:, k, :], KD)
                    dot(bank[6][ND:QK, :], lambda k: slot(1)[:, k * 288 + 256:k * 288 + 288], lambda k: hn[:, k, :], KD) \
                        .then_inc(s["kv_mm"], 1)
                    free(0, 1)
                    taken(1, 0, 1)
                    pe.wait_ge(s["kv_raw"], 2)
                    dot(bank[0][:, 0:T], lambda b: ones, lambda b: cq_sq[:, b, :], 3)
                    dot(bank[7][:, :], lambda b: ones, lambda b: ckv_sq[:, b, :], 2).then_inc(s["kv_rot"], 1)
                    pe.wait_ge(s["kv_ready"], 2)
                    mm(bank[6][ND:QK, 0:T], C("pmla")[ND:QK, ND:QK], kr_raw[ND:QK, 0:T], start=True, stop=True) \
                        .then_inc(s["kv_dup"], 1)
                    pe.wait_ge(s["cmp_ready"], 2)
                    end_phase()
                    with pe.Fori(0, 4) as i:
                        for q in range(2):
                            sl = 2 + q
                            it = i * 2 + q
                            landed(sl, i)
                            uq = slot(sl)[:, 0:576].rearrange("p (k h c) -> p k h c", k=3, h=2)
                            ukv = slot(sl)[:, 576:1088].rearrange("p (k h c) -> p k h c", k=2, h=2)
                            pe.wait_ge(s["att_ev"], it + (n["att_ev"] + 1))
                            for hh in range(2):
                                dot(bank[6][0:QK, hh * T:(hh + 1) * T], lambda k: uq[:, k, hh, :], lambda k: cqn[:, k, :], 3)
                                dot(bank[hh][0:ND, :], lambda k: ukv[:, k, hh, 0:ND], lambda k: ckvn[:, k, :], 2)
                            for t in range(4):
                                last = dot(bank[2][:, t * P:(t + 1) * P], lambda k: ckvn[:, k, t * P:(t + 1) * P],
                                           lambda k: ukv[:, k, :, ND:P], 2)
                            last.then_inc(s["q_mm"], 1)
                            free(sl)
                            pe.wait_ge(s["q_raw"], it + (4 + 1))
                            mm(bank[7][0:QK, :], C("pmla", QK), mq_raw[0:QK], start=True, stop=True).then_inc(s["q_rot"], 1)
                            pe.wait_ge(s["q_roped"], it + (8 + 1))

                            def unit(hh, qt):
                                def scores(bk):
                                    return mm(bk[:, :], mq_t[0:QK, hh, qt * P:(qt + 1) * P], kcat[hh][0:QK, :],
                                              start=True, stop=True)

                                def values(pt):
                                    return dot(bank[5][64 * hh:64 * hh + 64, qt * P:(qt + 1) * P],
                                               lambda k: mv[:, k, hh * 64:(hh + 1) * 64],
                                               lambda k: pt[:, k * P:(k + 1) * P], 4)

                                return Unit(scores=scores, values=values, before=None,
                                                       tiles=[k * P for k in range(4)])

                            attention([unit(h, t) for h in range(2) for t in range(2)], it * 4 + n["att_S"])
                    taken(4, 2, 3)
                    n["att_S"] += 32
                    n["att_ev"] += 8
                    pe.wait_ge(s["att_ev"], n["att_ev"] + 1)
                    end_phase()
                    gemm(2, (0, 1), 2, KD, lambda k: o2[:, k, 0:T], T)
                end_phase()
                w = T2 if l == 0 else T
                norm(w)
                end_phase()
                with pe.Fori(0, FB // 2) as i:
                    for q in range(2):
                        landed(2 + q, i)
                        pe.wait_ge(s["ffn_ev"], i * 2 + (n["ffn_ev"] + q + 1))
                        for x in range(2):
                            dot(bank[2 * q + x][:, 0:w], lambda k: slot(2 + q)[:, (2 * k + x) * P:(2 * k + x + 1) * P],
                                lambda k: hn[:, k, 0:w], KD).then_inc(s["ffn_mm"], 1)
                        free(2 + q)
                taken(FB // 2, 2, 3)
                n["ffn_ev"] += FB
                end_phase()
                gemm(2, (0, 1, 2, 3), 1, FB, lambda k: act[:, k, 0:w], w)
                end_phase()
            norm(T)
            end_phase()

        @block.scalar
        def _(act_e):
            n = counts()
            norms = [0]
            ended = [0]
            fn = nc.scalar.activation
            act_e.sem_inc(s["att_exp"], 3)
            act_e.sem_inc(s["att_PT"], 2)

            def end_phase():
                act_e.drain().then_inc(phase, 1)
                ended[0] += 1
                act_e.wait_ge(phase, 3 * ended[0])

            def norm(w, shift=None, layer=0):
                b = norms[0]
                for k in range(KD):
                    if k >= 2:
                        act_e.wait_ge(s["sq_used"], 6 * b + k - 1)
                    fn(sq[:, k % 2, 0:w], resid[:, k, 0:w], ACT.Square).then_inc(s["sq_ready"], 1)
                act_e.wait_ge(s["ss_ready"], b + 1)
                fn(rstd[:, 0:w], bank[0][:, 0:w], ACT.Sqrt, scale=1.0 / D, bias=C("eps")).then_inc(s["std_ready"], 1)
                if shift is not None:
                    for k in range(KD):
                        act_e.wait_ge(s["hn_scaled"], n["hn_scaled"] + k + 1)
                        for part in range(w // T):
                            x = hn[:, k, part * T:(part + 1) * T]
                            last = fn(x, x, ACT.Identity, bias=ada[layer][:, shift + k, part:part + 1])
                        last.then_inc(s["hn_ready"], 1)
                    n["hn_scaled"] += KD
                norms[0] += 1

            def gated_out():
                with act_e.Fori(0, 2) as i:
                    for m in range(4):
                        act_e.wait_ge(s["out_mm"], i * 4 + (n["out_mm"] + m + 1))
                        act_e.wait_ge(s["out_ev"], i * 4 + (n["out_mm"] + m + 1))
                        fn(out_sig[:, m, :], bank[m][:, T:T2], ACT.Sigmoid).then_inc(s["out_sig"], 1)
                n["out_mm"] += 8

            def attention(units, done, after):
                U = len(units)
                for t in range(U + 2):
                    if t < U:
                        u = units[t]
                        act_e.wait_ge(s["att_max"], done + (t + 1))
                        act_e.wait_ge(s["att_T"], done + (t + 1))
                        for b in range(u.branches):
                            o = b * u.w
                            last = fn(probs[t % 3][:, o:o + u.w], bank[t % 3][:, o:o + u.w], ACT.Exp,
                                      bias=nmax[:, t % 3, b:b + 1], accum_out=psum_[:, t % 3, b:b + 1])
                        last.then_inc(s["att_exp"], 1)
                    if t >= 2:
                        v = t - 2
                        w = units[v].branches * units[v].w
                        act_e.wait_ge(s["att_T"], done + (v + 4))
                        act_e.wait_ge(s["att_O"], done + (v + 1))
                        fn(probs_t[v % 2][:, 0:w], bank[3 + v % 2][:, 0:w], ACT.Copy).then_inc(s["att_PT"], 1)
                    if t in after:
                        after[t]()

            act_e.wait_ge(s["vec_turned"], 1)
            for v in range(VT):
                r = min(P, VR - v * P)
                fn(cols[:, v * P:v * P + r], bank[v][:, 0:r], ACT.Copy)
            act_e.drain()
            act_e.wait_ge(s["csil_zeroed"], 1)
            for x, name in enumerate(("c", "c_2", "c_ctx_2")):
                last = fn(csil[:, (x + 1) // 2, :, max(x - 1, 0)], cols[:, VO[name]:VO[name] + KD], ACT.Silu)
            last.then_inc(s["csil_ready"], 1)
            act_e.wait_ge(s["rope_reduced"], 1)
            fn(nsin[:, :], ang, ACT.Sin)
            fn(ncos[:, :], tmp_rope, ACT.Sin).then_inc(s["rope_sin"], 1)
            act_e.wait_ge(s["ada_ready"], 1)
            norm(T, 0)
            end_phase()

            act_e.wait_ge(s["dt_pe"], 1)
            fn(gates, bank[7][:, 0:160].rearrange("p (c n) -> p c n", c=2)[:, :, HEADS:80], ACT.Sigmoid).then_inc(s["gates_ready"], 1)
            fn(a_neg, rows32[:, HEADS:2 * HEADS], ACT.Exp)
            act_e.wait_ge(s["dt_dve"], 1)
            fn(dt_b, dt_a, ACT.Exp).then_inc(s["dt_act"], 1)
            act_e.wait_ge(s["dt_dve"], 2)
            fn(dt_a, dt_c, ACT.Ln).then_inc(s["dt_act"], 1)
            act_e.wait_ge(s["dt_dve"], 4)
            fn(ssm_small[:, 6, :], ssm_small[:, 7, :], ACT.Exp).then_inc(s["dt_act"], 1)

            with act_e.Fori(0, GRP) as g:
                act_e.wait_ge(s["ssm_z"], g + 1)
                for b in range(2):
                    fn(zs[:, 2 * b:2 * b + 2, :], bank[b][:, :], ACT.Silu)
                for b in range(6):
                    if b in (0, 4):
                        act_e.wait_ge(s["ssm_x"], g * 2 + (1 if b == 0 else 2))
                    j = g + (16 if b == 4 else 20) if b >= 4 else g * 4 + b
                    fn(conv[:, b, :], bank[2 + b // 2][:, (b % 2) * T:(b % 2 + 1) * T], ACT.Identity,
                       scale=cols[:, ds(j + (VO["conv_w"] + 3 * 24), 1)], bias=cols[:, ds(j + VO["conv_b"], 1)]) \
                        .then_inc(s["ssm_acc"], 1)
                act_e.wait_ge(s["ssm_taps"], g + 1)
                fn(conv, conv, ACT.Silu).then_inc(s["ssm_conv"], 1)
                act_e.wait_ge(s["ssm_tok"], g + 1)
                fn(bcb, bank[4][:, 0:3 * P + 16], ACT.Copy).then_inc(s["ssm_bcb"], 1)
                act_e.wait_ge(s["ssm_E"], g + 1)
                fn(e_bc, bank[7][:, :], ACT.Exp).then_inc(s["ssm_Ex"], 1)
                act_e.wait_ge(s["ssm_state"], g + 1)
                fn(state_t, bank[5][:, :], ACT.Copy).then_inc(s["ssm_stT"], 1)
                for u in range(4):
                    c, hh = u // 2, u % 2
                    act_e.wait_ge(s["ssm_seg"], g * 4 + (u + 1))
                    if u >= 2:
                        act_e.wait_ge(s["ssm_yd"], g * 4 + (u - 1))
                    for h in range(4):
                        last = fn(mexp[:, u % 2, h * P:(h + 1) * P], bank[u % 2][:, h * P:(h + 1) * P], ACT.Exp,
                                  bias=gsm[:, 2 + c, 4 * hh + h:4 * hh + h + 1])
                    last.then_inc(s["ssm_exp"], 1)
                act_e.wait_ge(s["ssm_y"], g + 1)
                fn(ysq, yssm, ACT.Square).then_inc(s["ssm_sq"], 1)
                act_e.wait_ge(s["ssm_ss"], g + 1)
                fn(rs_ssm, bank[7][:, 0:T], ACT.Sqrt, scale=1.0 / 512, bias=C("eps")).then_inc(s["ssm_std"], 1)
            end_phase()
            gated_out()
            end_phase()

            act_e.wait_ge(s["kv_mm"], 1)
            fn(k_raw[:, 0, :], bank[0][:, 0:T], ACT.Copy)
            fn(vc_raw, bank[0][:, T:T2], ACT.Copy)
            fn(k_raw[:, 1:3, :], bank[1][:, :], ACT.Copy).then_inc(s["kv_raw"], 1)
            act_e.wait_ge(s["kv_dup"], 1)
            for g in range(NKV):
                fn(kk[g], bank[g][:, :], ACT.Copy)
            act_e.wait_ge(s["hid_mm"], 1)
            fn(hid, bank[7][:, 0:8 * NCMP], ACT.Silu).then_inc(s["hid_silu"], 1)
            end_phase()

            def nsa_unit(t):
                return Unit(branches=2, w=P * (t % 2 + 1))

            with act_e.Fori(0, 4) as j:
                act_e.wait_ge(s["q_mm"], j + 1)
                fn(q_raw, bank[6][:, :], ACT.Copy).then_inc(s["q_raw"], 1)
                act_e.wait_ge(s["cs_max"], j + 1)
                fn(cs, cs, ACT.Exp).then_inc(s["cs_exp"], 1)

                def copy_cmp():
                    act_e.wait_ge(s["ct_mm"], j + 1)
                    fn(ct[0:NCMP, 0:512], bank[6][0:NCMP, :], ACT.Copy)
                    fn(ct[0:NCMP, 512:1024], bank[7][0:NCMP, :], ACT.Copy).then_inc(s["ct_ev"], 1)

                attention([nsa_unit(t) for t in range(8)], j * 8, {3: copy_cmp})
            n["att_S"] += 32
            end_phase()
            gated_out()
            end_phase()
            end_phase()
            norm(T, 24)
            end_phase()

            act_e.wait_ge(s["tok_mm"], 1)
            for t in range(TT):
                for x in range(2):
                    last = fn(h_tok[:, t, x * 512:(x + 1) * 512], bank[2 + 2 * t + x][:, :], ACT.Copy)
            last.then_inc(s["tok_ev"], 1)
            act_e.wait_ge(s["route_dve"], 1)
            fn(g4b, g4a, ACT.Exp).then_inc(s["route_act"], 1)
            act_e.wait_ge(s["route_dve"], 2)
            fn(e8b, e8a, ACT.Exp).then_inc(s["route_act"], 1)
            for k in range(KD):
                act_e.wait_ge(s["moe_X"], k + 1)
                fn(xs[:, k, :], bank[2 + k % 4][:, :], ACT.Copy).then_inc(s["moe_Xev"], 1)
            act_e.wait_ge(s["moe_St"], 1)
            for x in range(2):
                last = fn(s_t[:, 2 * x:2 * x + 2, :], bank[6 + x][:, :], ACT.Copy)
            last.then_inc(s["moe_Stev"], 1)

            def silu(i, q):
                act_e.wait_ge(s["moe_h"], i + 1)
                if since(i, 2):
                    act_e.wait_ge(s["moe_he"], i - 1)
                fn(hsil[:, q % 2, :], bank[q % 2][:, 0:FH], ACT.Silu).then_inc(s["moe_silu"], 1)

            for q in range(2):
                silu(q, q)
            with act_e.Fori(0, ITEMS // 2 - 1) as i:
                for q in range(2):
                    silu(i * 2 + (q + 2), q)
            end_phase()
            end_phase()
            norm(T)
            end_phase()

            for l in range(2):
                norm(T2, 0, 1 + l)
                end_phase()
                if l == 0:
                    with act_e.Fori(0, KVG) as g:
                        act_e.wait_ge(s["q_mm"], g + 5)
                        for b in range(3):
                            last = fn(gq_sq[:, b, :], bank[b][:, :], ACT.Square)
                        last.then_inc(s["q_sq"], 1)
                        fn(gv, bank[3][:, 0:4 * DH], ACT.Copy)
                        act_e.wait_ge(s["q_ss"], g + 1)
                        for b in range(2):
                            fn(gq_std[:, b, :], bank[5 + b][:, :], ACT.Sqrt, bias=C("eps64"))
                        fn(gq_std[:, 2, :], bank[7][:, :], ACT.Sqrt, scale=1.0 / DH, bias=C("eps")).then_inc(s["q_std"], 1)
                        attention([Unit(branches=1, w=512 if t < 2 else 256)
                                   for _ in range(4) for t in range(4)], g * 16 + n["att_S"], {})
                    n["att_S"] += 64
                    end_phase()
                else:
                    act_e.wait_ge(s["kv_mm"], 2)
                    for b in range(3):
                        fn(cq_sq[:, b, :], bank[1 + b][:, 0:T], ACT.Square)
                    for b in range(2):
                        fn(ckv_sq[:, b, :], bank[4 + b][:, :], ACT.Square)
                    fn(kr_raw[ND:QK, :], bank[6][ND:QK, :], ACT.Copy).then_inc(s["kv_raw"], 1)
                    act_e.wait_ge(s["kv_rot"], 2)
                    fn(rstd[:, 0:T], bank[0][:, 0:T], ACT.Sqrt, scale=1.0 / QL, bias=C("eps"))
                    fn(sq[:, 0, :], bank[7][:, :], ACT.Sqrt, scale=1.0 / KVL, bias=C("eps")).then_inc(s["kv_roped"], 1)
                    end_phase()
                    with act_e.Fori(0, 4) as i:
                        for q in range(2):
                            it = i * 2 + q
                            act_e.wait_ge(s["q_mm"], it + 9)
                            fn(mq_raw[0:QK], bank[6][0:QK, :], ACT.Copy)
                            for hh in range(2):
                                fn(kcat[hh][0:ND, :], bank[hh][0:ND, :], ACT.Copy)
                            fn(mv, bank[2][:, :], ACT.Copy).then_inc(s["q_raw"], 1)
                            attention([Unit(branches=1, w=512) for _ in range(4)], it * 4 + n["att_S"], {})
                    n["att_S"] += 32
                    end_phase()
                end_phase()
                w = T2 if l == 0 else T
                norm(w, 24, 1 + l)
                end_phase()
                cw, cb = VO["ffn_conv_w_2"] + l * 3 * 2 * FB, VO["ffn_conv_b_2"] + l * 2 * FB
                with act_e.Fori(0, FB // 2) as i:
                    for q in range(2):
                        j = i * 2 + q
                        act_e.wait_ge(s["ffn_ev"], j + (n["ffn_ev"] + 1))
                        for x in range(2):
                            act_e.wait_ge(s["ffn_mm"], j * 2 + (2 * n["ffn_ev"] + x + 1))
                            fn(ffn_acc[:, 2 * q + x, 0:w], bank[2 * q + x][:, 0:w], ACT.Identity,
                               scale=cols[:, ds(j + (cw + 2 * FB + x * FB), 1)], bias=cols[:, ds(j + (cb + x * FB), 1)]) \
                                .then_inc(s["ffn_acc"], 1)
                        act_e.wait_ge(s["ffn_taps"], j + (n["ffn_ev"] + 1))
                        g = ffn_acc[:, 2 * q + 1, 0:w]
                        fn(g, g, ACT.Silu).then_inc(s["ffn_silu"], 1)
                n["ffn_ev"] += FB
                end_phase()
                end_phase()
            norm(T)
            end_phase()

        @block.gpsimd
        def _(pool):
            nc.gpsimd.memset(csil[:, :, :, :], 0.0).then_inc(s["csil_zeroed"], 1)
            pool.wait_ge(phase, 3 * (MOE_PHASE - 1))
            nc.gpsimd.memset(ys, 0.0).then_inc(s["moe_zeroed"], 1)
            pool.wait_ge(s["route_dve"], 5)
            pool.wait_ge(s["moe_Xev"], KD)

            def copy_tile(i, q):
                tile = pool.value_load(tile_i.bitcast(I32)[0:1, ds(i, 1)], min_val=0, max_val=PT - 1)
                if since(i, 2):
                    pool.wait_ge(s["moe_h"], i - 1)
                nc.gpsimd.tensor_copy(x_t[q % 2], xs[:, :, bass.ts(tile, P)]).then_inc(s["moe_xt"], 1)

            for q in range(2):
                copy_tile(q, q)
            with pool.Fori(0, ITEMS // 2 - 1) as i:
                for q in range(2):
                    copy_tile(i * 2 + (q + 2), q)

        @block.vector
        def _(ve):
            n = counts()
            norms = [0]
            ended = [0]
            V = nc.vector
            ve.sem_inc(s["out_ev"], 4)
            ve.sem_inc(s["gemm_ev"], 4)
            ve.sem_inc(s["ffn_ev"], 2)
            ve.sem_inc(s["att_ev"], 1)

            def end_phase():
                ve.drain().then_inc(phase, 1)
                ended[0] += 1
                ve.wait_ge(phase, 3 * ended[0])

            def ada_copy(b, c, buf):
                ve.wait_ge(s["ada_mm"], c + 1)
                V.tensor_copy(row_buf[:, buf, :], bank[b][:, :]).then_inc(s["ada_rows"], 1)

            def ada_bias(layer, src, chunks, first, ncol, bias):
                src = src.rearrange("p (n c) -> p n c", c=2)[:, :, 0:ncol]
                V.tensor_tensor(ada[layer][:, ds(first * 4, chunks * 4), 0:ncol], src,
                                cols[:, ds(first * 4 + bias, chunks * 4)].unsqueeze(2).to_broadcast([P, chunks * 4, ncol]),
                                ALU.add).then_inc(s["ada_ready"], 1)

            def modulate(layer, which, ncol, gain):
                for part in range(ncol):
                    V.scalar_tensor_tensor(mod[layer][:, which, part, :], ada[layer][:, 8 + 24 * which:16 + 24 * which, part], 1.0,
                                           cols[:, gain:gain + KD], ALU.add, ALU.mult)
                ve.drain()

            def norm(w, gain, out, shifted):
                ve.wait_ge(s["std_ready"], norms[0] + 1)
                V.reciprocal(rstd[:, 0:w], rstd[:, 0:w])
                ve.drain()
                for k in range(KD):
                    for part in range(w // T):
                        a, b = part * T, (part + 1) * T
                        last = V.scalar_tensor_tensor(out[:, k, a:b], resid[:, k, a:b], gain(part)[:, k:k + 1],
                                                      rstd[:, a:b], ALU.mult, ALU.mult)
                    last.then_inc(s["hn_scaled"] if shifted else s["hn_ready"], 1)
                norms[0] += 1

            def gated_out(first):
                with ve.Fori(0, 2) as i:
                    for m in range(4):
                        ve.wait_ge(s["out_sig"], i * 4 + (n["out_mm"] + m + 1))
                        dst = merged[:, ds(i * 4 + m, 1), :].rearrange("p a t -> p (a t)")
                        if first:
                            V.tensor_tensor(dst, bank[m][:, 0:T], out_sig[:, m, :], ALU.mult).then_inc(s["out_ev"], 1)
                        else:
                            V.tensor_tensor(out_tmp[:, m % 2, :], bank[m][:, 0:T], out_sig[:, m, :], ALU.mult)
                            ve.drain()
                            V.tensor_tensor(dst, dst, out_tmp[:, m % 2, :], ALU.add).then_inc(s["out_ev"], 1)
                n["out_mm"] += 8

            def gemm(trips, per_trip, w, gate, layer=0):
                with ve.Fori(0, trips) as i:
                    for m in range(per_trip):
                        ve.wait_ge(s["gemm_mm"], i * per_trip + (n["gemm_mm"] + m + 1))
                        for part in range(w // T):
                            a, b = part * T, (part + 1) * T
                            dst = resid[:, ds(i * per_trip + m, 1), a:b].rearrange("p a t -> p (a t)")
                            last = V.scalar_tensor_tensor(
                                dst, bank[m % 4][:, a:b],
                                ada[layer][:, ds(i * per_trip + (gate + m), 1), part:part + 1].rearrange("p a t -> p (a t)"),
                                dst, ALU.mult, ALU.add)
                        last.then_inc(s["gemm_ev"], 1)
                n["gemm_mm"] += trips * per_trip

            def attention(units, done):
                U = len(units)
                for t in range(U + 1):
                    if t < U:
                        u = units[t]
                        ve.wait_ge(s["att_S"], done + (t + 1))
                        V.tensor_reduce(nmax[:, t % 3, 0:u.branches],
                                        bank[t % 3][:, 0:u.branches * u.w].rearrange("p (b k) -> p b k", b=u.branches),
                                        AX.X, ALU.max, negate=True).then_inc(s["att_max"], 1)
                    if t >= 1:
                        v = t - 1
                        u = units[v]
                        ve.wait_ge(s["att_exp"], done + (v + 4))
                        fac = pfac[:, v % 3, 0:u.branches]
                        V.reciprocal(fac, psum_[:, v % 3, 0:u.branches])
                        ve.drain()
                        if u.gate is not None:
                            V.tensor_tensor(fac, fac, u.gate, ALU.mult)
                            ve.drain()
                        for b in range(u.branches):
                            pb = probs[v % 3][:, b * u.w:(b + 1) * u.w]
                            last = V.tensor_scalar(pb, pb, fac[:, b:b + 1], None, ALU.mult)
                        last.then_inc(s["att_scaled"], 1)

            ve.wait_ge(setup_landed, 16 * SETUP_DMAS)
            V.tensor_copy(pos_f, pos_i.bitcast(I32))
            ve.drain()
            V.tensor_scalar(ang, pos_f, C("invf"), None, ALU.mult)
            ve.drain()
            for quarter, dst in ((0.25, tmp_rope), (0.0, ang)):
                V.tensor_scalar(turns, ang, 1.0 / (2 * math.pi), quarter, ALU.mult, ALU.add)
                ve.drain()
                V.tensor_scalar(turns, turns, 1.5 * 2 ** 23, None, ALU.add)
                ve.drain()
                V.tensor_scalar(turns, turns, -1.5 * 2 ** 23, None, ALU.add)
                ve.drain()
                src = ang
                for part in TWO_PI:
                    V.scalar_tensor_tensor(dst, turns, -part, src, ALU.mult, ALU.add)
                    ve.drain()
                    src = dst
                if quarter:
                    V.tensor_scalar(dst, dst, math.pi / 2, None, ALU.add)
                    ve.drain()
                V.tensor_scalar(dst, dst, PI_BELOW, -PI_BELOW, ALU.min, ALU.max)
                ve.drain()
            ve.drain().then_inc(s["rope_reduced"], 1)
            ve.wait_ge(s["csil_ready"], 1)
            for q in range(4):
                if q == 3:
                    ve.wait_ge(s["ada_cols"], 1)
                ada_copy(q, q, q % 3)
            ve.wait_ge(s["ada_cols"], 4)
            ada_bias(0, bank[4][:, 0:32], 4, 0, 1, VO["b_ada"])
            ve.drain()
            modulate(0, 0, 1, VO["norm1_g"])
            norm(T, lambda part: mod[0][:, 0, part, :], hn, True)
            end_phase()

            ve.wait_ge(s["rope_sin"], 1)
            V.tensor_scalar(ncos8, ncos[:, :], DH ** -0.5, None, ALU.mult)
            V.tensor_scalar(nsin8, nsin[:, :], DH ** -0.5, None, ALU.mult)
            ve.wait_ge(s["gates_ready"], 1)
            bias = rows32[:, 0:HEADS].unsqueeze(1).to_broadcast([P, 2, HEADS])
            V.tensor_tensor(dt_in, bank[7][:, 0:160].rearrange("p (c n) -> p c n", c=2)[:, :, 0:HEADS], bias, ALU.add)
            ve.drain()
            V.tensor_scalar(dt_a, dt_in, -1.0, None, ALU.mult)
            ve.drain()
            V.tensor_tensor(dt_a, dt_a, dt_in, ALU.min).then_inc(s["dt_dve"], 1)
            ve.wait_ge(s["dt_act"], 1)
            V.tensor_scalar(dt_c, dt_b, 1.0, None, ALU.add)
            ve.drain().then_inc(s["dt_dve"], 1)
            V.tensor_scalar(dt_d, dt_c, -1.0, None, ALU.add)
            ve.drain()
            ve.wait_ge(s["dt_act"], 2)
            V.tensor_scalar(dt_c, dt_d, 0.0, None, ALU.is_equal)
            ve.drain()
            V.tensor_tensor(dt_a, dt_a, dt_c, ALU.add)
            V.tensor_tensor(dt_d, dt_d, dt_c, ALU.add)
            ve.drain()
            V.reciprocal(dt_d, dt_d)
            V.tensor_tensor(dt_a, dt_a, dt_b, ALU.mult)
            ve.drain()
            V.tensor_tensor(dt_a, dt_a, dt_d, ALU.mult)
            V.tensor_scalar(dt_b, dt_in, 0.0, None, ALU.max)
            ve.drain()
            dt = ssm_small[:, 4:6, :]
            V.tensor_tensor(dt, dt_a, dt_b, ALU.add)
            ve.drain()
            V.tensor_tensor(ssm_small[:, 0:2, :], dt, a_neg.unsqueeze(1).to_broadcast([P, 2, HEADS]), ALU.mult)
            ve.drain()
            V.tensor_scalar(ssm_small[:, 0:2, :], ssm_small[:, 0:2, :], -1.0, None, ALU.mult)
            ve.drain().then_inc(s["dt_dve"], 1)
            ve.wait_ge(s["dt_pe"], 2)
            cum = bank[6][:, 0:2 * HEADS].rearrange("p (c n) -> p c n", c=2)
            V.tensor_scalar(ssm_small[:, 2:4, :], cum, -1.0, None, ALU.mult)
            ve.drain()
            V.tensor_tensor(ssm_small[:, 7, :], ssm_small[:, 2, :], bank[6][:, 2 * HEADS:3 * HEADS], ALU.add)
            ve.drain().then_inc(s["dt_dve"], 1)
            ve.wait_ge(s["dt_act"], 3)
            ve.drain().then_inc(s["group_done"], 1)

            with ve.Fori(0, GRP) as g:
                ada_copy(5, g * 2 + 4, 0)
                V.tensor_copy(gsm, ssm_small[:, :, ds(g * HPG, HPG)])
                ve.drain()
                V.tensor_copy(dt_wide.rearrange("p (h d) -> p h d", h=HPG), gsm[:, 1, :].unsqueeze(2).to_broadcast([P, HPG, HD])) \
                    .then_inc(s["gsm_ready"], 1)
                for back in range(1, CONV):
                    for b in range(6):
                        if back == 1 and b % 2 == 0:
                            ve.wait_ge(s["ssm_acc"], g * 6 + (b + 2))
                        j = g + (16 if b == 4 else 20) if b >= 4 else g * 4 + b
                        u = bank[2 + b // 2][:, (b % 2) * T:(b % 2 + 1) * T]
                        V.scalar_tensor_tensor(conv[:, b, back:T], u[:, 0:T - back],
                                               cols[:, ds(j + (VO["conv_w"] + (CONV - 1 - back) * 24), 1)],
                                               conv[:, b, back:T], ALU.mult, ALU.add)
                    if back < CONV - 1:
                        ve.drain()
                ve.drain().then_inc(s["ssm_taps"], 1)
                ada_copy(6, g * 2 + 5, 1)
                ve.wait_ge(s["ssm_tok"], g + 1)
                for c in range(2):
                    V.tensor_tensor(xdt[:, c, :].rearrange("p (h d) -> p h d", h=HPG),
                                    bank[5 + c][:, :].rearrange("p (h d) -> p h d", h=HPG),
                                    gsm[:, 4 + c, :].unsqueeze(2).to_broadcast([P, HPG, HD]), ALU.mult)
                ve.drain()
                V.tensor_tensor(xw.rearrange("p (h d) -> p h d", h=HPG), xdt[:, 0, :].rearrange("p (h d) -> p h d", h=HPG),
                                gsm[:, 6, :].unsqueeze(2).to_broadcast([P, HPG, HD]), ALU.mult).then_inc(s["ssm_xw"], 1)
                ve.wait_ge(s["ssm_bcb"], g + 1)
                ada_bias(0, ssm_ada, 2, g * 2 + 4, 1, VO["b_ada"])
                for u in range(4):
                    ve.wait_ge(s["ssm_exp"], g * 4 + (u + 1))
                    m = mexp[:, u % 2, :].rearrange("p (h t) -> p h t", h=4)
                    V.tensor_tensor(m, m, cb[:, u // 2, :].unsqueeze(1).to_broadcast([P, 4, P]), ALU.mult) \
                        .then_inc(s["ssm_M"], 1)
                ve.wait_ge(s["ssm_yoff"], g + 1)
                ve.wait_ge(s["ssm_Ex"], g + 1)
                V.tensor_tensor(yoff, bank[6][:, :].rearrange("p (b t) -> p b t", b=4),
                                e_bc.rearrange("p (b t) -> p b t", b=4), ALU.mult)
                ve.wait_ge(s["ssm_yd"], g * 4 + 4)
                for b in range(4):
                    V.scalar_tensor_tensor(yssm[:, b, :], conv[:, b, :], cols[:, ds(g * 4 + (VO["d_skip"] + b), 1)],
                                           bank[2 + b // 2][:, (b % 2) * T:(b % 2 + 1) * T], ALU.mult, ALU.add)
                ve.drain()
                V.tensor_tensor(yssm[:, :, P:T], yssm[:, :, P:T], yoff, ALU.add)
                ve.drain()
                V.tensor_tensor(yssm, yssm, zs, ALU.mult).then_inc(s["ssm_y"], 1)
                ve.wait_ge(s["ssm_std"], g + 1)
                V.reciprocal(rs_ssm, rs_ssm)
                ve.drain()
                for b in range(4):
                    last = V.scalar_tensor_tensor(ynorm[:, ds(g * 4 + b, 1), :].rearrange("p a t -> p (a t)"), yssm[:, b, :],
                                                  cols[:, ds(g * 4 + (VO["ssm_norm_g"] + b), 1)], rs_ssm, ALU.mult, ALU.mult)
                last.then_inc(s["group_done"], 1)
            end_phase()
            gated_out(True)
            end_phase()

            ve.wait_ge(s["kv_mm"], 1)
            V.tensor_copy(v_tok.rearrange("p b t d -> p (b t d)"), bank[2][:, :])
            ve.wait_ge(s["kv_raw"], 1)

            def over(table, m):
                return table.unsqueeze(1).to_broadcast([P, m, T])

            V.tensor_tensor(k_roped, k_raw, over(ncos[:, :], 3), ALU.mult)
            ve.wait_ge(s["kv_rot"], 1)
            V.tensor_tensor(k_tmp[:, 0:2, :], bank[3][:, :].rearrange("p (a t) -> p a t", a=2), over(nsin[:, :], 2), ALU.mult)
            V.tensor_tensor(k_tmp[:, 2, :], bank[4][:, 0:T], nsin[:, :], ALU.mult)
            ve.drain()
            V.tensor_tensor(k_roped, k_roped, k_tmp, ALU.add).then_inc(s["kv_roped"], 1)
            ve.wait_ge(s["kv_dup"], 1)
            for x, name in enumerate(("cmp_pe_k", "cmp_pe_v")):
                pe_cols = cols[:, VO[name]:VO[name] + 16]
                for g in range(NKV):
                    src = bank[5 + x][:, g * T:(g + 1) * T].rearrange("p (c j) -> p j c", j=STRIDE)
                    for h in range(2):
                        rows = slice(64 * h, 64 * h + 64)
                        for late in range(2):
                            V.tensor_tensor(blk[x][rows, 8 * late:8 * late + 8, g * NCMP:(g + 1) * NCMP],
                                            src[rows, h:STRIDE:2, late:late + NCMP],
                                            pe_cols[rows, 8 * late:8 * late + 8].unsqueeze(2).to_broadcast([64, 8, NCMP]), ALU.add)
            ve.drain().then_inc(s["kv_ready"], 1)
            ve.wait_ge(s["cmp_mm"], 1)
            V.tensor_copy(k_cmp, bank[4][:, 256:256 + 2 * NCMP])
            V.tensor_copy(v_cmp[0:NCMP].rearrange("p g d -> p (g d)"), bank[4][0:NCMP, 320:320 + 2 * DH])
            ve.drain().then_inc(s["cmp_ready"], 1)
            end_phase()

            with ve.Fori(0, 4) as j:
                for x in range(3):
                    ada_copy(x, j * 3 + (12 + x), x)
                gv_ = gates.rearrange("p q (u j h b) -> p u j h q b", u=2, j=4, h=2, b=3)
                for b in range(3):
                    for u in range(2):
                        V.tensor_copy(gsel[:, b, 4 * u:4 * u + 4].rearrange("p (h q) -> p h q", h=2),
                                      gv_[:, u, ds(j, 1), :, :, b].rearrange("p a h q -> p (a h) q"))
                ve.wait_ge(s["ada_cols"], j * 3 + 15)
                ada_bias(1, bank[3][:, 0:24], 3, j * 3, 2, VO["ada_b_2"])
                ve.wait_ge(s["q_raw"], j + 1)
                V.tensor_tensor(q_t, q_raw, over(ncos8, 2), ALU.mult)
                ve.wait_ge(s["q_rot"], j + 1)
                V.tensor_tensor(q_tmp, bank[7][:, :].rearrange("p (a t) -> p a t", a=2), over(nsin8, 2), ALU.mult)
                ve.drain()
                V.tensor_tensor(q_t, q_t, q_tmp, ALU.add).then_inc(s["q_roped"], 1)
                ve.wait_ge(s["cs_mm"], j + 1)
                for half in range(2):
                    V.tensor_tensor(cs[:, half:4:2, :], bank[7 - half][:, 0:4 * NCMP].rearrange("p (a c) -> p a c", a=2),
                                    C("cneg").unsqueeze(1).to_broadcast([P, 2, 2 * NCMP]), ALU.add)
                ve.drain()
                cs8 = cs.rearrange("p a (q c) -> p (a q) c", q=2)
                V.tensor_reduce(cs_m, cs8, AX.X, ALU.max)
                ve.drain()
                V.tensor_tensor(cs8, cs8, cs_m.unsqueeze(2).to_broadcast([P, 8, NCMP]), ALU.subtract).then_inc(s["cs_max"], 1)
                ve.wait_ge(s["cs_exp"], j + 1)
                V.tensor_tensor(cs, cs, C("c01").unsqueeze(1).to_broadcast([P, 4, 2 * NCMP]), ALU.mult)
                ve.drain()
                V.tensor_reduce(cs_s, cs8, AX.X, ALU.add)
                ve.drain()
                V.tensor_scalar(cs_s, cs_s, 1e-30, None, ALU.max)
                ve.drain()
                V.reciprocal(cs_s, cs_s)
                ve.drain()
                V.tensor_tensor(cs_s, cs_s, gsel[:, 0, :], ALU.mult)
                ve.drain()
                V.tensor_tensor(cs8, cs8, cs_s.unsqueeze(2).to_broadcast([P, 8, NCMP]), ALU.mult).then_inc(s["cs_ready"], 1)
                attention([Unit(branches=2, w=P * (t % 2 + 1), gate=gsel[:, 1:3, t]) for t in range(8)], j * 8)
                ve.wait_ge(s["att_O"], j * 8 + 10)
                for u in range(2):
                    last = V.tensor_copy(o_t[:, ds(j + 4 * u, 1), :].rearrange("p a t -> p (a t)"), bank[5][:, u * T:(u + 1) * T])
                last.then_inc(s["att_ev"], 1)
            n["att_S"] += 32
            end_phase()
            gated_out(False)
            end_phase()
            gemm(2, 4, T, 16)
            end_phase()
            modulate(0, 1, 1, VO["norm2_g"])
            norm(T, lambda part: mod[0][:, 1, part, :], hn, True)
            end_phase()

            ve.wait_ge(s["route_pe"], 1)

            def b2(x, m):
                return x.to_broadcast([P, 2, m])

            def first_max(x, rev, top, key, out, m):
                V.tensor_reduce(top, x, AX.X, ALU.max)
                ve.drain()
                V.tensor_tensor(key, x, b2(top, m), ALU.is_equal)
                ve.drain()
                V.tensor_tensor(key, key, rev.unsqueeze(1).to_broadcast([P, 2, m]), ALU.mult)
                ve.drain()
                V.tensor_reduce(t2f, key, AX.X, ALU.max)
                ve.drain()
                V.tensor_tensor(out, key, b2(t2f, m), ALU.is_equal)
                ve.drain()

            V.tensor_tensor(lg, bank[0][:, 0:72].rearrange("p (t n) -> p t n", t=2),
                            rows32[:, 3 * HEADS:].unsqueeze(1).to_broadcast([P, 2, 36]), ALU.add)
            ve.drain()
            gl, el = lg[:, :, 0:NG], lg[:, :, NG:NG + NE]
            first_max(gl, C("rev4"), t2a, g4b, g4c, NG)
            V.tensor_tensor(g4a, gl, b2(t2a, NG), ALU.subtract)
            ve.drain().then_inc(s["route_dve"], 1)
            for t in range(2):
                V.tensor_tensor(e32[:, t], el[:, t].rearrange("p (g e) -> p g e", g=NG),
                                g4c[:, t, :].unsqueeze(2).to_broadcast([P, NG, EPG]), ALU.mult)
            ve.drain()
            for t in range(2):
                V.tensor_reduce(e8c[:, t, :], e32[:, t].rearrange("p g e -> p e g"), AX.X, ALU.add)
            ve.drain()
            V.tensor_reduce(t2b, e8c, AX.X, ALU.max)
            ve.drain()
            V.tensor_tensor(e8a, e8c, b2(t2b, EPG), ALU.subtract)
            ve.drain().then_inc(s["route_dve"], 1)
            ve.wait_ge(s["route_act"], 1)
            V.tensor_reduce(t2a, g4b, AX.X, ALU.add)
            ve.drain()
            V.reciprocal(t2a, t2a)
            ve.wait_ge(s["route_act"], 2)
            V.tensor_reduce(t2b, e8b, AX.X, ALU.add)
            ve.drain()
            V.reciprocal(t2b, t2b)
            ve.drain()
            V.tensor_tensor(e8b, e8b, b2(t2b, EPG), ALU.mult)
            ve.drain()
            first_max(e8b, C("rev8"), t2b, e8c, e8d, EPG)
            V.scalar_tensor_tensor(e8b, e8d, -2.0, e8b, ALU.mult, ALU.add)
            ve.drain()
            first_max(e8b, C("rev8"), t2c, e8c, e8e, EPG)
            V.tensor_tensor(t2d, t2b, t2c, ALU.add)
            ve.drain()
            V.reciprocal(t2d, t2d)
            V.tensor_tensor(t2b, t2b, t2a, ALU.mult)
            V.tensor_tensor(t2c, t2c, t2a, ALU.mult)
            ve.drain()
            V.tensor_tensor(t2b, t2b, t2d, ALU.mult)
            V.tensor_tensor(t2c, t2c, t2d, ALU.mult)
            for t in range(2):
                og = g4c[:, t, :].unsqueeze(2).to_broadcast([P, NG, EPG])
                for dst, src in ((sel_a, e8d), (sel_b, e8e)):
                    V.tensor_tensor(dst[:, t, :].rearrange("p (g e) -> p g e", g=NG), og,
                                    src[:, t, :].unsqueeze(1).to_broadcast([P, NG, EPG]), ALU.mult)
            ve.drain()
            V.tensor_tensor(selm, sel_a, sel_b, ALU.add)
            ve.drain().then_inc(s["route_dve"], 1)
            ve.wait_ge(s["route_pe"], 2)
            V.tensor_copy(cnt_col[0:NE], bank[1][0:NE, 2 * NE:2 * NE + 1])
            V.tensor_copy(pos, bank[1][:, 0:2 * NE].rearrange("p (t e) -> p t e", t=2))
            ve.drain().then_inc(s["route_dve"], 1)
            ve.wait_ge(s["route_pe"], 3)
            V.tensor_copy(start, bank[0][:, 0:NE])
            ve.drain()
            V.tensor_tensor(pos, pos, start.unsqueeze(1).to_broadcast([P, 2, NE]), ALU.add)
            ve.drain()
            V.tensor_tensor(sel_a, sel_a, pos, ALU.mult)
            V.tensor_tensor(sel_b, sel_b, pos, ALU.mult)
            ve.drain()
            V.tensor_reduce(pos_a, sel_a, AX.X, ALU.add)
            V.tensor_reduce(pos_b, sel_b, AX.X, ALU.add)
            ve.drain()
            ve.wait_ge(s["moe_iota"], 16)
            for t in range(2):
                V.tensor_scalar(pick[:, t, :], iota, pos_a[:, t, :], None, ALU.is_equal)
            ve.drain()
            for t in range(2):
                V.scalar_tensor_tensor(pick[:, t, :], iota, pos_b[:, t, :], pick[:, t, :], ALU.is_equal, ALU.add)
            ve.drain().then_inc(s["moe_G"], 1)
            V.tensor_tensor(at_end, start.unsqueeze(1).to_broadcast([P, PT - 1, NE]),
                            C("tile_end").unsqueeze(2).to_broadcast([P, PT - 1, NE]), ALU.is_lt)
            V.tensor_tensor(before_place, start.unsqueeze(1).to_broadcast([P, PT, NE]),
                            C("place").unsqueeze(2).to_broadcast([P, PT, NE]), ALU.is_le)
            ve.drain()
            V.tensor_reduce(ends, at_end, AX.X, ALU.add)
            V.tensor_reduce(code_place, before_place, AX.X, ALU.add)
            ve.drain()
            V.tensor_tensor(ends, ends, C("tile"), ALU.add)
            V.tensor_tensor(code_place, code_place, C("code"), ALU.add)
            ve.drain()
            V.tensor_tensor(tile_f3, iota[:, 0:ITEMS].unsqueeze(1).to_broadcast([P, PT - 1, ITEMS]),
                            ends.unsqueeze(2).to_broadcast([P, PT - 1, ITEMS]), ALU.is_ge)
            ve.drain()
            V.tensor_reduce(tile_f, tile_f3.rearrange("p j i -> p i j"), AX.X, ALU.add)
            ve.drain()
            V.tensor_tensor(expert_f, iota[:, 0:ITEMS], tile_f, ALU.subtract)
            V.scalar_tensor_tensor(code_item, tile_f, 2.0 * NE - 1, iota[:, 0:ITEMS], ALU.mult, ALU.add)
            V.tensor_copy(tile_i.bitcast(I32), tile_f)
            ve.drain()
            V.tensor_scalar(expert_f, expert_f, NE - 1.0, None, ALU.min)
            ve.drain()
            V.tensor_copy(expert_i.bitcast(I32), expert_f)
            ve.drain().then_inc(s["route_dve"], 1)
            V.tensor_scalar(mask, code_item, code_place[:, 0:1], None, ALU.is_equal)
            for j in range(1, PT):
                ve.drain()
                V.scalar_tensor_tensor(mask, code_item, code_place[:, j:j + 1], mask, ALU.is_equal, ALU.add)
            for t in range(2):
                V.tensor_scalar(wpick[:, t, :], iota, pos_a[:, t, :], t2b[:, t, :], ALU.is_equal, ALU.mult)
                V.tensor_scalar(wpick_b, iota, pos_b[:, t, :], t2c[:, t, :], ALU.is_equal, ALU.mult)
                ve.drain()
                V.tensor_tensor(wpick[:, t, :], wpick[:, t, :], wpick_b, ALU.add)
                ve.drain()
            ve.drain().then_inc(s["moe_G"], 1)
            ve.wait_ge(s["moe_zeroed"], 1)

            def step(i, q):
                if since(i, 1) and upto(i, ITEMS + 1):
                    x = (q + 1) % 2
                    ve.wait_ge(s["moe_silu"], i)
                    if since(i, 3):
                        ve.wait_ge(s["moe_hT"], i - 2)
                    V.scalar_tensor_tensor(he[:, x, :], hsil[:, x, :], mask[:, ds(i - 1, 1)], bank[x][:, FH:2 * FH],
                                           ALU.mult, ALU.mult).then_inc(s["moe_he"], 1)
                    ve.wait_ge(s["moe_hT"], i)
                    if since(i, 3):
                        ve.wait_ge(s["moe_y"], i - 2)
                    V.tensor_copy(he_t[:, x, :], bank[2 + x][:, 0:FH]).then_inc(s["moe_hTev"], 1)
                if since(i, 2):
                    ve.drain()
                    tile = ve.value_load(tile_i.bitcast(I32)[0:1, ds(i - 2, 1)], min_val=0, max_val=PT - 1)
                    ve.wait_ge(s["moe_y"], i - 1)
                    for half in range(2):
                        y = ys[:, ds(tile, 1), half * 512:(half + 1) * 512].rearrange("p a d -> p (a d)")
                        last = V.tensor_tensor(y, y, bank[4 + 2 * (q % 2) + half][:, :], ALU.add)
                    last.then_inc(s["moe_yacc"], 1)

            for q in range(4):
                step(q, q)
            with ve.Fori(1, ITEMS // 4) as trip:
                for q in range(4):
                    step(trip * 4 + q, q)
            for q in range(2):
                step(ITEMS + q, q)
            end_phase()
            for k in range(KD):
                V.scalar_tensor_tensor(resid[:, k, 0:T], bank[k // 2][:, (k % 2) * T:(k % 2 + 1) * T], ada[0][:, 40 + k, 0:1],
                                       resid[:, k, 0:T], ALU.mult, ALU.add)
            end_phase()
            norm(T, lambda part: cols[:, VO["final_g"]:VO["final_g"] + KD], resid, False)
            end_phase()

            for l in range(2):
                for which, name in enumerate(("norm1_g_2", "norm2_g_2")):
                    modulate(1 + l, which, 2, VO[name] + KD * l)
                norm(T2, lambda part: mod[1 + l][:, 0, part, :], hn, True)
                end_phase()
                if l == 0:
                    with ve.Fori(0, KVG) as g:
                        for x in range(3):
                            ada_copy(x, g * 3 + (24 + x), x)
                        ve.wait_ge(s["ada_cols"], g * 3 + 27)
                        ada_bias(2, bank[4][:, 0:24], 3, g * 3, 2, VO["ada_b_2"] + 48)
                        ve.wait_ge(s["q_std"], g + 1)
                        V.reciprocal(gq_std.rearrange("p a t -> p (a t)"), gq_std.rearrange("p a t -> p (a t)"))
                        ve.drain()
                        for b in range(3):
                            gain = VO["gqa_q_norm_g_2"] if b < 2 else VO["gqa_k_norm_g_2"]
                            V.scalar_tensor_tensor(gq_n[:, b, :], bank[b][:, :], cols[:, gain:gain + 1], gq_std[:, b, :],
                                                   ALU.mult, ALU.mult)
                        ve.drain().then_inc(s["q_normed"], 1)
                        ve.wait_ge(s["q_rot"], g + 5)
                        V.tensor_tensor(gq_sq[:, :, 0:T], gq_n[:, :, 0:T], over(C("gcos"), 3), ALU.mult)
                        for b in range(3):
                            V.tensor_tensor(gq_std[:, b, 0:T], bank[5 + b][:, 0:T], C("gsin"), ALU.mult)
                        ve.drain()
                        V.tensor_tensor(gq_n[:, :, 0:T], gq_sq[:, :, 0:T], gq_std[:, :, 0:T], ALU.add).then_inc(s["q_roped"], 1)
                        attention([Unit(branches=1, w=512 if t < 2 else 256, gate=None)
                                   for _ in range(4) for t in range(4)], g * 16 + n["att_S"])
                        ve.wait_ge(s["att_O"], g * 16 + (n["att_S"] + 18))
                        for b in range(2):
                            last = V.tensor_copy(o2[:, ds(g * 2 + b, 1), :].rearrange("p a t -> p (a t)"), bank[5 + b][:, :])
                        last.then_inc(s["att_ev"], 1)
                    n["att_S"] += 64
                    end_phase()
                    gemm(2, 4, T2, 16, 1)
                else:
                    V.tensor_scalar(qcos[0:QK], C("mcos", QK), QK ** -0.5, None, ALU.mult)
                    V.tensor_scalar(qsin[0:QK], C("msin", QK), QK ** -0.5, None, ALU.mult)
                    ve.wait_ge(s["kv_roped"], 2)
                    V.reciprocal(rstd[:, 0:T], rstd[:, 0:T])
                    V.reciprocal(sq[:, 0, :], sq[:, 0, :])
                    ve.drain()
                    for b in range(3):
                        V.scalar_tensor_tensor(cqn[:, b, :], bank[1 + b][:, 0:T], col("mla_q_norm_g_2", b), rstd[:, 0:T],
                                               ALU.mult, ALU.mult)
                    for b in range(2):
                        V.scalar_tensor_tensor(ckvn[:, b, :], bank[4 + b][:, :], col("mla_kv_norm_g_2", b), sq[:, 0, :],
                                               ALU.mult, ALU.mult)
                    ve.drain().then_inc(s["kv_ready"], 1)
                    r = slice(ND, QK)
                    ve.wait_ge(s["kv_dup"], 2)
                    V.tensor_tensor(kr_roped[r, 0:T], kr_raw[r, 0:T], consts[r, CO["mcos"][0]:CO["mcos"][0] + T], ALU.mult)
                    V.tensor_tensor(kr_roped[r, T:T2], bank[6][r, 0:T], consts[r, CO["msin"][0]:CO["msin"][0] + T], ALU.mult)
                    ve.drain()
                    for hh in range(2):
                        V.tensor_tensor(kcat[hh][r, 0:T], kr_roped[r, 0:T], kr_roped[r, T:T2], ALU.add)
                        V.tensor_copy(kcat[hh][r, T:T2], kr_raw[r, T:T2])
                    ve.drain().then_inc(s["cmp_ready"], 1)
                    end_phase()
                    with ve.Fori(0, 4) as i:
                        for q in range(2):
                            it = i * 2 + q
                            ve.wait_ge(s["q_rot"], it + 9)
                            V.tensor_tensor(mq_t[0:QK], mq_raw[0:QK], qcos[0:QK].unsqueeze(1).to_broadcast([QK, 2, T]), ALU.mult)
                            V.tensor_tensor(mq_tmp[0:QK], bank[7][0:QK, :].rearrange("p (a t) -> p a t", a=2),
                                            qsin[0:QK].unsqueeze(1).to_broadcast([QK, 2, T]), ALU.mult)
                            ve.drain()
                            V.tensor_tensor(mq_t[0:QK], mq_t[0:QK], mq_tmp[0:QK], ALU.add).then_inc(s["q_roped"], 1)
                            attention([Unit(branches=1, w=512, gate=None) for _ in range(4)], it * 4 + n["att_S"])
                            ve.wait_ge(s["att_O"], it * 4 + (n["att_S"] + 6))
                            V.tensor_copy(o2[:, ds(it, 1), 0:T].rearrange("p a t -> p (a t)"), bank[5][:, 0:T]).then_inc(s["att_ev"], 1)
                    n["att_S"] += 32
                    end_phase()
                    gemm(2, 4, T, 16, 2)
                end_phase()
                w = T2 if l == 0 else T
                norm(w, lambda part: mod[1 + l][:, 1, part, :], hn, True)
                end_phase()
                cw = VO["ffn_conv_w_2"] + l * 3 * 2 * FB
                with ve.Fori(0, FB // 2) as i:
                    for q in range(2):
                        j = i * 2 + q
                        for tap in (0, 2):
                            for x in range(2):
                                if tap == 0:
                                    ve.wait_ge(s["ffn_acc"], j * 2 + (2 * n["ffn_ev"] + x + 1))
                                u = bank[2 * q + x][:, 0:w].rearrange("p (a t) -> p a t", t=T)
                                a = ffn_acc[:, 2 * q + x, 0:w].rearrange("p (a t) -> p a t", t=T)
                                uu, aa = (u[:, :, 0:T - 1], a[:, :, 1:T]) if tap == 0 else (u[:, :, 1:T], a[:, :, 0:T - 1])
                                V.scalar_tensor_tensor(aa, uu, cols[:, ds(j + (cw + tap * 2 * FB + x * FB), 1)], aa,
                                                       ALU.mult, ALU.add)
                            ve.drain() if tap == 0 else ve.drain().then_inc(s["ffn_taps"], 1)
                        ve.wait_ge(s["ffn_silu"], j + (n["ffn_ev"] + 1))
                        V.tensor_tensor(act[:, ds(j, 1), 0:w].rearrange("p a t -> p (a t)"), ffn_acc[:, 2 * q, 0:w],
                                        ffn_acc[:, 2 * q + 1, 0:w], ALU.mult).then_inc(s["ffn_ev"], 1)
                n["ffn_ev"] += FB
                end_phase()
                gemm(2, 4, w, 40, 1 + l)
                end_phase()
            norm(T, lambda part: cols[:, VO["final_norm_g_2"]:VO["final_norm_g_2"] + KD], resid, False)
            end_phase()


def kernel(**inputs):
    import concourse.bacc as bacc
    from concourse.bass_utils import run_bass_kernel_spmd as run

    x = {k: np.asarray(v) for k, v in inputs.items()}

    def rows(a):
        return np.broadcast_to(a, (P,) + a.shape)

    w_in, up, down, ada2 = x["w_in"][0], x["ffn_w_up_2"], x["ffn_w_down_2"], x["ada_w_2"]
    vec = dict(x)
    vec["d_skip"] = np.repeat(x["d_skip"], HD)
    for name in ("gqa_q_norm_g_2", "gqa_k_norm_g_2"):
        vec[name] = np.tile(x[name], 2)

    def span(o, i, w):
        return o + i * w, o + (i + 1) * w

    n256 = [span(0, i, 256) for i in range(4)]
    g_in, u_q, u_kv = x["gqa_w_in_2"][0], x["mla_w_uq_2"][0], x["mla_w_ukv_2"][0]
    wg, wu, wd = x["w_exp_gate"][0], x["w_exp_up"][0], x["w_exp_down"][0]
    o_b, o_c = O_XBC + DIN, O_XBC + DIN + GRP * ST
    mla_in = x["mla_w_in_2"][0]
    wide = np.zeros((P, 3072 - 2304), np.float32)
    chunks = {
        "ada": [pack(x["w_ada"][0], span(0, i, 512)) for i in range(12)],
        "z": [pack(w_in, span(O_Z, g, 512)) for g in range(4)],
        "x": [pack(w_in, span(O_XBC, g, 512)) for g in range(4)],
        "bc": [pack(w_in, span(o_b, g, P), span(o_c, g, P)) for g in range(4)],
        "wso": [pack(x["w_ssm_out"][0], c) for c in n256],
        "gs": [pack(w_in, span(O_GS, i, 256)) for i in range(4)],
        "kv": [pack(w_in, span(O_KC, i, 384)) for i in range(2)],
        "cw1": [pack(x["cmp_w1_k"][0]), pack(x["cmp_w1_v"][0])],
        "q": [pack(w_in, span(O_Q, j, P), span(O_Q, 4 + j, P)) for j in range(4)],
        "nga": [np.concatenate([pack(x["w_nsa_out"][0], c), pack(w_in, span(O_GA, i, 256))], axis=1)
                for i, c in enumerate(n256)],
        "wo": [pack(x["w_o"][0], c) for c in n256],
        "egu": [pack(np.concatenate([wg[e], wu[e]], axis=1)) for e in range(NE)],
        "edn": [pack(wd[e]) for e in range(NE)],
        "ada2": [pack(ada2[i // 12], span(0, i % 12, 512)) for i in range(24)],
        "gqa": [pack(g_in, span(0, g, 256), span(1024, g, 64), span(1024, g, 64), span(1280, g, 64)) for g in range(4)],
        "gqao": [pack(x["gqa_w_out_2"][0], c) for c in n256],
        "up": [pack(up[i // FB], span(0, i % FB, P), span(FFN, i % FB, P)) for i in range(2 * FB)],
        "down": [pack(down[i // 8], span(0, i % 8, P)) for i in range(16)],
        "mla": [pack(mla_in, (0, 384)), np.concatenate([pack(mla_in, (384, 672)), wide], axis=1)],
        "mlah": [np.concatenate([pack(u_q, span(0, j, 192)), pack(u_kv, span(0, j, 256))], axis=1) for j in range(8)],
        "mlao": [pack(x["mla_w_out_2"][0], c) for c in n256],
    }
    arrays = {name: np.concatenate(c, axis=0) for name, c in chunks.items()}
    for name, (m, w) in STREAMS.items():
        assert arrays[name].shape == (m * P, w), (name, arrays[name].shape)
    arrays["consts"] = constants()
    arrays["iota"] = rows(np.arange(NPOS, dtype=np.float32))
    arrays["vecs"] = np.concatenate([np.reshape(vec[name], (-1, P)) for name, _ in VECS], axis=0)
    arrays["xt"] = pack(x["x"][0].T)
    arrays["ctxt"] = pack(x["ctx_2"][0].T)
    arrays["positions"] = rows(x["positions"][0])
    arrays["ssm_rows"] = rows(np.concatenate([x["dt_bias"][0], x["a_log"][0]]))
    arrays["route_rows"] = rows(np.concatenate([x["b_router_group"][0], x["b_router_expert"][0]]))
    arrays["w_small"] = pack(w_in, (O_DT, O_DT + HEADS), (O_GN, O_GN + 3 * NH))
    arrays["w_route"] = pack(np.concatenate([x["w_router_group"][0], x["w_router_expert"][0]], axis=1))
    arrays["w_cmp2"] = pack(np.concatenate([x["cmp_w2_k"][0], x["cmp_w2_k"][0], x["cmp_w2_v"][0]], axis=1))

    nc = bacc.Bacc("TRN2", target_bir_lowering=False, num_devices=1)
    sent, dr = {}, {}
    for name, a in arrays.items():
        sent[f"in_{name}"] = np.ascontiguousarray(a)
        dr[name] = nc.dram_tensor(f"in_{name}", a.shape, mybir.dt.from_np(a.dtype), kind="ExternalInput").ap()
    dr["out"] = nc.dram_tensor("out", (P, KD * T), F32, kind="ExternalOutput").ap()
    build(nc, dr)
    got = run(nc, [sent], core_ids=[0]).results[0]["out"]
    return np.ascontiguousarray(got.reshape(P, KD, T).transpose(2, 1, 0).reshape(1, T, D))
```

```python
import math
from contextlib import ExitStack


import numpy as np

import concourse.bass as bass
from concourse import mybir

F32 = mybir.dt.float32
I32 = mybir.dt.int32
ACT = mybir.ActivationFunctionType
ALU = mybir.AluOpType
AX = mybir.AxisListType
ds = bass.ds

P = 128
D = 1024
KD = D // P
T = 256
TT = T // P
T2 = 2 * T
EPS = 1e-6
NEG = -1e30

GRP, HPG, HD, ST, CONV = 4, 8, 64, 128, 4
HEADS = GRP * HPG
DIN = HEADS * HD
CONV_DIM = DIN + 2 * GRP * ST
NH, NKV, DH = 16, 2, 64
CMP, STRIDE, HID = 32, 16, 256
NCMP = (T - CMP) // STRIDE + 1
NG, EPG, FH = 4, 8, 256
NE = NG * EPG
TOPK = 2
NPOS = TOPK * T
PT = NPOS // P
ITEMS = -(-(NE + PT - 1) // 4) * 4
KVG = 4
QL, KVL, RD, ND = 384, 256, 32, 64
QK = ND + RD
FFN = 2816
FB = FFN // P

_sizes = (DIN, CONV_DIM, HEADS, NH * DH) + (NKV * DH,) * 6 + (3 * NH, D, D)
O_Z, O_XBC, O_DT, O_Q, O_KC, O_VC, O_KS, O_VS, O_KW, O_VW, O_GN, O_GS, O_GA = (
    sum(_sizes[:i]) for i in range(len(_sizes)))

SLOTW = 4096
NSLOT = 6

CONSTS = [("ident", P), ("ones", P), ("tri", P), ("trix", P), ("mneg", P), ("halves", P), ("pnsa", P),
          ("pgqa", P), ("dup0", P), ("dup1", P), ("pmla", QK), ("invf", 1), ("eps", 1), ("eps64", 1),
          ("gcos", T), ("gsin", T), ("mcos", T), ("msin", T), ("cneg", 2 * NCMP), ("c01", 2 * NCMP),
          ("rev4", NG), ("rev8", EPG), ("place", PT), ("tile_end", PT - 1), ("tile", PT - 1), ("code", PT), ("fold", 2)]
CO, _o = {}, 0
for _n, _w in CONSTS:
    CO[_n] = (_o, _w)
    _o += _w
CW = _o

VECS = [("c", 8), ("b_ada", 48), ("norm1_g", 8), ("conv_b", 24), ("norm2_g", 8), ("final_g", 8),
        ("ssm_norm_g", 16), ("conv_w", 96), ("d_skip", 16), ("cmp_pe_k", 16), ("cmp_pe_v", 16),
        ("c_2", 8), ("c_ctx_2", 8), ("ada_b_2", 96), ("norm1_g_2", 16), ("norm2_g_2", 16),
        ("ffn_conv_b_2", 88), ("final_norm_g_2", 8), ("ffn_conv_w_2", 264), ("mla_q_norm_g_2", 3),
        ("mla_kv_norm_g_2", 2), ("gqa_q_norm_g_2", 1), ("gqa_k_norm_g_2", 1)]
VO, _o = {}, 0
for _n, _r in VECS:
    VO[_n] = _o
    _o += _r
VR = _o
VT = -(-VR // P)

STREAMS = {
    "ada": (12, 4096), "z": (4, 4096), "x": (4, 4096), "bc": (4, 2048), "wso": (4, 4096), "gs": (4, 2048),
    "kv": (2, 3072), "cw1": (2, 4096), "q": (4, 2048), "nga": (4, 4096), "wo": (4, 2048),
    "egu": (NE, 4096), "edn": (NE, 2048),
    "ada2": (24, 4096), "gqav": (1, 2048), "gqa": (4, 3072), "gqao": (4, 2048), "up": (2 * FB, 2048), "down": (16, FB * P),
    "mla": (2, 3072), "mlah": (8, 1088), "mlao": (4, 2048),
}


TWO_PI = (6.28125, 0.0019350051879882812,
          2 * math.pi - 6.28125 - 0.0019350051879882812)
PI_BELOW = 3.1415925
NSA_QUERIES, MOE_PHASE, GQA_QUERIES, MLA_LOW_RANK, MLA_QUERIES, LAST_PHASE = 4, 8, 11, 13, 14, 16
SETUP_DMAS, REST_DMAS = 1 + VT + 2, 6


class Unit:

    def __init__(self, scores=None, values=None, tiles=(), branches=1, w=0, gate=None):
        self.scores, self.values, self.tiles = scores, values, tiles
        self.branches, self.w, self.gate = branches, w, gate


def pack(w, *cols):
    w = np.concatenate([w[:, a:b] for a, b in cols], axis=1) if cols else w
    k, n = w.shape
    return w.reshape(k // P, P, n).transpose(1, 0, 2).reshape(P, -1)


def constants():
    c = np.zeros((P, CW), np.float32)

    def put(name, a):
        o, w = CO[name]
        c[:a.shape[0], o:o + w] = a

    i, j = np.arange(P)[:, None], np.arange(P)[None, :]
    put("ident", i == j)
    put("ones", np.ones((P, P)))
    put("tri", i <= j)
    put("trix", i < j)
    put("mneg", np.where(i <= j, 0.0, NEG))
    put("halves", i // 64 == j // 64)

    def rot(n, quarter):
        m = np.zeros((n, n))
        for o in range(n):
            b = o // quarter
            src, sign = (o + quarter, -1.0) if b % 2 == 0 else (o - quarter, 1.0)
            m[src, o] = sign
        return m

    put("pnsa", rot(P, 32))
    put("pgqa", rot(P, 16))
    m = np.zeros((QK, QK))
    m[ND:, ND:] = rot(RD, RD // 4)
    put("pmla", m)
    put("dup0", i == j % 64)
    put("dup1", i == 64 + j % 64)
    f = np.float32(10000.0) ** (-np.arange(0, DH, 2, dtype=np.float32) / np.float32(DH))
    put("invf", f[np.arange(P) % 32][:, None])
    put("eps", np.full((P, 1), EPS))
    put("eps64", np.full((P, 1), 64 * EPS))

    def axial(dim):
        t = np.arange(T)
        half = dim // 2
        inv = np.float32(10000.0) ** (-np.arange(0, half, 2, dtype=np.float32) / np.float32(half))
        ar = (t // 64).astype(np.float32)[:, None] * inv
        ac = (t % 64).astype(np.float32)[:, None] * inv
        a = np.concatenate([ar, ar, ac, ac], axis=1).T
        return np.cos(a), np.sin(a)

    gc, gs = axial(64)
    put("gcos", np.concatenate([gc, gc]))
    put("gsin", np.concatenate([gs, gs]))
    mc, ms = axial(RD)
    put("mcos", np.concatenate([np.ones((ND, T)), mc]))
    put("msin", np.concatenate([np.zeros((ND, T)), ms]))
    t = np.arange(P)[:, None, None] + P * np.arange(2)[None, :, None]
    ok = STRIDE * np.arange(NCMP)[None, None, :] + CMP - 1 <= t
    put("c01", ok.reshape(P, -1))
    put("cneg", np.where(ok, 0.0, NEG).reshape(P, -1))
    put("place", i + P * np.arange(PT)[None, :])
    put("tile_end", np.broadcast_to(P * np.arange(1, PT), (P, PT - 1)))
    put("tile", np.broadcast_to(np.arange(PT - 1), (P, PT - 1)))
    put("fold", i % 32 == np.arange(2)[None, :])
    put("code", np.broadcast_to(2 * NE * np.arange(PT) - 1, (P, PT)))
    put("rev4", np.broadcast_to(NG - np.arange(NG), (P, NG)))
    put("rev8", np.broadcast_to(EPG - np.arange(EPG), (P, EPG)))
    return c


def build(nc, dr):
    with ExitStack() as ctx:
        def sb(name, shape, dt=F32):
            return ctx.enter_context(nc.sbuf_tensor(name, shape, dt))

        def sem(name):
            return ctx.enter_context(nc.semaphore(name))

        bank = [ctx.enter_context(nc.psum_tensor(f"bank{i}", [P, 512], F32)) for i in range(8)]

        consts = sb("consts", [P, CW])
        cols = sb("cols", [P, VR])
        resid = sb("resid", [P, KD, T2])
        hn = sb("hn", [P, KD, T2])
        ring = sb("ring", [P, NSLOT * SLOTW])
        w_small = sb("w_small", [P, KD, HEADS + 3 * NH])
        w_route = sb("w_route", [P, KD, NG + NE])
        w_cmp2 = sb("w_cmp2", [P, 2, 192])
        rows32 = sb("rows32", [P, 3 * HEADS + NG + NE])
        ncos = sb("ncos", [P, T])
        nsin = sb("nsin", [P, T])
        ada = [sb(f"ada{i}", [P, 48, 2]) for i in range(3)]
        mod = [sb(f"mod{i}", [P, 2, 2, KD]) for i in range(3)]
        csil = sb("csil", [P, 2, KD, 32])
        ckv_rstd = sb("ckv_rstd", [P, 512])
        rstd = sb("rstd", [P, 512])
        arena = sb("arena", [P, 12288])

        def C(name, rows=P):
            o, w = CO[name]
            return consts[0:rows, o:o + w]

        def col(name, i=0):
            return cols[:, VO[name] + i:VO[name] + i + 1] if isinstance(i, int) else cols[:, ds(i + VO[name], 1)]

        def slot(s, w=SLOTW):
            return ring[:, s * SLOTW:s * SLOTW + w]

        def w_down(q):
            return ring[:, 2 * SLOTW + q * SLOTW // 2:2 * SLOTW + (q + 1) * SLOTW // 2]

        class Place:

            def __init__(self, buf, at=0):
                self.buf, self.at = buf, at

            def __call__(self, *shape):
                n = int(np.prod(shape))
                ap = self.buf[:, self.at:self.at + n]
                self.at += n
                assert self.at <= self.buf.shape[1]
                if len(shape) == 2:
                    ap = ap.rearrange("p (a b) -> p a b", a=shape[0])
                if len(shape) == 3:
                    ap = ap.rearrange("p (a b c) -> p a b c", a=shape[0], b=shape[1])
                return ap

        ident, ones = C("ident"), C("ones")

        setup_landed = sem("setup_landed")
        rest_landed = sem("rest_landed")
        slot_landed = [sem(f"slot{i}_landed") for i in range(NSLOT)]
        slot_free = [sem(f"slot{i}_free") for i in range(NSLOT)]
        gu_landed = [sem(f"gate_up{i}_landed") for i in range(2)]
        dn_landed = [sem(f"down{i}_landed") for i in range(4)]
        phase = sem("phase_ended")
        names = """
            vec_turned vec_ready csil_zeroed csil_ready ada_mm ada_rows ada_cols ada_ready
            sq_ready ss_ready std_ready hn_scaled hn_ready rope_reduced rope_sin
            dt_pe dt_dve dt_act group_done gsm_ready
            ssm_z ssm_zs ssm_x ssm_acc ssm_taps ssm_conv ssm_tok ssm_bcb ssm_xw ssm_E ssm_Ex ssm_state ssm_stT ssm_seg
            ssm_exp ssm_M ssm_yd ssm_yoff ssm_yo ssm_y ssm_sq ssm_ss ssm_std
            out_mm out_sig out_ev gemm_mm gemm_ev
            kv_mm kv_raw kv_rot kv_roped kv_dup kv_ready gates_ready hid_mm hid_silu cmp_mm cmp_ready
            q_mm q_raw q_rot q_roped q_sq q_ss q_std q_normed q_set v_set q_unset v_unset v_mm v_ready
            cs_mm cs_max cs_exp cs_ready ct_mm ct_ev
            att_S att_max att_exp att_scaled att_T att_PT att_O att_ev
            route_pe route_dve route_act tok_mm tok_ev
            moe_iota moe_zeroed moe_G moe_X moe_Xev moe_St moe_Stev moe_xt moe_h moe_silu moe_he moe_hT moe_hTev
            moe_y moe_yacc moe_sc
            ffn_mm ffn_acc ffn_taps ffn_silu ffn_ev stored""".split()
        s = {n: sem(n) for n in names}

        def counts():
            return dict.fromkeys(names, 0)

        spare = ring[:, 4 * SLOTW:6 * SLOTW]
        row_buf = spare[:, 2 * SLOTW - 3 * 512:].rearrange("p (a n) -> p a n", a=3)
        pl = Place(arena)
        vec_rows = pl(VT, P)
        pos_i, pos_f, ang, turns, tmp_rope = pl(T), pl(T), pl(T), pl(T), pl(T)
        pl = Place(arena)
        gates = pl(2, 3 * NH)
        ncos8, nsin8 = pl(T), pl(T)
        merged = pl(KD, T)
        after_merged = pl.at
        dt_in, dt_a, dt_b, dt_c, dt_d = (pl(2, HEADS) for _ in range(5))
        ssm_small = pl(4 * 2, HEADS)
        gsm = pl(4 * 2, HPG)
        a_neg = pl(HEADS)
        ynorm = pl(DIN // P, T)
        zs = pl(4, T)
        conv = pl(6, T)
        xdt = pl(2, 512)
        yssm = pl(4, T)
        pl = Place(spare)
        xw, bcb, state_t, e_bc, yoff = pl(512), pl(3 * P), pl(512), pl(512), pl(4, P)
        b_tok, cb = bcb[:, 0:P], bcb[:, P:3 * P].rearrange("p (c t) -> p c t", c=2)
        acc = pl(6, T)
        mexp = pl(2, 512)
        ysq = pl(4 * T)
        rs_ssm = pl(T)
        dt_wide = pl(512)
        pl = Place(arena, 10752)
        out_sig = pl(4, T)
        out_tmp = pl(2, T)
        pl = Place(arena, after_merged)
        ct = pl(4, 8 * P)
        pl = Place(arena, after_merged)
        k_raw, k_roped, k_tmp = pl(3, T), pl(3, T), pl(3, T)
        vc_raw = pl(T)
        blk = [pl(16, 2 * NCMP) for _ in range(2)]
        hid = pl(4, 2 * NCMP)
        pl = Place(arena, after_merged + 4 * 8 * P)
        v_tok = pl(2, 2, P)
        kk = [pl(2, T) for _ in range(NKV)]
        k_cmp = pl(2 * NCMP)
        v_cmp = pl(2, DH)
        o_t = pl(KD, T)
        gsel = pl(4, 3 * 8)
        cs, cs_m, cs_s = pl(4, 2 * NCMP), pl(8), pl(8)
        assert pl.at <= 10752
        pl = Place(spare)
        q_raw, q_t, q_tmp = pl(2, T), pl(2, T), pl(2, T)
        pl = Place(spare, 3640)
        q_all = pl(KD, T)
        nsa_ct = [pl(4 * P) for _ in range(2)]
        pl = Place(spare)
        probs = [pl(512) for _ in range(4)]
        probs_t = [pl(512) for _ in range(2)]
        nmax, psum_, pfac = pl(4, 2), pl(4, 2), pl(4, 2)
        nsa_q = [pl(T) for _ in range(2)]
        assert pl.at <= 2 * SLOTW - 3 * 512
        pl = Place(arena)
        h_tok = pl(2, D)
        xs = pl(KD, NPOS)
        ys = pl(PT, D)
        x_t = [pl(KD, P) for _ in range(2)]
        pl = Place(spare)
        iota = pl(NPOS)
        lg = pl(2, NG + NE)
        t2a, t2b, t2c, t2d, t2f, pos_a, pos_b = (pl(2, 1) for _ in range(7))
        g4a, g4b, g4c = (pl(2, NG) for _ in range(3))
        e8a, e8b, e8c, e8d, e8e = (pl(2, EPG) for _ in range(5))
        e32 = pl(2, NG, EPG)
        sel_a, sel_b, selm, pos = (pl(2, NE) for _ in range(4))
        cnt_col = pl(1)
        start = pl(NE)
        at_end, ends = pl(PT - 1, NE), pl(PT - 1)
        before_place, code_place = pl(PT, NE), pl(PT)
        tile_f3, tile_f, expert_f, code_item, mask = pl(PT - 1, ITEMS), pl(ITEMS), pl(ITEMS), pl(ITEMS), pl(ITEMS)
        tile_i, expert_i = pl(ITEMS), pl(ITEMS)
        pick, wpick, wpick_b = pl(2, NPOS), pl(2, NPOS), pl(NPOS)
        s_t = pl(PT, T)
        hsil, he, he_t = pl(2, FH), pl(2, FH), pl(2, FH)
        assert pl.at <= 2 * SLOTW
        pl = Place(arena)
        o2 = pl(KD, T2)
        o2x = arena[:, 0:KD * T].rearrange("p (k t) -> p k t", k=KD)
        gqa_all = pl(KD, T2)
        gka = pl(KVG, T2)
        gva = pl(4, KVG * DH)
        gq_cos, gq_sin = pl(T), pl(T)
        pl = Place(arena)
        gq_sq, gq_std = pl(3, 512), pl(3, 512)
        pl = Place(spare, 3200)
        gqa_q = [pl(512) for _ in range(2)]
        gqa_k = [pl(512) for _ in range(2)]
        gqa_v = [pl(4, DH) for _ in range(2)]
        assert pl.at <= 2 * SLOTW - 3 * 512
        pl = Place(arena, KD * T)
        mqa = pl(2 * KD, T)
        cqn = pl(3, T)
        ckvn = pl(2, T2)
        mka = [hn, pl(KD, T2)]
        pl = Place(ring[:, SLOTW:2 * SLOTW])
        mva = pl(4, 2 * KD * ND)
        pl = Place(spare, 3200)
        mla_q = [pl(2, T) for _ in range(2)]
        mla_v = [pl(4, P) for _ in range(2)]
        kr_raw, kr_roped = pl(512), pl(512)
        qcos, qsin = pl(T), pl(T)
        assert pl.at <= 2 * SLOTW
        pl = Place(spare)
        mq_raw = [pl(2, T) for _ in range(2)]
        mq_t, mq_tmp = pl(2, T), pl(2, T)
        cq_sq, ckv_sq = Place(spare)(3, T), Place(spare, 3 * T)(2, T2)
        act = Place(arena)(FB, T2)
        ffn_acc = Place(spare)(4, T2)

        def gqa_block(b, g):
            block = gqa_all[:, ds(g * 2 + b, 1), :] if b < 2 else gka[:, ds(g, 1), :]
            return block.rearrange("p a t -> p (a t)")

        def mla_keys(rows, trip, q, hh):
            return mka[q][rows, ds(trip * 2 + hh, 1), :].rearrange("p a t -> p (a t)")

        def since(i, first):
            return not isinstance(i, int) or i >= first

        def upto(i, end):
            return not isinstance(i, int) or i < end

        block = ctx.enter_context(nc.Block())

        @block.sync
        def _(sp):
            used = [0] * NSLOT

            def stream(trips, plan):
                per = {sl: sum(e[1] == sl for e in plan) for _, sl, _ in plan}

                def body(i):
                    for x, (name, sl, chunk) in enumerate(plan):
                        before = sum(e[1] == sl for e in plan[:x])
                        sp.wait_ge(slot_free[sl], i * per[sl] + (used[sl] + before + 1))
                        sp.dma_start(slot(sl, STREAMS[name][1]), dr[name][bass.ts(chunk(i), P), :]) \
                            .then_inc(slot_landed[sl], 16)
                if trips > 1:
                    with sp.Fori(0, trips) as i:
                        body(i)
                else:
                    body(0)
                for _, sl, _ in plan:
                    used[sl] += trips

            sp.dma_start(consts[:, :], dr["consts"]).then_inc(setup_landed, 16)
            for v in range(VT):
                r = min(P, VR - v * P)
                sp.dma_start(vec_rows[0:r, v, :], dr["vecs"][v * P:v * P + r, :]).then_inc(setup_landed, 16)
            sp.dma_start(pos_i.bitcast(I32), dr["positions"]).then_inc(setup_landed, 16)
            sp.dma_start(resid[:, :, 0:T], dr["xt"].rearrange("p (k t) -> p k t", k=KD)).then_inc(setup_landed, 16)

            def c4(q):
                return lambda i: i * 4 + q

            def c2(q):
                return lambda i: i * 2 + q

            def c1(i):
                return i

            def at(n):
                return lambda i: n + i

            def ada2(first):
                return [("ada2", 1 + q, (lambda q: lambda i: i * 3 + (first + q))(q)) for q in range(3)]

            stream(1, [("ada", q, at(q)) for q in range(4)])
            sp.dma_start(rows32[:, 0:2 * HEADS], dr["ssm_rows"]).then_inc(rest_landed, 16)
            sp.dma_start(rows32[:, 3 * HEADS:], dr["route_rows"]).then_inc(rest_landed, 16)
            sp.dma_start(w_small[:, :, :], dr["w_small"].rearrange("p (k n) -> p k n", k=KD)).then_inc(rest_landed, 16)
            sp.dma_start(w_route[:, :, :], dr["w_route"].rearrange("p (k n) -> p k n", k=KD)).then_inc(rest_landed, 16)
            sp.dma_start(w_cmp2[:, :, :], dr["w_cmp2"].rearrange("p (k n) -> p k n", k=2)).then_inc(rest_landed, 16)
            sp.dma_start(resid[:, :, T:T2], dr["ctxt"].rearrange("p (k t) -> p k t", k=KD)).then_inc(rest_landed, 16)
            stream(1, [("x", 1, at(0)), ("bc", 2, at(0))])
            stream(GRP - 1, [("x", 1, at(1)), ("bc", 2, at(1)), ("z", 0, c1)])
            stream(1, [("z", 0, at(GRP - 1))])
            stream(1, [("ada", 1, at(4)), ("wso", 2, at(0)), ("gs", 3, at(0)), ("wso", 0, at(1)), ("ada", 4, at(5)),
                       ("gs", 5, at(1)), ("ada", 1, at(6)), ("ada", 4, at(7)), ("wso", 2, at(2)), ("gs", 3, at(2)),
                       ("ada", 1, at(8)), ("ada", 4, at(9)), ("wso", 0, at(3)), ("gs", 5, at(3)), ("ada", 1, at(10)),
                       ("ada", 4, at(11))])
            stream(1, [("kv", 2, at(0)), ("kv", 3, at(1)), ("cw1", 1, at(0)), ("cw1", 0, at(1))])
            stream(4, [("q", 2, c1), ("ada2", 3, c1)])
            stream(1, [("nga", 1, at(0)), ("nga", 2, at(1)), ("ada2", 0, at(4)), ("ada2", 3, at(5)), ("ada2", 0, at(6)),
                       ("ada2", 3, at(7)), ("nga", 1, at(2)), ("ada2", 0, at(8)), ("ada2", 3, at(9)), ("nga", 2, at(3)),
                       ("ada2", 0, at(10)), ("ada2", 3, at(11))])
            stream(2, [("wo", 3, c2(0)), ("wo", 0, c2(1))])

            for sl in range(4):
                sp.wait_ge(slot_free[sl], used[sl] + 1)
            sp.wait_ge(phase, 3 * (MOE_PHASE - 1))
            sp.dma_start(iota, dr["iota"]).then_inc(s["moe_iota"], 16)
            sp.wait_ge(s["route_dve"], 5)

            def load_item(i, q, first):
                e = sp.value_load(expert_i.bitcast(I32)[0:1, ds(i, 1)], min_val=0, max_val=NE - 1)
                if not first or q >= 2:
                    sp.wait_ge(s["moe_h"], i - 1)
                sp.dma_start(slot(q % 2), dr["egu"][bass.ts(e, P), :]).then_inc(gu_landed[q % 2], 16)
                if not first:
                    sp.wait_ge(s["moe_y"], i - 3)
                sp.dma_start(w_down(q), dr["edn"][bass.ts(e, P), :]).then_inc(dn_landed[q], 16)

            for q in range(4):
                load_item(q, q, True)
            with sp.Fori(0, ITEMS // 4 - 1) as i:
                for q in range(4):
                    load_item(i * 4 + (q + 4), q, False)
            sp.wait_ge(phase, 3 * MOE_PHASE)

            def up_stream(l):
                def load(j, q):
                    sp.dma_start(slot(2 + q, STREAMS["up"][1]), dr["up"][bass.ts(j, P), :]).then_inc(slot_landed[2 + q], 16)

                for q in range(2):
                    sp.wait_ge(slot_free[2 + q], used[2 + q] + 1)
                    load(FB * l + q, q)
                with sp.Fori(1, FB // 2) as i:
                    for q in range(2):
                        sp.wait_ge(s["ffn_mm"], i * 4 + (2 * FB * l + 2 * q - 2))
                        load(i * 2 + (FB * l + q), q)
                for q in range(2):
                    used[2 + q] += 1

            for l in range(2):
                if l == 0:
                    stream(1, [("gqav", 1, c1)])
                    stream(4, [("gqa", 0, c1)] + ada2(12))
                    stream(2, [("gqao", 1, c2(0)), ("gqao", 2, c2(1))])
                else:
                    stream(1, [("mla", 0, at(0)), ("mla", 1, at(1))])
                    stream(4, [("mlah", 2, c2(0)), ("mlah", 3, c2(1))])
                    stream(2, [("mlao", 0, c2(0)), ("mlao", 2, c2(1))])
                up_stream(l)
                stream(2, [("down", q, (lambda q: lambda i: i * 4 + q + 8 * l)(q)) for q in range(4)])

            sp.wait_ge(phase, 3 * LAST_PHASE)
            sp.dma_start(dr["out"].rearrange("p (k t) -> p k t", k=KD), resid[:, :, 0:T]).then_inc(s["stored"], 16)
            sp.wait_ge(s["stored"], 16)

        @block.tensor
        def _(pe):
            used = [0] * NSLOT
            n = counts()
            ended = [0]
            mm, tr = nc.tensor.matmul, nc.tensor.transpose
            for sl in range(4):
                pe.sem_inc(slot_free[sl], 1)

            def end_phase():
                pe.drain().then_inc(phase, 1)
                ended[0] += 1
                pe.wait_ge(phase, 3 * ended[0])

            def landed(sl, i=0):
                pe.wait_ge(slot_landed[sl], (i + used[sl] + 1) * 16)

            def free(*slots):
                for sl in slots:
                    pe.drain().then_inc(slot_free[sl], 1)

            def taken(trips, *slots):
                for sl in slots:
                    used[sl] += trips

            def dot(out, lhs, rhs, k):
                for i in range(k):
                    last = mm(out, lhs(i), rhs(i), start=i == 0, stop=i == k - 1)
                return last

            def ada_rows(b, sl, count, which):
                pe.wait_ge(slot_landed[sl], count * 16)
                for k in range(KD):
                    o = 32 * (k % 4)
                    last = mm(bank[b][o:o + 32, :], csil[:, which, k, :], slot(sl)[:, k * 512:(k + 1) * 512],
                              start=k < 4, stop=k >= 4)
                last.then_inc(s["ada_mm"], 1)
                free(sl)

            def ada_cols(out, c, buf, ncol):
                pe.wait_ge(s["ada_rows"], c + 1)
                for x in range(4):
                    last = mm(out[:, 2 * x:2 * x + ncol], row_buf[:, buf, x * P:(x + 1) * P], C("fold")[:, 0:ncol],
                              start=True, stop=True)
                last.then_inc(s["ada_cols"], 1)

            def sums(w):
                for k in range(KD):
                    pe.wait_ge(s["sq_ready"], n["sq_ready"] + k + 1)
                    last = mm(bank[7][:, 0:w], ones, hn[:, k, 0:w], start=k == 0, stop=k == KD - 1)
                last.then_inc(s["ss_ready"], 1)
                n["sq_ready"] += KD

            def norm(w):
                sums(w)
                n["hn_ready"] += KD

            def normed():
                pe.wait_ge(s["hn_ready"], n["hn_ready"])

            def hn_block(k):
                pe.wait_ge(s["hn_ready"], n["hn_ready"] - KD + k + 1)
                return hn[:, k, :]

            def gemm(trips, slots, per, kb, rhs, w):
                q4 = len(slots) * per
                with pe.Fori(0, trips) as i:
                    for c, sl in enumerate(slots):
                        landed(sl, i)
                        for b in range(per):
                            m = c * per + b
                            pe.wait_ge(s["gemm_ev"], i * q4 + (n["gemm_mm"] + m + 1))
                            last = dot(bank[m % 4][:, 0:w],
                                       lambda k: slot(sl)[:, (k * per + b) * P:(k * per + b + 1) * P],
                                       lambda k: rhs(k), kb)
                            last.then_inc(s["gemm_mm"], 1)
                        free(sl)
                taken(trips, *slots)
                n["gemm_mm"] += trips * q4

            def gated_out(pairs, kb, rhs, gate_at, ada_slots, which, chunk, ready):
                with pe.Fori(0, 2) as i:
                    for c, (sl, gsl) in enumerate(pairs):
                        landed(sl, i)
                        if gsl != sl:
                            landed(gsl, i)
                        for b in range(2):
                            m = c * 2 + b
                            x = ada_slots[m]
                            ada_rows(4 + m % 2, x, i * ada_slots.count(x) + (used[x] + ada_slots[:m].count(x) + 1), which)
                            pe.wait_ge(s["out_ev"], i * 4 + (n["out_mm"] + m + 1))
                            dot(bank[m][:, 0:T], lambda k: slot(sl)[:, (k * 2 + b) * P:(k * 2 + b + 1) * P], rhs, kb)
                            last = dot(bank[m][:, T:T2],
                                       lambda k: slot(gsl)[:, gate_at + (k * 2 + b) * P:gate_at + (k * 2 + b + 1) * P],
                                       lambda k: hn[:, k, 0:T], KD)
                            last.then_inc(s["out_mm"], 1)
                            if m == 0:
                                pe.wait_ge(s["ada_ready"], i + ready)
                            ada_cols(bank[6][:, 8 * m:8 * m + 8], i * 4 + (chunk + m), m % 3, 1 + which)
                        free(*sorted({sl, gsl}))
                for sl, gsl in pairs:
                    taken(2, *{sl, gsl})
                taken(2, *ada_slots)
                n["out_mm"] += 8

            def attention(units, trips, done, halves):
                U = len(units)

                def step(t, it):
                    n = it * U + t
                    if upto(it, trips):
                        if t % (U // 2) == 0:
                            pe.wait_ge(s["q_set"], it * 2 + (halves + 2 * t // U + 1))
                        if since(n, 4):
                            pe.wait_ge(s["att_exp"], n + (done - 3))
                        units[t].scores(it, bank[t % 4]).then_inc(s["att_S"], 1)
                    if since(n, 2) and upto(n - 2, trips * U):
                        pe.wait_ge(s["att_scaled"], n + (done - 1))
                        if since(n, 4):
                            pe.wait_ge(s["att_PT"], n + (done - 3))
                        for x, c in enumerate(units[t - 2].tiles):
                            last = tr(bank[4 + t % 2][:, x * P:(x + 1) * P], probs[(t - 2) % 4][:, c:c + P], ident)
                        last.then_inc(s["att_T"], 1)
                    if since(n, 3):
                        v, vit = (t - 3) % U, it if t >= 3 else it - 1
                        pe.wait_ge(s["att_PT"], n + (done - 2))
                        if v % (U // 2) == 0:
                            pe.wait_ge(s["v_set"], vit * 2 + (halves + 2 * v // U + 1))
                            if since(vit, 1):
                                pe.wait_ge(s["att_ev"], vit * 2 + (halves + 2 * v // U - 1))
                        units[v].values(vit, bank[6 + 2 * v // U], probs_t[v % 2]).then_inc(s["att_O"], 1)

                for t in range(U):
                    step(t, 0)
                with pe.Fori(1, trips) as it:
                    for t in range(U):
                        step(t, it)
                for t in range(3):
                    step(t, trips)
                pe.wait_ge(s["att_ev"], halves + 2 * trips)

            pe.wait_ge(setup_landed, 16 * SETUP_DMAS)
            for v in range(VT):
                r = min(P, VR - v * P)
                last = tr(bank[v][:, 0:r], vec_rows[0:r, v, :], ident[0:r, 0:r])
            last.then_inc(s["vec_turned"], 1)
            pe.wait_ge(s["csil_ready"], 1)
            norm(T)
            for q in range(4):
                ada_rows(q, q, 1, 0)
                if q >= 1:
                    ada_cols(bank[4][:, (q - 1) * 8:q * 8], q - 1, (q - 1) % 3, 1)
            ada_cols(bank[4][:, 24:32], 3, 0, 1)
            taken(1, 0, 1, 2, 3)

            pe.wait_ge(rest_landed, 16 * REST_DMAS)
            def hx(k):
                return hn[:, k, 0:T]

            xt = [conv[:, b, :] for b in range(4)]
            b_t, c_tt = conv[:, 4, :], conv[:, 5, :]
            dtag = [gsm[:, c, :] for c in range(2)]

            def project(b, sl, width, first):
                for x in range(2):
                    last = dot(bank[b][:, x * T:(x + 1) * T],
                               lambda k: slot(sl)[:, k * width + (first + x) * P:k * width + (first + x + 1) * P], hx, KD)
                return last

            def project_x(g, x):
                if x == 0:
                    landed(1, g)
                project(6 + x, 1, 512, 2 * x).then_inc(s["ssm_x"], 1)
                if x == 1:
                    free(1)

            def project_bc(g):
                landed(2, g)
                pe.wait_ge(s["ssm_taps"], g * 3 + 1)
                project(6, 2, T, 0).then_inc(s["ssm_x"], 1)
                free(2)

            def squares():
                dot(bank[7][:, 0:T], lambda b: ones, lambda b: ysq[:, b * T:(b + 1) * T], 4).then_inc(s["ssm_ss"], 1)

            def group(g, last_group):
                pe.wait_ge(s["ssm_conv"], g + 1)
                for c in range(2):
                    for b in range(4):
                        tr(bank[c][:, b * P:(b + 1) * P], xt[b][:, c * P:(c + 1) * P], ident)
                tr(bank[2][:, 0:P], b_t[:, 0:P], ident)
                for c in range(2):
                    last = mm(bank[2][:, (1 + c) * P:(2 + c) * P], b_t[:, c * P:(c + 1) * P], c_tt[:, c * P:(c + 1) * P],
                              start=True, stop=True)
                last.then_inc(s["ssm_tok"], 1)
                if since(g, 1):
                    pe.wait_ge(s["ssm_sq"], g)
                    squares()
                if not last_group:
                    project_x(g + 1, 0)
                pe.wait_ge(s["gsm_ready"], g + 1)
                for pr in range(4):
                    last = mm(bank[3][:, pr * P:(pr + 1) * P], dt_wide[:, pr * P:(pr + 1) * P], C("tri"),
                              start=True, stop=True)
                last.then_inc(s["ssm_E"], 1)

                def decays(u):
                    c, hh = u // 2, u % 2
                    if u >= 2:
                        pe.wait_ge(s["ssm_exp"], g * 4 + (u - 1))
                    mm(bank[4 + u % 2][:, :], ident, C("mneg").unsqueeze(1).to_broadcast([P, 4, P]), start=True, stop=False)
                    for h in range(4):
                        head = 4 * hh + h
                        last = mm(bank[4 + u % 2][:, h * P:(h + 1) * P], dtag[c][:, head:head + 1].to_broadcast([P, P]),
                                  C("tri"), start=False, stop=h == 3)
                    last.then_inc(s["ssm_seg"], 1)

                def within(u):
                    c, hh = u // 2, u % 2
                    pe.wait_ge(s["ssm_M"], g * 4 + (u + 1))
                    for h in range(4):
                        head = 4 * hh + h
                        o = (h // 2) * T + c * P
                        last = mm(bank[1 + hh][64 * (h % 2):64 * (h % 2) + 64, o:o + P],
                                  xdt[:, c, head * HD:(head + 1) * HD], mexp[:, u % 2, h * P:(h + 1) * P],
                                  start=True, stop=True)
                    last.then_inc(s["ssm_yd"], 1)

                decays(0)
                decays(1)
                pe.wait_ge(s["ssm_xw"], g + 1)
                pe.wait_ge(s["ssm_bcb"], g + 1)
                mm(bank[0][:, :], b_tok, xw, start=True, stop=True).then_inc(s["ssm_state"], 1)
                if not last_group:
                    if since(g, 1):
                        pe.wait_ge(s["ssm_std"], g)
                    project_x(g + 1, 1)
                within(0)
                decays(2)
                within(1)
                decays(3)
                pe.wait_ge(s["ssm_Ex"], g + 1)
                pe.wait_ge(s["ssm_stT"], g + 1)
                for pr in range(4):
                    last = mm(bank[3][:, pr * P:(pr + 1) * P], state_t[:, pr * P:(pr + 1) * P], c_tt[:, P:T],
                              start=True, stop=True)
                last.then_inc(s["ssm_yoff"], 1)
                if not last_group:
                    project_bc(g + 1)
                within(2)
                within(3)
                landed(0, g)
                if last_group:
                    pe.wait_ge(s["ssm_std"], g)
                else:
                    pe.wait_ge(s["ssm_taps"], g * 3 + 5)
                project(7, 0, 512, 0).then_inc(s["ssm_z"], 1)
                if not last_group:
                    pe.wait_ge(s["ssm_taps"], g * 3 + 6)
                project(6, 0, 512, 2).then_inc(s["ssm_z"], 1)
                free(0)

            for c in range(2):
                last = dot(bank[5][:, c * 80:(c + 1) * 80], lambda k: hn_block(k)[:, c * P:(c + 1) * P],
                           lambda k: w_small[:, k, :], KD)
            last.then_inc(s["dt_pe"], 1)
            for x in range(2):
                project_x(0, x)
            pe.wait_ge(s["dt_dve"], 3)
            for c in range(2):
                mm(bank[4][:, c * HEADS:(c + 1) * HEADS], C("tri"), ssm_small[:, c, :], start=True, stop=True)
            mm(bank[4][:, 2 * HEADS:3 * HEADS], ones, ssm_small[:, 0, :], start=True, stop=True).then_inc(s["dt_pe"], 1)
            project_bc(0)
            group(0, False)
            with pe.Fori(1, GRP - 1) as g:
                group(g, False)
            group(GRP - 1, True)
            taken(GRP, 0, 1, 2)
            pe.wait_ge(s["ssm_sq"], GRP)
            squares()
            end_phase()
            for sl in (4, 5):
                pe.sem_inc(slot_free[sl], 1)
            gated_out([(2, 3), (0, 5)], DIN // P, lambda k: ynorm[:, k, :], 0, (1, 4, 1, 4), 0, 4, 1)
            end_phase()

            def kvw(sl, x):
                return lambda k: slot(sl)[:, k * 384 + x * P:k * 384 + (x + 1) * P]

            landed(2)
            dot(bank[0][:, 0:T], kvw(2, 0), hx, KD)
            dot(bank[0][:, T:T2], kvw(2, 1), hx, KD)
            dot(bank[1][:, 0:T], kvw(2, 2), hx, KD)
            landed(3)
            dot(bank[1][:, T:T2], kvw(3, 1), hx, KD)
            for br in range(2):
                for t in range(TT):
                    last = dot(bank[2][:, (br * 2 + t) * P:(br * 2 + t + 1) * P], lambda k: hn[:, k, t * P:(t + 1) * P],
                               kvw(3, 2 * br), KD)
            last.then_inc(s["kv_mm"], 1)
            free(2, 3)
            pe.wait_ge(s["kv_raw"], 1)
            mm(bank[3][:, :], C("pnsa"), k_raw[:, 0:2, :], start=True, stop=True)
            mm(bank[4][:, 0:T], C("pnsa"), k_raw[:, 2, :], start=True, stop=True).then_inc(s["kv_rot"], 1)
            pe.wait_ge(s["kv_roped"], 1)
            for g in range(NKV):
                dup = C(f"dup{g}")
                mm(bank[5][:, g * T:(g + 1) * T], dup, k_roped[:, 0, :], start=True, stop=True)
                mm(bank[6][:, g * T:(g + 1) * T], dup, vc_raw, start=True, stop=True)
                last = mm(bank[g][:, :], dup, k_roped[:, 1:3, :], start=True, stop=True)
            last.then_inc(s["kv_dup"], 1)
            pe.wait_ge(s["kv_ready"], 1)
            for x in range(2):
                landed(1 - x)
                for hb in range(2):
                    o = (x * 2 + hb) * 2 * NCMP
                    last = dot(bank[7][:, o:o + 2 * NCMP],
                               lambda k: slot(1 - x)[:, k * HID + hb * P:k * HID + hb * P + P],
                               lambda k: blk[x][:, k, :], 16)
            last.then_inc(s["hid_mm"], 1)
            free(1, 0)
            taken(1, 0, 1, 2, 3)
            pe.wait_ge(s["hid_silu"], 1)
            dot(bank[4][:, 256:256 + 2 * NCMP], lambda k: w_cmp2[:, k, 0:P], lambda k: hid[:, k, :], 2)
            for g in range(NKV):
                last = dot(bank[4][0:NCMP, 320 + g * DH:320 + (g + 1) * DH],
                           lambda k: hid[:, 2 + k, g * NCMP:(g + 1) * NCMP], lambda k: w_cmp2[:, k, P:P + DH], 2)
            last.then_inc(s["cmp_mm"], 1)
            pe.wait_ge(s["cmp_ready"], 1)
            end_phase()
            def turn_cmp(j):
                pe.wait_ge(s["cs_ready"], j + 1)
                if since(j, 1):
                    pe.wait_ge(s["ct_ev"], j)
                for t in range(8):
                    last = tr(bank[4 + t // 4][0:NCMP, (t % 4) * P:(t % 4 + 1) * P],
                              cs[:, t // 2, (t % 2) * NCMP:(t % 2 + 1) * NCMP], ident)
                last.then_inc(s["ct_mm"], 1)

            def queries(j):
                landed(2, j)
                if since(j, 1):
                    pe.wait_ge(s["q_raw"], j)
                for u in range(2):
                    last = dot(bank[0][:, u * T:(u + 1) * T], lambda k: slot(2)[:, (2 * k + u) * P:(2 * k + u + 1) * P], hx, KD)
                last.then_inc(s["q_mm"], 1)
                free(2)
                ada_rows(6, 3, j + (used[3] + 1), 1)
                if since(j, 1):
                    turn_cmp(j - 1)
                pe.wait_ge(s["q_raw"], j + 1)
                mm(bank[1][:, :], C("pnsa"), q_raw, start=True, stop=True).then_inc(s["q_rot"], 1)
                ada_cols(bank[3][:, 256:264], j + 12, 0, 2)
                pe.wait_ge(s["q_roped"], j + 1)
                for t, (u, half, qt) in enumerate(order):
                    last = mm(bank[2 + half][:, (2 * u + qt) * NCMP:(2 * u + qt + 1) * NCMP],
                              q_t[64 * half:64 * half + 64, u, qt * P:(qt + 1) * P],
                              k_cmp[64 * half:64 * half + 64, u * NCMP:(u + 1) * NCMP], start=True, stop=True)
                last.then_inc(s["cs_mm"], 1)

            order = [(u, half, qt) for u in range(2) for half in range(2) for qt in range(2)]
            queries(0)
            with pe.Fori(1, 4) as j:
                queries(j)
            turn_cmp(3)
            taken(4, 2, 3)
            n["q_mm"] += 4
            end_phase()

            def unit(t):
                u, half, qt = order[t]
                w = P * (qt + 1)

                def scores(j, b):
                    rows = slice(64 * half, 64 * half + 64)
                    mm(b[:, 0:2 * w], nsa_q[u][rows, qt * P:(qt + 1) * P], kk[u][rows, :, 0:w], start=True, stop=False)
                    diag = b[:, 0:2 * w].rearrange("p (b k) -> p b k", b=2)[:, :, qt * P:w]
                    return mm(diag, C("mneg"), ident.unsqueeze(1).to_broadcast([P, 2, P]), start=False, stop=True)

                def values(j, b, pt):
                    out = b[64 * half:64 * half + 64, qt * P:(qt + 1) * P]
                    for x in range(2 * (qt + 1)):
                        br, kt = x // (qt + 1), x % (qt + 1)
                        mm(out, v_tok[:, br, kt, u * DH:(u + 1) * DH], pt[:, x * P:(x + 1) * P], start=x == 0, stop=False)
                    return mm(out, v_cmp[0:NCMP, u, :], nsa_ct[u][0:NCMP, (t % 4) * P:(t % 4 + 1) * P], start=False, stop=True)

                return Unit(scores=scores, values=values, tiles=[x * P for x in range(2 * (qt + 1))])

            attention([unit(t) for t in range(8)], 4, 0, 0)
            end_phase()
            gated_out([(1, 1), (2, 2)], KD, lambda k: o_t[:, k, :], 2048, (0, 3, 0, 3), 1, 16, 7)
            end_phase()
            gemm(2, (3, 0), 2, KD, lambda k: merged[:, k, :], T)
            norm(T)
            normed()
            end_phase()

            for t in range(TT):
                last = dot(bank[0][:, t * 36:(t + 1) * 36], lambda k: hn[:, k, t * P:(t + 1) * P],
                           lambda k: w_route[:, k, :], KD)
            last.then_inc(s["route_pe"], 1)
            for t in range(TT):
                for k in range(KD):
                    last = tr(bank[2 + 2 * t + k // 4][:, (k % 4) * P:(k % 4 + 1) * P], hn[:, k, t * P:(t + 1) * P], ident)
            last.then_inc(s["tok_mm"], 1)
            pe.wait_ge(s["route_dve"], 3)
            mm(bank[1][:, 0:NE], C("trix"), selm[:, 0, :], start=True, stop=True)
            mm(bank[1][:, NE:2 * NE], C("trix"), selm[:, 1, :], start=True, stop=False)
            mm(bank[1][:, NE:2 * NE], ones, selm[:, 0, :], start=False, stop=True)
            dot(bank[1][0:NE, 2 * NE:2 * NE + 1], lambda t: selm[:, t, :], lambda t: ones[:, 0:1], TT).then_inc(s["route_pe"], 1)
            pe.wait_ge(s["route_dve"], 4)
            mm(bank[0][:, 0:NE], cnt_col[0:NE].to_broadcast([NE, P]), C("trix", NE)[:, 0:NE], start=True, stop=True) \
                .then_inc(s["route_pe"], 1)
            pe.wait_ge(s["moe_G"], 1)
            pe.wait_ge(s["tok_ev"], 1)
            for k in range(KD):
                if k >= 4:
                    pe.wait_ge(s["moe_Xev"], k - 3)
                dot(bank[2 + k % 4][:, :], lambda t: h_tok[:, t, k * P:(k + 1) * P], lambda t: pick[:, t, :], TT) \
                    .then_inc(s["moe_X"], 1)
            pe.wait_ge(s["moe_Xev"], KD)

            def turn_weights():
                pe.wait_ge(s["moe_G"], 2)
                for j in range(PT):
                    for t in range(TT):
                        last = tr(bank[6 + j // 2][:, (j % 2) * T + t * P:(j % 2) * T + (t + 1) * P],
                                  wpick[:, t, j * P:(j + 1) * P], ident)
                last.then_inc(s["moe_St"], 1)

            def step(i, q, trip):
                if upto(i, ITEMS):
                    pe.wait_ge(s["moe_xt"], i + 1)
                    pe.wait_ge(gu_landed[q % 2], trip * 32 + 16 * (q // 2 + 1))
                    if since(i, 2):
                        pe.wait_ge(s["moe_he"], i - 1)
                    dot(bank[q % 2][:, :], lambda k: x_t[q % 2][:, k, :], lambda k: slot(q % 2)[:, k * 512:(k + 1) * 512], KD) \
                        .then_inc(s["moe_h"], 1)
                if since(i, 1) and upto(i, ITEMS + 1):
                    x = (q + 1) % 2
                    pe.wait_ge(s["moe_he"], i)
                    for b in range(2):
                        last = tr(bank[2 + x][:, b * P:(b + 1) * P], he[:, x, b * P:(b + 1) * P], ident)
                    last.then_inc(s["moe_hT"], 1)
                if since(i, 2):
                    d = (q + 2) % 4
                    pe.wait_ge(s["moe_hTev"], i - 1)
                    pe.wait_ge(dn_landed[d], trip * 16 + (0 if q < 2 else 16))
                    if since(i, 4):
                        pe.wait_ge(s["moe_yacc"], i - 3)
                    for half in range(2):
                        last = dot(bank[4 + 2 * (q % 2) + half][:, :], lambda k: he_t[:, q % 2, k * P:(k + 1) * P],
                                   lambda k: w_down(d)[:, k * D + half * 512:k * D + half * 512 + 512], 2)
                    last.then_inc(s["moe_y"], 1)

            step(0, 0, 0)
            turn_weights()
            for q in range(1, 4):
                if q == 3:
                    pe.wait_ge(s["moe_Stev"], 1)
                step(q, q, 0)
            with pe.Fori(1, ITEMS // 4) as trip:
                for q in range(4):
                    step(trip * 4 + q, q, trip)
            for q in range(2):
                step(ITEMS + q, q, ITEMS // 4)
            pe.wait_ge(s["moe_yacc"], ITEMS)
            for m in range(KD):
                last = dot(bank[m // 2][:, (m % 2) * T:(m % 2 + 1) * T], lambda j: ys[:, j, m * P:(m + 1) * P],
                           lambda j: s_t[:, j, :], PT)
            end_phase()
            assert ended[0] == MOE_PHASE
            end_phase()
            norm(T)
            normed()
            end_phase()

            for l in range(2):
                norm(T2)
                if l == 0:
                    landed(1)
                    for t in range(4):
                        last = dot(bank[6 + t // 2][:, (t % 2) * T:(t % 2 + 1) * T], lambda k: hn_block(k)[:, t * P:(t + 1) * P],
                                   lambda k: slot(1)[:, k * T:(k + 1) * T], KD)
                    last.then_inc(s["v_mm"], 1)
                    free(1)
                    taken(1, 1)

                    def block_step(b, g):
                        c = g * 3 + b
                        if upto(g, KVG):
                            if b == 0:
                                landed(0, g)
                            if since(c, 3):
                                pe.wait_ge(s["q_normed"], c - 2)
                            dot(bank[b][:, :], lambda k: slot(0)[:, k * 384 + b * P:k * 384 + (b + 1) * P],
                                lambda k: hn[:, k, :], KD).then_inc(s["q_mm"], 1)
                            if b == 2:
                                free(0)
                        if since(c, 1) and upto(c - 1, 3 * KVG):
                            pe.wait_ge(s["q_sq"], c)
                            if since(c, 2):
                                pe.wait_ge(s["q_std"], c - 1)
                            mm(bank[3][:, :], C("halves"), gq_sq[:, (b - 1) % 3, :], start=True, stop=True).then_inc(s["q_ss"], 1)
                        if since(c, 2):
                            x, xg = (b - 2) % 3, g if b == 2 else g - 1
                            pe.wait_ge(s["q_normed"], c - 1)
                            if since(c, 3):
                                pe.wait_ge(s["q_roped"], c + (4 - 2))
                            mm(bank[4][:, 0:T], C("pgqa"), gqa_block(x, xg)[:, 0:T], start=True, stop=True).then_inc(s["q_rot"], 1)
                        if b == 0 and since(g, 1):
                            if since(g, 2):
                                pe.wait_ge(s["ada_ready"], g + 8)
                            for x in range(3):
                                ada_cols(bank[5][:, 8 * x:8 * x + 8], g * 3 + (21 + x), x, 2)
                        if upto(g, KVG):
                            if b == 0 and not since(g, 1):
                                pe.wait_ge(s["v_ready"], 1)
                            if b == 2:
                                pe.wait_ge(s["ada_rows"], g * 3 + 25)
                            ada_rows(6 + b % 2, 1 + b, g + (used[1 + b] + 1), 1)

                    for b in range(3):
                        block_step(b, 0)
                    with pe.Fori(1, KVG) as g:
                        for b in range(3):
                            block_step(b, g)
                    for b in range(2):
                        block_step(b, KVG)
                    taken(4, 0, 1, 2, 3)
                    end_phase()

                    def unit(b, half, qt):
                        x = qt < 2
                        nk = 4 if x else 2
                        k0 = 0 if x else T
                        rows = slice(64 * half, 64 * half + 64)

                        def scores(g, bk):
                            return mm(bk[:, 0:nk * P], gqa_q[b][rows, qt * P:(qt + 1) * P],
                                      gqa_k[b][rows, k0:T2], start=True, stop=True)

                        def values(g, bk, pt):
                            return dot(bk[rows, qt * P:(qt + 1) * P], lambda k: gqa_v[b][:, k + k0 // P, :],
                                       lambda k: pt[:, k * P:(k + 1) * P], nk)

                        return Unit(scores=scores, values=values, tiles=[k * P for k in range(nk)])

                    attention([unit(b, h, t) for b in range(2) for h in range(2) for t in range(4)], KVG, 32, 8)
                    end_phase()
                    gemm(2, (1, 2), 2, KD, lambda k: o2[:, k, :], T2)
                else:
                    landed(0)
                    for b in range(3):
                        last = dot(bank[1 + b][:, 0:T], lambda k: slot(0)[:, k * 384 + b * P:k * 384 + (b + 1) * P],
                                   lambda k: hn_block(k)[:, 0:T], KD)
                    landed(1)
                    for b in range(2):
                        dot(bank[4 + b][:, :], lambda k: slot(1)[:, k * 288 + b * P:k * 288 + (b + 1) * P],
                            lambda k: hn[:, k, :], KD)
                    dot(bank[6][ND:QK, :], lambda k: slot(1)[:, k * 288 + 256:k * 288 + 288], lambda k: hn[:, k, :], KD) \
                        .then_inc(s["kv_mm"], 1)
                    free(0, 1)
                    taken(1, 0, 1)
                    pe.wait_ge(s["kv_raw"], 2)
                    dot(bank[0][:, 0:T], lambda b: ones, lambda b: cq_sq[:, b, :], 3)
                    dot(bank[7][:, :], lambda b: ones, lambda b: ckv_sq[:, b, :], 2).then_inc(s["kv_rot"], 1)
                    pe.wait_ge(s["kv_ready"], 2)
                    mm(bank[6][ND:QK, 0:T], C("pmla")[ND:QK, ND:QK], kr_raw[ND:QK, 0:T], start=True, stop=True) \
                        .then_inc(s["kv_dup"], 1)
                    end_phase()

                    def heads(it, q, trip):
                        if upto(it, 8):
                            sl = 2 + q
                            landed(sl, trip)
                            uq = slot(sl)[:, 0:576].rearrange("p (k h c) -> p k h c", k=3, h=2)
                            ukv = slot(sl)[:, 576:1088].rearrange("p (k h c) -> p k h c", k=2, h=2)
                            b4 = 4 * q
                            if since(it, 2):
                                pe.wait_ge(s["q_raw"], it + (4 - 1))
                                pe.wait_ge(s["q_roped"], it + (16 - 1))
                            for hh in range(2):
                                dot(bank[b4][0:QK, hh * T:(hh + 1) * T], lambda k: uq[:, k, hh, :], lambda k: cqn[:, k, :], 3)
                            for hh in range(2):
                                dot(bank[b4 + 1 + hh][0:ND, :], lambda k: ukv[:, k, hh, 0:ND], lambda k: ckvn[:, k, :], 2)
                            for t in range(4):
                                last = dot(bank[b4 + 3][:, t * P:(t + 1) * P], lambda k: ckvn[:, k, t * P:(t + 1) * P],
                                           lambda k: ukv[:, k, :, ND:P], 2)
                            last.then_inc(s["q_mm"], 1)
                            free(sl)
                        if since(it, 1):
                            x = 1 - q
                            pe.wait_ge(s["q_raw"], it + 4)
                            mm(bank[4 * x][0:QK, :], C("pmla", QK), mq_raw[x][0:QK], start=True, stop=True).then_inc(s["q_rot"], 1)

                    for q in range(2):
                        heads(q, q, 0)
                    with pe.Fori(1, 4) as trip:
                        for q in range(2):
                            heads(trip * 2 + q, q, trip)
                    heads(8, 0, 4)
                    taken(4, 2, 3)
                    end_phase()

                    def unit(q, hh, qt):
                        def scores(trip, bk):
                            return mm(bk[:, :], mla_q[q][0:QK, hh, qt * P:(qt + 1) * P],
                                      mla_keys(slice(0, QK), trip, q, hh), start=True, stop=True)

                        def values(trip, bk, pt):
                            return dot(bk[64 * hh:64 * hh + 64, qt * P:(qt + 1) * P],
                                       lambda k: mla_v[q][:, k, hh * 64:(hh + 1) * 64], lambda k: pt[:, k * P:(k + 1) * P], 4)

                        return Unit(scores=scores, values=values, tiles=[k * P for k in range(4)])

                    pe.wait_ge(s["cmp_ready"], 2)
                    attention([unit(q, h, t) for q in range(2) for h in range(2) for t in range(2)], 4, 96, 16)
                    end_phase()
                    gemm(2, (0, 2), 2, KD, lambda k: o2x[:, k, :], T)
                w = T2 if l == 0 else T
                norm(w)
                with pe.Fori(0, FB // 2) as i:
                    for q in range(2):
                        landed(2 + q, i)
                        pe.wait_ge(s["ffn_ev"], i * 2 + (n["ffn_ev"] + q + 1))
                        for x in range(2):
                            dot(bank[2 * q + x][:, 0:w], lambda k: slot(2 + q)[:, (2 * k + x) * P:(2 * k + x + 1) * P],
                                lambda k: hn_block(k)[:, 0:w], KD).then_inc(s["ffn_mm"], 1)
                free(2, 3)
                taken(FB // 2, 2, 3)
                n["ffn_ev"] += FB

                def act_block(k):
                    pe.wait_ge(s["ffn_ev"], n["ffn_ev"] + 2 - FB + max(k + 1, FB - 1))
                    return act[:, k, 0:w]

                gemm(2, (0, 1, 2, 3), 1, FB, act_block, w)
            norm(T)
            normed()
            end_phase()

        @block.scalar
        def _(act_e):
            n = counts()
            norms = [0]
            ended = [0]
            fn = nc.scalar.activation

            def end_phase():
                act_e.drain().then_inc(phase, 1)
                ended[0] += 1
                act_e.wait_ge(phase, 3 * ended[0])

            def sums(w, updated):
                b = norms[0]
                for k in range(KD):
                    if updated:
                        act_e.wait_ge(s["gemm_ev"], n["gemm_ev"] + 4 + k + 1)
                    fn(hn[:, k, 0:w], resid[:, k, 0:w], ACT.Square).then_inc(s["sq_ready"], 1)
                n["gemm_ev"] += KD * updated
                act_e.wait_ge(s["ss_ready"], b + 1)
                fn(rstd[:, 0:w], bank[7][:, 0:w], ACT.Sqrt, scale=1.0 / D, bias=C("eps")).then_inc(s["std_ready"], 1)
                norms[0] += 1

            def shifted(w, shift, layer):
                for k in range(KD):
                    act_e.wait_ge(s["hn_scaled"], n["hn_scaled"] + k + 1)
                    for part in range(w // T):
                        x = hn[:, k, part * T:(part + 1) * T]
                        last = fn(x, x, ACT.Identity, bias=ada[layer][:, shift + k, part:part + 1])
                    last.then_inc(s["hn_ready"], 1)
                n["hn_scaled"] += KD

            def norm(w, shift=None, layer=0, updated=True):
                sums(w, updated)
                if shift is not None:
                    shifted(w, shift, layer)

            def gated_out():
                with act_e.Fori(0, 2) as i:
                    for m in range(4):
                        act_e.wait_ge(s["out_mm"], i * 4 + (n["out_mm"] + m + 1))
                        act_e.wait_ge(s["out_ev"], i * 4 + (n["out_mm"] + m + 1))
                        fn(out_sig[:, m, :], bank[m][:, T:T2], ACT.Sigmoid).then_inc(s["out_sig"], 1)
                n["out_mm"] += 8

            def attention(units, trips, done):
                U = len(units)

                def step(t, it):
                    n = it * U + t
                    if upto(it, trips):
                        u = units[t]
                        act_e.wait_ge(s["att_max"], n + (done + 1))
                        if since(n, 4):
                            act_e.wait_ge(s["att_T"], n + (done - 3))
                        for b in range(u.branches):
                            o = b * u.w
                            last = fn(probs[t % 4][:, o:o + u.w], bank[t % 4][:, o:o + u.w], ACT.Exp,
                                      bias=nmax[:, t % 4, b:b + 1], accum_out=psum_[:, t % 4, b:b + 1])
                        last.then_inc(s["att_exp"], 1)
                    if since(n, 2):
                        w = units[t - 2].branches * units[t - 2].w
                        act_e.wait_ge(s["att_T"], n + (done - 1))
                        if since(n, 4):
                            act_e.wait_ge(s["att_O"], n + (done - 3))
                        fn(probs_t[t % 2][:, 0:w], bank[4 + t % 2][:, 0:w], ACT.Copy).then_inc(s["att_PT"], 1)

                for t in range(U):
                    step(t, 0)
                with act_e.Fori(1, trips) as it:
                    for t in range(U):
                        step(t, it)
                for t in range(2):
                    step(t, trips)

            act_e.wait_ge(s["vec_turned"], 1)
            for v in range(VT):
                r = min(P, VR - v * P)
                fn(cols[:, v * P:v * P + r], bank[v][:, 0:r], ACT.Copy)
            act_e.drain()
            act_e.wait_ge(s["csil_zeroed"], 1)
            for x, name in enumerate(("c", "c_2", "c_ctx_2")):
                last = fn(csil[:, (x + 1) // 2, :, max(x - 1, 0)], cols[:, VO[name]:VO[name] + KD], ACT.Silu)
            last.then_inc(s["csil_ready"], 1)
            act_e.wait_ge(setup_landed, 16 * SETUP_DMAS)
            sums(T, False)
            act_e.wait_ge(s["rope_reduced"], 1)
            fn(nsin[:, :], ang, ACT.Sin)
            fn(ncos[:, :], tmp_rope, ACT.Sin).then_inc(s["rope_sin"], 1)
            act_e.wait_ge(s["ada_ready"], 1)
            shifted(T, 0, 0)

            act_e.wait_ge(s["dt_pe"], 1)
            fn(gates, bank[5][:, 0:160].rearrange("p (c n) -> p c n", c=2)[:, :, HEADS:80], ACT.Sigmoid).then_inc(s["gates_ready"], 1)
            fn(a_neg, rows32[:, HEADS:2 * HEADS], ACT.Exp)
            act_e.wait_ge(s["dt_dve"], 1)
            fn(dt_b, dt_a, ACT.Exp).then_inc(s["dt_act"], 1)
            act_e.wait_ge(s["dt_dve"], 2)
            fn(dt_a, dt_c, ACT.Ln).then_inc(s["dt_act"], 1)
            act_e.wait_ge(s["dt_dve"], 4)
            fn(ssm_small[:, 6, :], ssm_small[:, 7, :], ACT.Exp).then_inc(s["dt_act"], 1)

            def newest(g, x):
                act_e.wait_ge(s["ssm_x"], g * 3 + (x + 1))
                for y in range(2):
                    j = g + (16 + 4 * y) if x == 2 else g * 4 + (2 * x + y)
                    last = fn(acc[:, 2 * x + y, :], bank[6 + x % 2][:, y * T:(y + 1) * T], ACT.Identity,
                              scale=cols[:, ds(j + (VO["conv_w"] + 3 * 24), 1)], bias=cols[:, ds(j + VO["conv_b"], 1)])
                last.then_inc(s["ssm_acc"], 1)

            def square():
                fn(ysq, yssm, ACT.Square).then_inc(s["ssm_sq"], 1)

            def root(count):
                act_e.wait_ge(s["ssm_ss"], count)
                fn(rs_ssm, bank[7][:, 0:T], ACT.Sqrt, scale=1.0 / 512, bias=C("eps")).then_inc(s["ssm_std"], 1)

            def group(g, last_group):
                act_e.wait_ge(s["ssm_taps"], g * 3 + 3)
                if since(g, 1):
                    act_e.wait_ge(s["ssm_y"], g)
                fn(conv, acc, ACT.Silu).then_inc(s["ssm_conv"], 1)
                if since(g, 1):
                    square()
                act_e.wait_ge(s["ssm_tok"], g + 1)
                fn(bcb, bank[2][:, 0:3 * P], ACT.Copy).then_inc(s["ssm_bcb"], 1)
                if since(g, 1):
                    root(g)
                if not last_group:
                    newest(g + 1, 0)
                act_e.wait_ge(s["ssm_E"], g + 1)
                fn(e_bc, bank[3][:, :], ACT.Exp).then_inc(s["ssm_Ex"], 1)

                def decay(u):
                    c, hh = u // 2, u % 2
                    act_e.wait_ge(s["ssm_seg"], g * 4 + (u + 1))
                    if u >= 2:
                        act_e.wait_ge(s["ssm_yd"], g * 4 + (u - 1))
                    for h in range(4):
                        last = fn(mexp[:, u % 2, h * P:(h + 1) * P], bank[4 + u % 2][:, h * P:(h + 1) * P], ACT.Exp,
                                  bias=gsm[:, 2 + c, 4 * hh + h:4 * hh + h + 1])
                    last.then_inc(s["ssm_exp"], 1)

                decay(0)
                decay(1)
                act_e.wait_ge(s["ssm_state"], g + 1)
                fn(state_t, bank[0][:, :], ACT.Copy).then_inc(s["ssm_stT"], 1)
                if not last_group:
                    newest(g + 1, 1)
                decay(2)
                decay(3)
                if not last_group:
                    newest(g + 1, 2)
                for b in range(2):
                    act_e.wait_ge(s["ssm_z"], g * 2 + (b + 1))
                    last = fn(zs[:, 2 * b:2 * b + 2, :], bank[7 - b][:, :], ACT.Silu)
                last.then_inc(s["ssm_zs"], 1)

            for x in range(3):
                newest(0, x)
            group(0, False)
            with act_e.Fori(1, GRP - 1) as g:
                group(g, False)
            group(GRP - 1, True)
            act_e.wait_ge(s["ssm_y"], GRP)
            square()
            root(GRP)
            end_phase()
            gated_out()
            end_phase()

            act_e.wait_ge(s["kv_mm"], 1)
            fn(k_raw[:, 0, :], bank[0][:, 0:T], ACT.Copy)
            fn(vc_raw, bank[0][:, T:T2], ACT.Copy)
            fn(k_raw[:, 1:3, :], bank[1][:, :], ACT.Copy).then_inc(s["kv_raw"], 1)
            act_e.wait_ge(s["kv_dup"], 1)
            for g in range(NKV):
                fn(kk[g], bank[g][:, :], ACT.Copy)
            act_e.wait_ge(s["hid_mm"], 1)
            fn(hid, bank[7][:, 0:8 * NCMP], ACT.Silu).then_inc(s["hid_silu"], 1)
            end_phase()

            def queries(j):
                if upto(j, 4):
                    act_e.wait_ge(s["q_mm"], j + 1)
                    fn(q_raw, bank[0][:, :], ACT.Copy).then_inc(s["q_raw"], 1)
                if since(j, 1):
                    act_e.wait_ge(s["ct_mm"], j)
                    for x in range(2):
                        last = fn(ct[0:NCMP, ds(j - 1, 1), x * 512:(x + 1) * 512].rearrange("p a q -> p (a q)"),
                                  bank[4 + x][0:NCMP, :], ACT.Copy)
                    last.then_inc(s["ct_ev"], 1)
                if upto(j, 4):
                    act_e.wait_ge(s["cs_max"], j + 1)
                    fn(cs, cs, ACT.Exp).then_inc(s["cs_exp"], 1)

            queries(0)
            with act_e.Fori(1, 4) as j:
                queries(j)
            queries(4)
            end_phase()
            attention([Unit(branches=2, w=P * (t % 2 + 1)) for t in range(8)], 4, 0)
            end_phase()
            gated_out()
            end_phase()
            norm(T, 24)
            end_phase()

            act_e.wait_ge(s["tok_mm"], 1)
            for t in range(TT):
                for x in range(2):
                    last = fn(h_tok[:, t, x * 512:(x + 1) * 512], bank[2 + 2 * t + x][:, :], ACT.Copy)
            last.then_inc(s["tok_ev"], 1)
            act_e.wait_ge(s["route_dve"], 1)
            fn(g4b, g4a, ACT.Exp).then_inc(s["route_act"], 1)
            act_e.wait_ge(s["route_dve"], 2)
            fn(e8b, e8a, ACT.Exp).then_inc(s["route_act"], 1)
            for k in range(KD):
                act_e.wait_ge(s["moe_X"], k + 1)
                fn(xs[:, k, :], bank[2 + k % 4][:, :], ACT.Copy).then_inc(s["moe_Xev"], 1)
            act_e.wait_ge(s["moe_St"], 1)
            for x in range(2):
                last = fn(s_t[:, 2 * x:2 * x + 2, :], bank[6 + x][:, :], ACT.Copy)
            last.then_inc(s["moe_Stev"], 1)

            def silu(i, q):
                act_e.wait_ge(s["moe_h"], i + 1)
                if since(i, 2):
                    act_e.wait_ge(s["moe_he"], i - 1)
                fn(hsil[:, q % 2, :], bank[q % 2][:, 0:FH], ACT.Silu).then_inc(s["moe_silu"], 1)

            for q in range(2):
                silu(q, q)
            with act_e.Fori(0, ITEMS // 2 - 1) as i:
                for q in range(2):
                    silu(i * 2 + (q + 2), q)
            end_phase()
            end_phase()
            norm(T, updated=False)
            end_phase()

            for l in range(2):
                norm(T2, 0, 1 + l, updated=l == 1)
                if l == 0:
                    act_e.wait_ge(s["v_mm"], 1)
                    for x in range(2):
                        last = fn(gva[:, 2 * x:2 * x + 2, :], bank[6 + x][:, :], ACT.Copy)
                    last.then_inc(s["v_ready"], 1)

                    def block_step(b, g):
                        c = g * 3 + b
                        if upto(g, KVG):
                            act_e.wait_ge(s["q_mm"], c + 5)
                            fn(gq_sq[:, b, :], bank[b][:, :], ACT.Square).then_inc(s["q_sq"], 1)
                        if since(c, 1):
                            x = (b - 1) % 3
                            act_e.wait_ge(s["q_ss"], c)
                            if x < 2:
                                last = fn(gq_std[:, x, :], bank[3][:, :], ACT.Sqrt, bias=C("eps64"))
                            else:
                                last = fn(gq_std[:, x, :], bank[3][:, :], ACT.Sqrt, scale=1.0 / DH, bias=C("eps"))
                            last.then_inc(s["q_std"], 1)

                    for b in range(3):
                        block_step(b, 0)
                    with act_e.Fori(1, KVG) as g:
                        for b in range(3):
                            block_step(b, g)
                    block_step(0, KVG)
                    end_phase()
                    attention([Unit(branches=1, w=512 if t < 2 else 256) for _ in range(4) for t in range(4)], KVG, 32)
                    end_phase()
                else:
                    act_e.wait_ge(s["kv_mm"], 2)
                    for b in range(3):
                        fn(cq_sq[:, b, :], bank[1 + b][:, 0:T], ACT.Square)
                    for b in range(2):
                        fn(ckv_sq[:, b, :], bank[4 + b][:, :], ACT.Square)
                    fn(kr_raw[ND:QK, :], bank[6][ND:QK, :], ACT.Copy).then_inc(s["kv_raw"], 1)
                    act_e.wait_ge(s["kv_rot"], 2)
                    fn(rstd[:, 0:T], bank[0][:, 0:T], ACT.Sqrt, scale=1.0 / QL, bias=C("eps"))
                    fn(ckv_rstd[:, :], bank[7][:, :], ACT.Sqrt, scale=1.0 / KVL, bias=C("eps")).then_inc(s["kv_roped"], 1)
                    end_phase()

                    def heads(q, trip):
                        it = trip * 2 + q
                        act_e.wait_ge(s["q_mm"], it + 17)
                        if since(it, 2):
                            act_e.wait_ge(s["q_roped"], it + 15)
                        fn(mq_raw[q][0:QK], bank[4 * q][0:QK, :], ACT.Copy)
                        for hh in range(2):
                            fn(mla_keys(slice(0, ND), trip, q, hh), bank[4 * q + 1 + hh][0:ND, :], ACT.Copy)
                        fn(mva[:, :, ds(it * P, P)], bank[4 * q + 3][:, :].rearrange("p (t d) -> p t d", t=4), ACT.Copy) \
                            .then_inc(s["q_raw"], 1)

                    for q in range(2):
                        heads(q, 0)
                    with act_e.Fori(1, 4) as trip:
                        for q in range(2):
                            heads(q, trip)
                    end_phase()
                    attention([Unit(branches=1, w=512) for _ in range(8)], 4, 96)
                    end_phase()
                w = T2 if l == 0 else T
                norm(w, 24, 1 + l)
                cw, cb = VO["ffn_conv_w_2"] + l * 3 * 2 * FB, VO["ffn_conv_b_2"] + l * 2 * FB
                with act_e.Fori(0, FB // 2) as i:
                    for q in range(2):
                        j = i * 2 + q
                        act_e.wait_ge(s["ffn_ev"], j + (n["ffn_ev"] + 1))
                        for x in range(2):
                            act_e.wait_ge(s["ffn_mm"], j * 2 + (2 * n["ffn_ev"] + x + 1))
                            fn(ffn_acc[:, 2 * q + x, 0:w], bank[2 * q + x][:, 0:w], ACT.Identity,
                               scale=cols[:, ds(j + (cw + 2 * FB + x * FB), 1)], bias=cols[:, ds(j + (cb + x * FB), 1)]) \
                                .then_inc(s["ffn_acc"], 1)
                        act_e.wait_ge(s["ffn_taps"], j + (n["ffn_ev"] + 1))
                        g = ffn_acc[:, 2 * q + 1, 0:w]
                        fn(g, g, ACT.Silu).then_inc(s["ffn_silu"], 1)
                n["ffn_ev"] += FB
            norm(T)
            end_phase()

        @block.gpsimd
        def _(pool):
            nc.gpsimd.memset(csil[:, :, :, :], 0.0).then_inc(s["csil_zeroed"], 1)

            def attention(U, trips, done, ready, first, queries, values):
                def half_set(it, half):
                    end = done + (half + 1) * U // 2 - U
                    if since(it, 1):
                        pool.wait_ge(s["att_S"], it * U + end)
                        pool.sem_inc(s["q_unset"], 1)
                    queries(it, half).then_inc(s["q_set"], 1)
                    if since(it, 1):
                        pool.wait_ge(s["att_O"], it * U + end)
                        pool.sem_inc(s["v_unset"], 1)
                    values(it, half).then_inc(s["v_set"], 1)

                for what, count in first:
                    pool.wait_ge(what, count)
                for half in range(2):
                    half_set(0, half)
                pool.wait_ge(phase, 3 * ready)
                with pool.Fori(1, trips) as it:
                    for half in range(2):
                        half_set(it, half)

            def copy(out, src):
                return nc.gpsimd.tensor_copy(out, src)

            attention(8, 4, 0, NSA_QUERIES, [(phase, 3 * NSA_QUERIES)],
                      lambda j, u: copy(nsa_q[u], q_all[:, ds(j * 2 + u, 1), :].rearrange("p a t -> p (a t)")),
                      lambda j, u: copy(nsa_ct[u][0:NCMP], ct[0:NCMP, ds(j, 1), u * 512:(u + 1) * 512].rearrange("p a q -> p (a q)")))

            pool.wait_ge(phase, 3 * (MOE_PHASE - 1))
            nc.gpsimd.memset(ys, 0.0).then_inc(s["moe_zeroed"], 1)
            pool.wait_ge(s["route_dve"], 5)
            pool.wait_ge(s["moe_Xev"], KD)

            def copy_tile(i, q):
                tile = pool.value_load(tile_i.bitcast(I32)[0:1, ds(i, 1)], min_val=0, max_val=PT - 1)
                if since(i, 2):
                    pool.wait_ge(s["moe_h"], i - 1)
                nc.gpsimd.tensor_copy(x_t[q % 2], xs[:, :, bass.ts(tile, P)]).then_inc(s["moe_xt"], 1)

            for q in range(2):
                copy_tile(q, q)
            with pool.Fori(0, ITEMS // 2 - 1) as i:
                for q in range(2):
                    copy_tile(i * 2 + (q + 2), q)

            def gqa_queries(g, b):
                copy(gqa_k[b], gqa_block(2, g))
                return copy(gqa_q[b], gqa_block(b, g))

            attention(16, KVG, 32, GQA_QUERIES, [(s["v_ready"], 1), (s["q_roped"], 4 + 3)], gqa_queries, lambda g, b: copy(gqa_v[b], gva[:, :, ds(g * DH, DH)]))

            pool.wait_ge(phase, 3 * MLA_LOW_RANK)
            rows = slice(ND, QK)
            for q in range(2):
                copy(mka[q][rows, :, :], kr_raw[rows].unsqueeze(1).to_broadcast([RD, KD, T2]))
            pool.drain().then_inc(s["cmp_ready"], 1)

            attention(8, 4, 96, MLA_QUERIES, [(s["q_raw"], 4 + 2), (s["q_roped"], 16 + 2)],
                      lambda trip, q: copy(mla_q[q][0:QK], mqa[0:QK, ds((trip * 2 + q) * 2, 2), :]),
                      lambda trip, q: copy(mla_v[q], mva[:, :, ds((trip * 2 + q) * P, P)]))

        @block.vector
        def _(ve):
            n = counts()
            norms = [0]
            ended = [0]
            V = nc.vector
            ve.sem_inc(s["out_ev"], 4)
            ve.sem_inc(s["gemm_ev"], 4)
            ve.sem_inc(s["ffn_ev"], 2)

            def end_phase():
                ve.drain().then_inc(phase, 1)
                ended[0] += 1
                ve.wait_ge(phase, 3 * ended[0])

            def ada_copy(b, c, buf):
                ve.wait_ge(s["ada_mm"], c + 1)
                V.tensor_copy(row_buf[:, buf, :], bank[b][:, :]).then_inc(s["ada_rows"], 1)

            def ada_bias(layer, src, chunks, first, ncol, bias):
                src = src.rearrange("p (n c) -> p n c", c=2)[:, :, 0:ncol]
                V.tensor_tensor(ada[layer][:, ds(first * 4, chunks * 4), 0:ncol], src,
                                cols[:, ds(first * 4 + bias, chunks * 4)].unsqueeze(2).to_broadcast([P, chunks * 4, ncol]),
                                ALU.add).then_inc(s["ada_ready"], 1)

            def modulate(layer, which, ncol, gain):
                for part in range(ncol):
                    V.scalar_tensor_tensor(mod[layer][:, which, part, :], ada[layer][:, 8 + 24 * which:16 + 24 * which, part], 1.0,
                                           cols[:, gain:gain + KD], ALU.add, ALU.mult)
                ve.drain()

            def norm(w, gain, out, shifted):
                ve.wait_ge(s["std_ready"], norms[0] + 1)
                V.reciprocal(rstd[:, 0:w], rstd[:, 0:w])
                ve.drain()
                for k in range(KD):
                    for part in range(w // T):
                        a, b = part * T, (part + 1) * T
                        last = V.scalar_tensor_tensor(out[:, k, a:b], resid[:, k, a:b], gain(part)[:, k:k + 1],
                                                      rstd[:, a:b], ALU.mult, ALU.mult)
                    last.then_inc(s["hn_scaled"] if shifted else s["hn_ready"], 1)
                norms[0] += 1

            def gated_out(first, layer, bias, chunk, before):
                with ve.Fori(0, 2) as i:
                    for m in range(4):
                        ada_copy(4 + m % 2, i * 4 + (chunk + m), m % 3)
                        ve.wait_ge(s["out_sig"], i * 4 + (n["out_mm"] + m + 1))
                        dst = merged[:, ds(i * 4 + m, 1), :].rearrange("p a t -> p (a t)")
                        if first:
                            V.tensor_tensor(dst, bank[m][:, 0:T], out_sig[:, m, :], ALU.mult).then_inc(s["out_ev"], 1)
                        else:
                            V.tensor_tensor(out_tmp[:, m % 2, :], bank[m][:, 0:T], out_sig[:, m, :], ALU.mult)
                            ve.drain()
                            V.tensor_tensor(dst, dst, out_tmp[:, m % 2, :], ALU.add).then_inc(s["out_ev"], 1)
                    ve.wait_ge(s["ada_cols"], i * 4 + (chunk + 4))
                    ada_bias(layer, bank[6][:, 0:32], 4, i * 4 + before, 1 if first else 2, bias)
                n["out_mm"] += 8

            def gemm(trips, per_trip, w, gate, layer=0):
                with ve.Fori(0, trips) as i:
                    for m in range(per_trip):
                        ve.wait_ge(s["gemm_mm"], i * per_trip + (n["gemm_mm"] + m + 1))
                        for part in range(w // T):
                            a, b = part * T, (part + 1) * T
                            dst = resid[:, ds(i * per_trip + m, 1), a:b].rearrange("p a t -> p (a t)")
                            last = V.scalar_tensor_tensor(
                                dst, bank[m % 4][:, a:b],
                                ada[layer][:, ds(i * per_trip + (gate + m), 1), part:part + 1].rearrange("p a t -> p (a t)"),
                                dst, ALU.mult, ALU.add)
                        last.then_inc(s["gemm_ev"], 1)
                n["gemm_mm"] += trips * per_trip

            def attention(units, trips, done, outputs):
                U = len(units)

                def evacuate(it, half):
                    ve.wait_ge(s["att_O"], it * U + (done + (half + 1) * U // 2))
                    outputs(it, half, bank[6 + half]).then_inc(s["att_ev"], 1)

                def step(t, it):
                    n = it * U + t
                    if upto(it, trips):
                        u = units[t]
                        ve.wait_ge(s["att_S"], n + (done + 1))
                        V.tensor_reduce(nmax[:, t % 4, 0:u.branches],
                                        bank[t % 4][:, 0:u.branches * u.w].rearrange("p (b k) -> p b k", b=u.branches),
                                        AX.X, ALU.max, negate=True).then_inc(s["att_max"], 1)
                    if since(n, 1) and upto(n - 1, trips * U):
                        v = (t - 1) % U
                        u = units[v]
                        ve.wait_ge(s["att_exp"], n + done)
                        fac = pfac[:, v % 4, 0:u.branches]
                        V.reciprocal(fac, psum_[:, v % 4, 0:u.branches])
                        ve.drain()
                        if u.gate is not None:
                            V.tensor_tensor(fac, fac, u.gate(it if t >= 1 else it - 1), ALU.mult)
                            ve.drain()
                        for b in range(u.branches):
                            pb = probs[v % 4][:, b * u.w:(b + 1) * u.w]
                            last = V.tensor_scalar(pb, pb, fac[:, b:b + 1], None, ALU.mult)
                        last.then_inc(s["att_scaled"], 1)
                    if t == U // 2 + 3:
                        evacuate(it, 0)
                    if t == 3 and since(it, 1):
                        evacuate(it - 1, 1)

                for t in range(U):
                    step(t, 0)
                with ve.Fori(1, trips) as it:
                    for t in range(U):
                        step(t, it)
                step(0, trips)
                evacuate(trips - 1, 1)

            ve.wait_ge(setup_landed, 16 * SETUP_DMAS)
            V.tensor_copy(pos_f, pos_i.bitcast(I32))
            ve.drain()
            V.tensor_scalar(ang, pos_f, C("invf"), None, ALU.mult)
            ve.drain()
            for quarter, dst in ((0.25, tmp_rope), (0.0, ang)):
                V.tensor_scalar(turns, ang, 1.0 / (2 * math.pi), quarter, ALU.mult, ALU.add)
                ve.drain()
                V.tensor_scalar(turns, turns, 1.5 * 2 ** 23, None, ALU.add)
                ve.drain()
                V.tensor_scalar(turns, turns, -1.5 * 2 ** 23, None, ALU.add)
                ve.drain()
                src = ang
                for part in TWO_PI:
                    V.scalar_tensor_tensor(dst, turns, -part, src, ALU.mult, ALU.add)
                    ve.drain()
                    src = dst
                if quarter:
                    V.tensor_scalar(dst, dst, math.pi / 2, None, ALU.add)
                    ve.drain()
                V.tensor_scalar(dst, dst, PI_BELOW, -PI_BELOW, ALU.min, ALU.max)
                ve.drain()
            ve.drain().then_inc(s["rope_reduced"], 1)
            ve.wait_ge(s["csil_ready"], 1)
            for q in range(4):
                if q == 3:
                    ve.wait_ge(s["ada_cols"], 1)
                ada_copy(q, q, q % 3)
            ve.wait_ge(s["ada_cols"], 4)
            ada_bias(0, bank[4][:, 0:32], 4, 0, 1, VO["b_ada"])
            ve.drain()
            modulate(0, 0, 1, VO["norm1_g"])
            norm(T, lambda part: mod[0][:, 0, part, :], hn, True)

            ve.wait_ge(s["rope_sin"], 1)
            V.tensor_scalar(ncos8, ncos[:, :], DH ** -0.5, None, ALU.mult)
            V.tensor_scalar(nsin8, nsin[:, :], DH ** -0.5, None, ALU.mult)
            ve.wait_ge(s["gates_ready"], 1)
            bias = rows32[:, 0:HEADS].unsqueeze(1).to_broadcast([P, 2, HEADS])
            V.tensor_tensor(dt_in, bank[5][:, 0:160].rearrange("p (c n) -> p c n", c=2)[:, :, 0:HEADS], bias, ALU.add)
            ve.drain()
            V.tensor_scalar(dt_a, dt_in, -1.0, None, ALU.mult)
            ve.drain()
            V.tensor_tensor(dt_a, dt_a, dt_in, ALU.min).then_inc(s["dt_dve"], 1)
            ve.wait_ge(s["dt_act"], 1)
            V.tensor_scalar(dt_c, dt_b, 1.0, None, ALU.add)
            ve.drain().then_inc(s["dt_dve"], 1)
            V.tensor_scalar(dt_d, dt_c, -1.0, None, ALU.add)
            ve.drain()
            ve.wait_ge(s["dt_act"], 2)
            V.tensor_scalar(dt_c, dt_d, 0.0, None, ALU.is_equal)
            ve.drain()
            V.tensor_tensor(dt_a, dt_a, dt_c, ALU.add)
            V.tensor_tensor(dt_d, dt_d, dt_c, ALU.add)
            ve.drain()
            V.reciprocal(dt_d, dt_d)
            V.tensor_tensor(dt_a, dt_a, dt_b, ALU.mult)
            ve.drain()
            V.tensor_tensor(dt_a, dt_a, dt_d, ALU.mult)
            V.tensor_scalar(dt_b, dt_in, 0.0, None, ALU.max)
            ve.drain()
            dt = ssm_small[:, 4:6, :]
            V.tensor_tensor(dt, dt_a, dt_b, ALU.add)
            ve.drain()
            V.tensor_tensor(ssm_small[:, 0:2, :], dt, a_neg.unsqueeze(1).to_broadcast([P, 2, HEADS]), ALU.mult)
            ve.drain()
            V.tensor_scalar(ssm_small[:, 0:2, :], ssm_small[:, 0:2, :], -1.0, None, ALU.mult)
            ve.drain().then_inc(s["dt_dve"], 1)
            ve.wait_ge(s["dt_pe"], 2)
            cum = bank[4][:, 0:2 * HEADS].rearrange("p (c n) -> p c n", c=2)
            V.tensor_scalar(ssm_small[:, 2:4, :], cum, -1.0, None, ALU.mult)
            ve.drain()
            V.tensor_tensor(ssm_small[:, 7, :], ssm_small[:, 2, :], bank[4][:, 2 * HEADS:3 * HEADS], ALU.add)
            ve.drain().then_inc(s["dt_dve"], 1)
            ve.wait_ge(s["dt_act"], 3)
            ve.drain()

            def taps(g, x):
                ve.wait_ge(s["ssm_acc"], g * 3 + (x + 1))
                for back in range(1, CONV):
                    for y in range(2):
                        j = g + (16 + 4 * y) if x == 2 else g * 4 + (2 * x + y)
                        a = acc[:, 2 * x + y, back:T]
                        V.scalar_tensor_tensor(a, bank[6 + x % 2][:, y * T:(y + 1) * T - back],
                                               cols[:, ds(j + (VO["conv_w"] + (CONV - 1 - back) * 24), 1)], a, ALU.mult, ALU.add)
                    ve.drain() if back < CONV - 1 else ve.drain().then_inc(s["ssm_taps"], 1)

            def normed(g):
                ve.wait_ge(s["ssm_std"], g + 1)
                V.reciprocal(rs_ssm, rs_ssm)
                ve.drain()
                for b in range(4):
                    V.scalar_tensor_tensor(ynorm[:, ds(g * 4 + b, 1), :].rearrange("p a t -> p (a t)"), yssm[:, b, :],
                                           cols[:, ds(g * 4 + (VO["ssm_norm_g"] + b), 1)], rs_ssm, ALU.mult, ALU.mult)
                ve.drain()

            def group(g, last_group):
                V.tensor_copy(gsm, ssm_small[:, :, ds(g * HPG, HPG)])
                ve.drain()
                V.tensor_copy(dt_wide.rearrange("p (h d) -> p h d", h=HPG), gsm[:, 1, :].unsqueeze(2).to_broadcast([P, HPG, HD])) \
                    .then_inc(s["gsm_ready"], 1)
                ve.wait_ge(s["ssm_tok"], g + 1)
                for c in range(2):
                    V.tensor_tensor(xdt[:, c, :].rearrange("p (h d) -> p h d", h=HPG),
                                    bank[c][:, :].rearrange("p (h d) -> p h d", h=HPG),
                                    gsm[:, 4 + c, :].unsqueeze(2).to_broadcast([P, HPG, HD]), ALU.mult)
                ve.drain()
                V.tensor_tensor(xw.rearrange("p (h d) -> p h d", h=HPG), xdt[:, 0, :].rearrange("p (h d) -> p h d", h=HPG),
                                gsm[:, 6, :].unsqueeze(2).to_broadcast([P, HPG, HD]), ALU.mult).then_inc(s["ssm_xw"], 1)
                if since(g, 1):
                    normed(g - 1)
                if not last_group:
                    taps(g + 1, 0)
                ve.wait_ge(s["ssm_bcb"], g + 1)

                def decayed(u):
                    ve.wait_ge(s["ssm_exp"], g * 4 + (u + 1))
                    m = mexp[:, u % 2, :].rearrange("p (h t) -> p h t", h=4)
                    V.tensor_tensor(m, m, cb[:, u // 2, :].unsqueeze(1).to_broadcast([P, 4, P]), ALU.mult) \
                        .then_inc(s["ssm_M"], 1)

                decayed(0)
                decayed(1)
                if not last_group:
                    taps(g + 1, 1)
                decayed(2)
                decayed(3)
                ve.wait_ge(s["ssm_yoff"], g + 1)
                ve.wait_ge(s["ssm_Ex"], g + 1)
                V.tensor_tensor(yoff, bank[3][:, :].rearrange("p (b t) -> p b t", b=4),
                                e_bc.rearrange("p (b t) -> p b t", b=4), ALU.mult)
                if not last_group:
                    taps(g + 1, 2)
                ve.wait_ge(s["ssm_yd"], g * 4 + 4)
                for b in range(4):
                    V.scalar_tensor_tensor(yssm[:, b, :], conv[:, b, :], cols[:, ds(g * 4 + (VO["d_skip"] + b), 1)],
                                           bank[1 + b // 2][:, (b % 2) * T:(b % 2 + 1) * T], ALU.mult, ALU.add)
                ve.drain()
                V.tensor_tensor(yssm[:, :, P:T], yssm[:, :, P:T], yoff, ALU.add)
                ve.drain()
                ve.wait_ge(s["ssm_zs"], g + 1)
                V.tensor_tensor(yssm, yssm, zs, ALU.mult)
                ve.drain().then_inc(s["ssm_y"], 1)

            for x in range(3):
                taps(0, x)
            group(0, False)
            with ve.Fori(1, GRP - 1) as g:
                group(g, False)
            group(GRP - 1, True)
            normed(GRP - 1)
            end_phase()
            gated_out(True, 0, VO["b_ada"], 4, 4)
            end_phase()

            ve.wait_ge(s["kv_mm"], 1)
            V.tensor_copy(v_tok.rearrange("p b t d -> p (b t d)"), bank[2][:, :])
            ve.wait_ge(s["kv_raw"], 1)

            def over(table, m):
                return table.unsqueeze(1).to_broadcast([P, m, T])

            V.tensor_tensor(k_roped, k_raw, over(ncos[:, :], 3), ALU.mult)
            ve.wait_ge(s["kv_rot"], 1)
            V.tensor_tensor(k_tmp[:, 0:2, :], bank[3][:, :].rearrange("p (a t) -> p a t", a=2), over(nsin[:, :], 2), ALU.mult)
            V.tensor_tensor(k_tmp[:, 2, :], bank[4][:, 0:T], nsin[:, :], ALU.mult)
            ve.drain()
            V.tensor_tensor(k_roped, k_roped, k_tmp, ALU.add).then_inc(s["kv_roped"], 1)
            ve.wait_ge(s["kv_dup"], 1)
            for x, name in enumerate(("cmp_pe_k", "cmp_pe_v")):
                pe_cols = cols[:, VO[name]:VO[name] + 16]
                for g in range(NKV):
                    src = bank[5 + x][:, g * T:(g + 1) * T].rearrange("p (c j) -> p j c", j=STRIDE)
                    for h in range(2):
                        rows = slice(64 * h, 64 * h + 64)
                        for late in range(2):
                            V.tensor_tensor(blk[x][rows, 8 * late:8 * late + 8, g * NCMP:(g + 1) * NCMP],
                                            src[rows, h:STRIDE:2, late:late + NCMP],
                                            pe_cols[rows, 8 * late:8 * late + 8].unsqueeze(2).to_broadcast([64, 8, NCMP]), ALU.add)
            ve.drain().then_inc(s["kv_ready"], 1)
            ve.wait_ge(s["cmp_mm"], 1)
            V.tensor_copy(k_cmp, bank[4][:, 256:256 + 2 * NCMP])
            V.tensor_copy(v_cmp[0:NCMP].rearrange("p g d -> p (g d)"), bank[4][0:NCMP, 320:320 + 2 * DH])
            ve.drain().then_inc(s["cmp_ready"], 1)
            end_phase()

            gv_ = gates.rearrange("p q (u j h b) -> p u j h q b", u=2, j=4, h=2, b=3)
            for j in range(4):
                for b in range(3):
                    for u in range(2):
                        V.tensor_copy(gsel[:, j, 8 * b + 4 * u:8 * b + 4 * u + 4].rearrange("p (h q) -> p h q", h=2),
                                      gv_[:, u, j, :, :, b])
            ve.drain()

            def queries(j):
                ada_copy(6, j + 12, 0)
                ve.wait_ge(s["q_raw"], j + 1)
                V.tensor_tensor(q_t, q_raw, over(ncos8, 2), ALU.mult)
                ve.wait_ge(s["q_rot"], j + 1)
                V.tensor_tensor(q_tmp, bank[1][:, :].rearrange("p (a t) -> p a t", a=2), over(nsin8, 2), ALU.mult)
                ve.drain()
                V.tensor_tensor(q_t, q_t, q_tmp, ALU.add)
                ve.wait_ge(s["ada_cols"], j + 13)
                ada_bias(1, bank[3][:, 256:264], 1, j, 2, VO["ada_b_2"])
                ve.drain().then_inc(s["q_roped"], 1)
                V.tensor_copy(q_all[:, ds(j * 2, 2), :], q_t)
                ve.wait_ge(s["cs_mm"], j + 1)
                if since(j, 1):
                    ve.wait_ge(s["ct_mm"], j)
                for half in range(2):
                    V.tensor_tensor(cs[:, half:4:2, :], bank[2 + half][:, 0:4 * NCMP].rearrange("p (a c) -> p a c", a=2),
                                    C("cneg").unsqueeze(1).to_broadcast([P, 2, 2 * NCMP]), ALU.add)
                ve.drain()
                cs8 = cs.rearrange("p a (q c) -> p (a q) c", q=2)
                V.tensor_reduce(cs_m, cs8, AX.X, ALU.max)
                ve.drain()
                V.tensor_tensor(cs8, cs8, cs_m.unsqueeze(2).to_broadcast([P, 8, NCMP]), ALU.subtract).then_inc(s["cs_max"], 1)
                ve.wait_ge(s["cs_exp"], j + 1)
                V.tensor_tensor(cs, cs, C("c01").unsqueeze(1).to_broadcast([P, 4, 2 * NCMP]), ALU.mult)
                ve.drain()
                V.tensor_reduce(cs_s, cs8, AX.X, ALU.add)
                ve.drain()
                V.tensor_scalar(cs_s, cs_s, 1e-30, None, ALU.max)
                ve.drain()
                V.reciprocal(cs_s, cs_s)
                ve.drain()
                V.tensor_tensor(cs_s, cs_s, gsel[:, ds(j, 1), 0:8].rearrange("p a n -> p (a n)"), ALU.mult)
                ve.drain()
                V.tensor_tensor(cs8, cs8, cs_s.unsqueeze(2).to_broadcast([P, 8, NCMP]), ALU.mult).then_inc(s["cs_ready"], 1)

            queries(0)
            with ve.Fori(1, 4) as j:
                queries(j)
            end_phase()

            def nsa_gate(t):
                return lambda j: gsel[:, ds(j, 1), 8 + t:24:8].rearrange("p a n -> p (a n)")

            attention([Unit(branches=2, w=P * (t % 2 + 1), gate=nsa_gate(t)) for t in range(8)], 4, 0,
                      lambda j, u, b: V.tensor_copy(o_t[:, ds(j + 4 * u, 1), :].rearrange("p a t -> p (a t)"), b[:, 0:T]))
            end_phase()
            gated_out(False, 1, VO["ada_b_2"], 16, 4)
            end_phase()
            gemm(2, 4, T, 16)
            modulate(0, 1, 1, VO["norm2_g"])
            norm(T, lambda part: mod[0][:, 1, part, :], hn, True)
            end_phase()

            ve.wait_ge(s["route_pe"], 1)

            def b2(x, m):
                return x.to_broadcast([P, 2, m])

            def first_max(x, rev, top, key, out, m):
                V.tensor_reduce(top, x, AX.X, ALU.max)
                ve.drain()
                V.tensor_tensor(key, x, b2(top, m), ALU.is_equal)
                ve.drain()
                V.tensor_tensor(key, key, rev.unsqueeze(1).to_broadcast([P, 2, m]), ALU.mult)
                ve.drain()
                V.tensor_reduce(t2f, key, AX.X, ALU.max)
                ve.drain()
                V.tensor_tensor(out, key, b2(t2f, m), ALU.is_equal)
                ve.drain()

            V.tensor_tensor(lg, bank[0][:, 0:72].rearrange("p (t n) -> p t n", t=2),
                            rows32[:, 3 * HEADS:].unsqueeze(1).to_broadcast([P, 2, 36]), ALU.add)
            ve.drain()
            gl, el = lg[:, :, 0:NG], lg[:, :, NG:NG + NE]
            first_max(gl, C("rev4"), t2a, g4b, g4c, NG)
            V.tensor_tensor(g4a, gl, b2(t2a, NG), ALU.subtract)
            ve.drain().then_inc(s["route_dve"], 1)
            for t in range(2):
                V.tensor_tensor(e32[:, t], el[:, t].rearrange("p (g e) -> p g e", g=NG),
                                g4c[:, t, :].unsqueeze(2).to_broadcast([P, NG, EPG]), ALU.mult)
            ve.drain()
            for t in range(2):
                V.tensor_reduce(e8c[:, t, :], e32[:, t].rearrange("p g e -> p e g"), AX.X, ALU.add)
            ve.drain()
            V.tensor_reduce(t2b, e8c, AX.X, ALU.max)
            ve.drain()
            V.tensor_tensor(e8a, e8c, b2(t2b, EPG), ALU.subtract)
            ve.drain().then_inc(s["route_dve"], 1)
            ve.wait_ge(s["route_act"], 1)
            V.tensor_reduce(t2a, g4b, AX.X, ALU.add)
            ve.drain()
            V.reciprocal(t2a, t2a)
            ve.wait_ge(s["route_act"], 2)
            V.tensor_reduce(t2b, e8b, AX.X, ALU.add)
            ve.drain()
            V.reciprocal(t2b, t2b)
            ve.drain()
            V.tensor_tensor(e8b, e8b, b2(t2b, EPG), ALU.mult)
            ve.drain()
            first_max(e8b, C("rev8"), t2b, e8c, e8d, EPG)
            V.scalar_tensor_tensor(e8b, e8d, -2.0, e8b, ALU.mult, ALU.add)
            ve.drain()
            first_max(e8b, C("rev8"), t2c, e8c, e8e, EPG)
            V.tensor_tensor(t2d, t2b, t2c, ALU.add)
            ve.drain()
            V.reciprocal(t2d, t2d)
            V.tensor_tensor(t2b, t2b, t2a, ALU.mult)
            V.tensor_tensor(t2c, t2c, t2a, ALU.mult)
            ve.drain()
            V.tensor_tensor(t2b, t2b, t2d, ALU.mult)
            V.tensor_tensor(t2c, t2c, t2d, ALU.mult)
            for t in range(2):
                og = g4c[:, t, :].unsqueeze(2).to_broadcast([P, NG, EPG])
                for dst, src in ((sel_a, e8d), (sel_b, e8e)):
                    V.tensor_tensor(dst[:, t, :].rearrange("p (g e) -> p g e", g=NG), og,
                                    src[:, t, :].unsqueeze(1).to_broadcast([P, NG, EPG]), ALU.mult)
            ve.drain()
            V.tensor_tensor(selm, sel_a, sel_b, ALU.add)
            ve.drain().then_inc(s["route_dve"], 1)
            ve.wait_ge(s["route_pe"], 2)
            V.tensor_copy(cnt_col[0:NE], bank[1][0:NE, 2 * NE:2 * NE + 1])
            V.tensor_copy(pos, bank[1][:, 0:2 * NE].rearrange("p (t e) -> p t e", t=2))
            ve.drain().then_inc(s["route_dve"], 1)
            ve.wait_ge(s["route_pe"], 3)
            V.tensor_copy(start, bank[0][:, 0:NE])
            ve.drain()
            V.tensor_tensor(pos, pos, start.unsqueeze(1).to_broadcast([P, 2, NE]), ALU.add)
            ve.drain()
            V.tensor_tensor(sel_a, sel_a, pos, ALU.mult)
            V.tensor_tensor(sel_b, sel_b, pos, ALU.mult)
            ve.drain()
            V.tensor_reduce(pos_a, sel_a, AX.X, ALU.add)
            V.tensor_reduce(pos_b, sel_b, AX.X, ALU.add)
            ve.drain()
            ve.wait_ge(s["moe_iota"], 16)
            for t in range(2):
                V.tensor_scalar(pick[:, t, :], iota, pos_a[:, t, :], None, ALU.is_equal)
            ve.drain()
            for t in range(2):
                V.scalar_tensor_tensor(pick[:, t, :], iota, pos_b[:, t, :], pick[:, t, :], ALU.is_equal, ALU.add)
            ve.drain().then_inc(s["moe_G"], 1)
            V.tensor_tensor(at_end, start.unsqueeze(1).to_broadcast([P, PT - 1, NE]),
                            C("tile_end").unsqueeze(2).to_broadcast([P, PT - 1, NE]), ALU.is_lt)
            V.tensor_tensor(before_place, start.unsqueeze(1).to_broadcast([P, PT, NE]),
                            C("place").unsqueeze(2).to_broadcast([P, PT, NE]), ALU.is_le)
            ve.drain()
            V.tensor_reduce(ends, at_end, AX.X, ALU.add)
            V.tensor_reduce(code_place, before_place, AX.X, ALU.add)
            ve.drain()
            V.tensor_tensor(ends, ends, C("tile"), ALU.add)
            V.tensor_tensor(code_place, code_place, C("code"), ALU.add)
            ve.drain()
            V.tensor_tensor(tile_f3, iota[:, 0:ITEMS].unsqueeze(1).to_broadcast([P, PT - 1, ITEMS]),
                            ends.unsqueeze(2).to_broadcast([P, PT - 1, ITEMS]), ALU.is_ge)
            ve.drain()
            V.tensor_reduce(tile_f, tile_f3.rearrange("p j i -> p i j"), AX.X, ALU.add)
            ve.drain()
            V.tensor_tensor(expert_f, iota[:, 0:ITEMS], tile_f, ALU.subtract)
            V.scalar_tensor_tensor(code_item, tile_f, 2.0 * NE - 1, iota[:, 0:ITEMS], ALU.mult, ALU.add)
            V.tensor_copy(tile_i.bitcast(I32), tile_f)
            ve.drain()
            V.tensor_scalar(expert_f, expert_f, NE - 1.0, None, ALU.min)
            ve.drain()
            V.tensor_copy(expert_i.bitcast(I32), expert_f)
            ve.drain().then_inc(s["route_dve"], 1)
            V.tensor_scalar(mask, code_item, code_place[:, 0:1], None, ALU.is_equal)
            for j in range(1, PT):
                ve.drain()
                V.scalar_tensor_tensor(mask, code_item, code_place[:, j:j + 1], mask, ALU.is_equal, ALU.add)
            for t in range(2):
                V.tensor_scalar(wpick[:, t, :], iota, pos_a[:, t, :], t2b[:, t, :], ALU.is_equal, ALU.mult)
                V.tensor_scalar(wpick_b, iota, pos_b[:, t, :], t2c[:, t, :], ALU.is_equal, ALU.mult)
                ve.drain()
                V.tensor_tensor(wpick[:, t, :], wpick[:, t, :], wpick_b, ALU.add)
                ve.drain()
            ve.drain().then_inc(s["moe_G"], 1)
            ve.wait_ge(s["moe_zeroed"], 1)

            def step(i, q):
                if since(i, 1) and upto(i, ITEMS + 1):
                    x = (q + 1) % 2
                    ve.wait_ge(s["moe_silu"], i)
                    if since(i, 3):
                        ve.wait_ge(s["moe_hT"], i - 2)
                    V.scalar_tensor_tensor(he[:, x, :], hsil[:, x, :], mask[:, ds(i - 1, 1)], bank[x][:, FH:2 * FH],
                                           ALU.mult, ALU.mult).then_inc(s["moe_he"], 1)
                    ve.wait_ge(s["moe_hT"], i)
                    if since(i, 3):
                        ve.wait_ge(s["moe_y"], i - 2)
                    V.tensor_copy(he_t[:, x, :], bank[2 + x][:, 0:FH]).then_inc(s["moe_hTev"], 1)
                if since(i, 2):
                    ve.drain()
                    tile = ve.value_load(tile_i.bitcast(I32)[0:1, ds(i - 2, 1)], min_val=0, max_val=PT - 1)
                    ve.wait_ge(s["moe_y"], i - 1)
                    for half in range(2):
                        y = ys[:, ds(tile, 1), half * 512:(half + 1) * 512].rearrange("p a d -> p (a d)")
                        last = V.tensor_tensor(y, y, bank[4 + 2 * (q % 2) + half][:, :], ALU.add)
                    last.then_inc(s["moe_yacc"], 1)

            for q in range(4):
                step(q, q)
            with ve.Fori(1, ITEMS // 4) as trip:
                for q in range(4):
                    step(trip * 4 + q, q)
            for q in range(2):
                step(ITEMS + q, q)
            end_phase()
            for k in range(KD):
                V.scalar_tensor_tensor(resid[:, k, 0:T], bank[k // 2][:, (k % 2) * T:(k % 2 + 1) * T], ada[0][:, 40 + k, 0:1],
                                       resid[:, k, 0:T], ALU.mult, ALU.add)
            end_phase()
            norm(T, lambda part: cols[:, VO["final_g"]:VO["final_g"] + KD], resid, False)
            end_phase()

            for l in range(2):
                for which, name in enumerate(("norm1_g_2", "norm2_g_2")):
                    modulate(1 + l, which, 2, VO[name] + KD * l)
                norm(T2, lambda part: mod[1 + l][:, 0, part, :], hn, True)
                if l == 0:
                    def block_step(b, g):
                        c = g * 3 + b
                        if since(c, 1) and upto(c - 1, 3 * KVG):
                            x, xg = (b - 1) % 3, g if b >= 1 else g - 1
                            ve.wait_ge(s["q_std"], c)
                            V.reciprocal(gq_std[:, x, :], gq_std[:, x, :])
                            ve.drain()
                            gain = VO["gqa_q_norm_g_2"] if x < 2 else VO["gqa_k_norm_g_2"]
                            V.scalar_tensor_tensor(gqa_block(x, xg), bank[x][:, :], cols[:, gain:gain + 1], gq_std[:, x, :],
                                                   ALU.mult, ALU.mult)
                            ve.drain().then_inc(s["q_normed"], 1)
                        if since(c, 2):
                            x, xg = (b - 2) % 3, g if b == 2 else g - 1
                            block = gqa_block(x, xg)[:, 0:T]
                            V.tensor_tensor(gq_cos, block, C("gcos"), ALU.mult)
                            ve.wait_ge(s["q_rot"], c + (4 - 1))
                            V.tensor_tensor(gq_sin, bank[4][:, 0:T], C("gsin"), ALU.mult)
                            ve.drain()
                            V.tensor_tensor(block, gq_cos, gq_sin, ALU.add)
                            ve.drain().then_inc(s["q_roped"], 1)
                        if b == 0 and since(g, 1):
                            ve.wait_ge(s["ada_cols"], g * 3 + 24)
                            ada_bias(2, bank[5][:, 0:24], 3, g * 3 - 3, 2, VO["ada_b_2"] + 48)
                        if upto(g, KVG):
                            ada_copy(6 + b % 2, g * 3 + (24 + b), b)

                    for b in range(3):
                        block_step(b, 0)
                    with ve.Fori(1, KVG) as g:
                        for b in range(3):
                            block_step(b, g)
                    for b in range(2):
                        block_step(b, KVG)
                    end_phase()
                    attention([Unit(branches=1, w=512 if t < 2 else 256) for _ in range(4) for t in range(4)], KVG, 32,
                              lambda g, b, bk: V.tensor_copy(o2[:, ds(g * 2 + b, 1), :].rearrange("p a t -> p (a t)"), bk[:, :]))
                    end_phase()
                    gemm(2, 4, T2, 16, 1)
                else:
                    V.tensor_scalar(qcos[0:QK], C("mcos", QK), QK ** -0.5, None, ALU.mult)
                    V.tensor_scalar(qsin[0:QK], C("msin", QK), QK ** -0.5, None, ALU.mult)
                    ve.wait_ge(s["kv_roped"], 2)
                    V.reciprocal(rstd[:, 0:T], rstd[:, 0:T])
                    V.reciprocal(ckv_rstd[:, :], ckv_rstd[:, :])
                    ve.drain()
                    for b in range(3):
                        V.scalar_tensor_tensor(cqn[:, b, :], bank[1 + b][:, 0:T], col("mla_q_norm_g_2", b), rstd[:, 0:T],
                                               ALU.mult, ALU.mult)
                    for b in range(2):
                        V.scalar_tensor_tensor(ckvn[:, b, :], bank[4 + b][:, :], col("mla_kv_norm_g_2", b), ckv_rstd[:, :],
                                               ALU.mult, ALU.mult)
                    ve.drain().then_inc(s["kv_ready"], 1)
                    r = slice(ND, QK)
                    ve.wait_ge(s["kv_dup"], 2)
                    V.tensor_tensor(kr_roped[r, 0:T], kr_raw[r, 0:T], consts[r, CO["mcos"][0]:CO["mcos"][0] + T], ALU.mult)
                    V.tensor_tensor(kr_roped[r, T:T2], bank[6][r, 0:T], consts[r, CO["msin"][0]:CO["msin"][0] + T], ALU.mult)
                    ve.drain()
                    V.tensor_tensor(kr_raw[r, 0:T], kr_roped[r, 0:T], kr_roped[r, T:T2], ALU.add)
                    end_phase()

                    def heads(it, q):
                        if since(it, 1):
                            x = 1 - q
                            ve.wait_ge(s["q_raw"], it + 4)
                            V.tensor_tensor(mq_t[0:QK], mq_raw[x][0:QK], qcos[0:QK].unsqueeze(1).to_broadcast([QK, 2, T]), ALU.mult)
                            ve.wait_ge(s["q_rot"], it + 16)
                            V.tensor_tensor(mq_tmp[0:QK], bank[4 * x][0:QK, :].rearrange("p (a t) -> p a t", a=2),
                                            qsin[0:QK].unsqueeze(1).to_broadcast([QK, 2, T]), ALU.mult)
                            ve.drain()
                            V.tensor_tensor(mqa[0:QK, ds(it * 2 - 2, 2), :], mq_t[0:QK], mq_tmp[0:QK], ALU.add)
                            ve.drain().then_inc(s["q_roped"], 1)

                    for q in range(2):
                        heads(q, q)
                    with ve.Fori(1, 4) as trip:
                        for q in range(2):
                            heads(trip * 2 + q, q)
                    heads(8, 0)
                    end_phase()
                    attention([Unit(branches=1, w=512) for _ in range(8)], 4, 96,
                              lambda trip, q, b: V.tensor_copy(o2x[:, ds(trip * 2 + q, 1), :].rearrange("p a t -> p (a t)"), b[:, 0:T]))
                    end_phase()
                    gemm(2, 4, T, 16, 2)
                w = T2 if l == 0 else T
                norm(w, lambda part: mod[1 + l][:, 1, part, :], hn, True)
                cw = VO["ffn_conv_w_2"] + l * 3 * 2 * FB
                with ve.Fori(0, FB // 2) as i:
                    for q in range(2):
                        j = i * 2 + q
                        for tap in (0, 2):
                            for x in range(2):
                                if tap == 0:
                                    ve.wait_ge(s["ffn_acc"], j * 2 + (2 * n["ffn_ev"] + x + 1))
                                u = bank[2 * q + x][:, 0:w].rearrange("p (a t) -> p a t", t=T)
                                a = ffn_acc[:, 2 * q + x, 0:w].rearrange("p (a t) -> p a t", t=T)
                                uu, aa = (u[:, :, 0:T - 1], a[:, :, 1:T]) if tap == 0 else (u[:, :, 1:T], a[:, :, 0:T - 1])
                                V.scalar_tensor_tensor(aa, uu, cols[:, ds(j + (cw + tap * 2 * FB + x * FB), 1)], aa,
                                                       ALU.mult, ALU.add)
                            ve.drain() if tap == 0 else ve.drain().then_inc(s["ffn_taps"], 1)
                        ve.wait_ge(s["ffn_silu"], j + (n["ffn_ev"] + 1))
                        V.tensor_tensor(act[:, ds(j, 1), 0:w].rearrange("p a t -> p (a t)"), ffn_acc[:, 2 * q, 0:w],
                                        ffn_acc[:, 2 * q + 1, 0:w], ALU.mult).then_inc(s["ffn_ev"], 1)
                n["ffn_ev"] += FB
                gemm(2, 4, w, 40, 1 + l)
            norm(T, lambda part: cols[:, VO["final_norm_g_2"]:VO["final_norm_g_2"] + KD], resid, False)
            end_phase()


def kernel(**inputs):
    import concourse.bacc as bacc
    from concourse.bass_utils import run_bass_kernel_spmd as run

    x = {k: np.asarray(v) for k, v in inputs.items()}

    def rows(a):
        return np.broadcast_to(a, (P,) + a.shape)

    w_in, up, down, ada2 = x["w_in"][0], x["ffn_w_up_2"], x["ffn_w_down_2"], x["ada_w_2"]
    vec = dict(x)
    vec["d_skip"] = np.repeat(x["d_skip"], HD)
    for name in ("gqa_q_norm_g_2", "gqa_k_norm_g_2"):
        vec[name] = np.tile(x[name], 2)

    def span(o, i, w):
        return o + i * w, o + (i + 1) * w

    n256 = [span(0, i, 256) for i in range(4)]
    g_in, u_q, u_kv = x["gqa_w_in_2"][0], x["mla_w_uq_2"][0], x["mla_w_ukv_2"][0]
    wg, wu, wd = x["w_exp_gate"][0], x["w_exp_up"][0], x["w_exp_down"][0]
    o_b, o_c = O_XBC + DIN, O_XBC + DIN + GRP * ST
    mla_in = x["mla_w_in_2"][0]
    wide = np.zeros((P, 3072 - 2304), np.float32)
    chunks = {
        "ada": [pack(x["w_ada"][0], span(0, i, 512)) for i in range(12)],
        "z": [pack(w_in, span(O_Z, g, 512)) for g in range(4)],
        "x": [pack(w_in, span(O_XBC, g, 512)) for g in range(4)],
        "bc": [pack(w_in, span(o_b, g, P), span(o_c, g, P)) for g in range(4)],
        "wso": [pack(x["w_ssm_out"][0], c) for c in n256],
        "gs": [pack(w_in, span(O_GS, i, 256)) for i in range(4)],
        "kv": [pack(w_in, span(O_KC, i, 384)) for i in range(2)],
        "cw1": [pack(x["cmp_w1_k"][0]), pack(x["cmp_w1_v"][0])],
        "q": [pack(w_in, span(O_Q, j, P), span(O_Q, 4 + j, P)) for j in range(4)],
        "nga": [np.concatenate([pack(x["w_nsa_out"][0], c), pack(w_in, span(O_GA, i, 256))], axis=1)
                for i, c in enumerate(n256)],
        "wo": [pack(x["w_o"][0], c) for c in n256],
        "egu": [pack(np.concatenate([wg[e], wu[e]], axis=1)) for e in range(NE)],
        "edn": [pack(wd[e]) for e in range(NE)],
        "ada2": [pack(ada2[i // 12], span(0, i % 12, 512)) for i in range(24)],
        "gqav": [pack(g_in, (1280, 1536))],
        "gqa": [pack(g_in, span(0, g, 256), span(1024, g, 64), span(1024, g, 64)) for g in range(4)],
        "gqao": [pack(x["gqa_w_out_2"][0], c) for c in n256],
        "up": [pack(up[i // FB], span(0, i % FB, P), span(FFN, i % FB, P)) for i in range(2 * FB)],
        "down": [pack(down[i // 8], span(0, i % 8, P)) for i in range(16)],
        "mla": [pack(mla_in, (0, 384)), np.concatenate([pack(mla_in, (384, 672)), wide], axis=1)],
        "mlah": [np.concatenate([pack(u_q, span(0, j, 192)), pack(u_kv, span(0, j, 256))], axis=1) for j in range(8)],
        "mlao": [pack(x["mla_w_out_2"][0], c) for c in n256],
    }
    arrays = {name: np.concatenate(c, axis=0) for name, c in chunks.items()}
    for name, (m, w) in STREAMS.items():
        assert arrays[name].shape == (m * P, w), (name, arrays[name].shape)
    arrays["consts"] = constants()
    arrays["iota"] = rows(np.arange(NPOS, dtype=np.float32))
    arrays["vecs"] = np.concatenate([np.reshape(vec[name], (-1, P)) for name, _ in VECS], axis=0)
    arrays["xt"] = pack(x["x"][0].T)
    arrays["ctxt"] = pack(x["ctx_2"][0].T)
    arrays["positions"] = rows(x["positions"][0])
    arrays["ssm_rows"] = rows(np.concatenate([x["dt_bias"][0], x["a_log"][0]]))
    arrays["route_rows"] = rows(np.concatenate([x["b_router_group"][0], x["b_router_expert"][0]]))
    arrays["w_small"] = pack(w_in, (O_DT, O_DT + HEADS), (O_GN, O_GN + 3 * NH))
    arrays["w_route"] = pack(np.concatenate([x["w_router_group"][0], x["w_router_expert"][0]], axis=1))
    arrays["w_cmp2"] = pack(np.concatenate([x["cmp_w2_k"][0], x["cmp_w2_k"][0], x["cmp_w2_v"][0]], axis=1))

    nc = bacc.Bacc("TRN2", target_bir_lowering=False, num_devices=1)
    sent, dr = {}, {}
    for name, a in arrays.items():
        sent[f"in_{name}"] = np.ascontiguousarray(a)
        dr[name] = nc.dram_tensor(f"in_{name}", a.shape, mybir.dt.from_np(a.dtype), kind="ExternalInput").ap()
    dr["out"] = nc.dram_tensor("out", (P, KD * T), F32, kind="ExternalOutput").ap()
    build(nc, dr)
    got = run(nc, [sent], core_ids=[0]).results[0]["out"]
    return np.ascontiguousarray(got.reshape(P, KD, T).transpose(2, 1, 0).reshape(1, T, D))
```
